# Optimizing a Trainium2 kernel written in Bass

```python
import math
import jax, jax.numpy as jnp
from jax import lax
import numpy as np

D_MODEL = 1024
BATCH = 1
SEQ = 256
DEPTH = 2

N_META = 16
D_FF = 2816
REC_WIDTH = 512
REC_BLOCKS = 8
REC_BLOCK_DIM = REC_WIDTH // REC_BLOCKS
CONV_WIDTH = 4
LRU_C = 8.0
N_Q_HEADS = 8
N_KV_HEADS = 2
Q_PER_KV = N_Q_HEADS // N_KV_HEADS
HEAD_DIM = 64
ATTN_WIDTH = N_Q_HEADS * HEAD_DIM
KV_WIDTH = N_KV_HEADS * HEAD_DIM
WINDOW = 128
BLOCK = 128
ROPE_DIM = HEAD_DIM // 4
ROPE_THETA = 500000.0
D_IN = 2 * REC_WIDTH + ATTN_WIDTH + 2 * KV_WIDTH
D_MIX = REC_WIDTH + ATTN_WIDTH
DEEPNORM_ALPHA = (2.0 * DEPTH) ** 0.25
DEEPNORM_BETA = (8.0 * DEPTH) ** -0.25
LN_EPS = 1e-5
RMS_EPS = 1e-6
NEG_INF = -1e30

kernel_name = "hybrid_rglru_swa_sink_macaron_deepnorm"

def layer_norm(x, g, b):
    xf = x.astype(jnp.float32)
    mu = jnp.mean(xf, axis=-1, keepdims=True)
    var = jnp.mean(jnp.square(xf - mu), axis=-1, keepdims=True)
    return ((xf - mu) * lax.rsqrt(var + LN_EPS) * g.astype(jnp.float32) + b.astype(jnp.float32)).astype(x.dtype)

def rms_norm(x, g):
    xf = x.astype(jnp.float32)
    ms = jnp.mean(jnp.square(xf), axis=-1, keepdims=True)
    return (xf * lax.rsqrt(ms + RMS_EPS) * g.astype(jnp.float32)).astype(x.dtype)

def swiglu(x, w_gate, w_up, w_down):
    return (jax.nn.silu(x @ w_gate) * (x @ w_up)) @ w_down

def causal_depthwise_conv(x, w, b):
    L = x.shape[1]
    xp = jnp.pad(x, ((0, 0), (CONV_WIDTH - 1, 0), (0, 0)))
    y = b + xp[:, 0:L] * w[0]
    for k in range(1, CONV_WIDTH):
        y = y + xp[:, k:k + L] * w[k]
    return y

def rglru(x, wa, ba, wx, bx, lam):
    B, L, _ = x.shape
    xb = x.reshape(B, L, REC_BLOCKS, REC_BLOCK_DIM)
    r = jax.nn.sigmoid(jnp.einsum('blhi,hij->blhj', xb, wa).reshape(B, L, REC_WIDTH) + ba).astype(jnp.float32)
    i = jax.nn.sigmoid(jnp.einsum('blhi,hij->blhj', xb, wx).reshape(B, L, REC_WIDTH) + bx)
    log_a = -LRU_C * jax.nn.softplus(-lam.astype(jnp.float32)) * r
    a = jnp.exp(log_a)
    gated_x = jnp.sqrt(-jnp.expm1(2.0 * log_a)) * (i * x).astype(jnp.float32)

    def combine(c1, c2):
        a1, b1 = c1
        a2, b2 = c2
        return a1 * a2, a2 * b1 + b2

    _, h = lax.associative_scan(combine, (a, gated_x), axis=1)
    return h.astype(x.dtype)

def rope_tables(L):
    pos = jnp.arange(L, dtype=jnp.float32)
    inv_freq = ROPE_THETA ** (-jnp.arange(0, ROPE_DIM, 2, dtype=jnp.float32) / ROPE_DIM)
    ang = pos[:, None] * inv_freq[None, :]
    return jnp.cos(ang), jnp.sin(ang)

def apply_partial_rope(t, cos, sin):
    tf = t.astype(jnp.float32)
    x1 = tf[..., :ROPE_DIM // 2]
    x2 = tf[..., ROPE_DIM // 2:ROPE_DIM]
    c = cos[None, :, None, :]
    s = sin[None, :, None, :]
    out = jnp.concatenate([x1 * c - x2 * s, x2 * c + x1 * s, tf[..., ROPE_DIM:]], axis=-1)
    return out.astype(t.dtype)

def swa_sink_attention(q, k, v, sinks):
    B, L = q.shape[0], q.shape[1]
    pad = (-L) % BLOCK
    nb = (L + pad) // BLOCK
    padl = ((0, 0), (pad, 0), (0, 0), (0, 0))
    qb = jnp.pad(q, padl).reshape(B, nb, BLOCK, N_KV_HEADS, Q_PER_KV, HEAD_DIM)
    kb = jnp.pad(k, padl).reshape(B, nb, BLOCK, N_KV_HEADS, HEAD_DIM)
    vb = jnp.pad(v, padl).reshape(B, nb, BLOCK, N_KV_HEADS, HEAD_DIM)
    prev = ((0, 0), (1, 0), (0, 0), (0, 0), (0, 0))
    k_band = jnp.concatenate([jnp.pad(kb, prev)[:, :-1], kb], axis=2)
    v_band = jnp.concatenate([jnp.pad(vb, prev)[:, :-1], vb], axis=2)
    k_meta = k[:, :N_META]
    v_meta = v[:, :N_META]
    scale = HEAD_DIM ** -0.5
    s_band = jnp.einsum('bnqgrd,bnkgd->bngrqk', qb, k_band).astype(jnp.float32) * scale
    s_meta = jnp.einsum('bnqgrd,bmgd->bngrqm', qb, k_meta).astype(jnp.float32) * scale
    q_pos = jnp.arange(nb)[:, None] * BLOCK + jnp.arange(BLOCK)[None, :] - pad
    k_pos = (jnp.arange(nb)[:, None] - 1) * BLOCK + jnp.arange(2 * BLOCK)[None, :] - pad
    dist = q_pos[:, :, None] - k_pos[:, None, :]
    band_mask = (dist >= 0) & (dist < WINDOW) & (k_pos[:, None, :] >= N_META)
    meta_mask = jnp.arange(N_META)[None, None, :] <= q_pos[:, :, None]
    s_band = jnp.where(band_mask[None, :, None, None], s_band, NEG_INF)
    s_meta = jnp.where(meta_mask[None, :, None, None], s_meta, NEG_INF)
    sink = jnp.broadcast_to(sinks.astype(jnp.float32).reshape(1, 1, N_KV_HEADS, Q_PER_KV, 1, 1),
                            s_meta.shape[:-1] + (1,))
    probs = jax.nn.softmax(jnp.concatenate([sink, s_meta, s_band], axis=-1), axis=-1)
    p_meta = probs[..., 1:1 + N_META].astype(v.dtype)
    p_band = probs[..., 1 + N_META:].astype(v.dtype)
    o = (jnp.einsum('bngrqm,bmgd->bnqgrd', p_meta, v_meta)
         + jnp.einsum('bngrqk,bnkgd->bnqgrd', p_band, v_band))
    return o.reshape(B, nb * BLOCK, ATTN_WIDTH)[:, pad:]

def hybrid_mixer(h, w_in, conv_w, conv_b, ga_w, ga_b, gx_w, gx_b, lam, sinks, g_rec, g_attn, w_out, cos, sin):
    B, L, _ = h.shape
    proj = h @ w_in
    x_rec, gate, q, k, v = jnp.split(
        proj, [REC_WIDTH, 2 * REC_WIDTH, 2 * REC_WIDTH + ATTN_WIDTH, 2 * REC_WIDTH + ATTN_WIDTH + KV_WIDTH], axis=-1)
    x_rec = causal_depthwise_conv(x_rec, conv_w, conv_b)
    y_rec = rglru(x_rec, ga_w, ga_b, gx_w, gx_b, lam) * jax.nn.gelu(gate, approximate=True)
    q = apply_partial_rope(q.reshape(B, L, N_Q_HEADS, HEAD_DIM), cos, sin)
    k = apply_partial_rope(k.reshape(B, L, N_KV_HEADS, HEAD_DIM), cos, sin)
    v = v.reshape(B, L, N_KV_HEADS, HEAD_DIM)
    y_attn = swa_sink_attention(q, k, v, sinks)
    y = jnp.concatenate([rms_norm(y_rec, g_rec), rms_norm(y_attn, g_attn)], axis=-1)
    return y @ w_out

def setup_inputs(seed: int = 0) -> dict:
    key = jax.random.key(seed)
    ks = jax.random.split(key, 26)
    f32 = jnp.float32

    def nrm(k, shape, scale):
        return jax.random.normal(k, shape, f32) * scale

    u = jax.random.uniform(ks[12], (DEPTH, REC_WIDTH), f32, 0.9, 0.999)
    s = u ** (1.0 / LRU_C)
    lru_lambda = jnp.log(s) - jnp.log1p(-s)
    return {
        'x': nrm(ks[0], (BATCH, SEQ, D_MODEL), 1.0),
        'meta_tokens': nrm(ks[1], (N_META, D_MODEL), 1.0),
        'ffn1_w_gate': nrm(ks[2], (DEPTH, D_MODEL, D_FF), D_MODEL ** -0.5),
        'ffn1_w_up': nrm(ks[3], (DEPTH, D_MODEL, D_FF), D_MODEL ** -0.5),
        'ffn1_w_down': nrm(ks[4], (DEPTH, D_FF, D_MODEL), D_FF ** -0.5 * DEEPNORM_BETA),
        'ln1_g': 1.0 + nrm(ks[5], (DEPTH, D_MODEL), 0.02),
        'ln1_b': nrm(ks[6], (DEPTH, D_MODEL), 0.02),
        'w_in': nrm(ks[7], (DEPTH, D_MODEL, D_IN), D_MODEL ** -0.5),
        'conv_w': nrm(ks[8], (DEPTH, CONV_WIDTH, REC_WIDTH), CONV_WIDTH ** -0.5),
        'conv_b': nrm(ks[9], (DEPTH, REC_WIDTH), 0.02),
        'gate_a_w': nrm(ks[10], (DEPTH, REC_BLOCKS, REC_BLOCK_DIM, REC_BLOCK_DIM), REC_BLOCK_DIM ** -0.5),
        'gate_a_b': nrm(ks[11], (DEPTH, REC_WIDTH), 0.02),
        'gate_x_w': nrm(ks[13], (DEPTH, REC_BLOCKS, REC_BLOCK_DIM, REC_BLOCK_DIM), REC_BLOCK_DIM ** -0.5),
        'gate_x_b': nrm(ks[14], (DEPTH, REC_WIDTH), 0.02),
        'lru_lambda': lru_lambda,
        'attn_sinks': nrm(ks[15], (DEPTH, N_Q_HEADS), 0.5),
        'norm_rec_g': 1.0 + nrm(ks[16], (DEPTH, REC_WIDTH), 0.02),
        'norm_attn_g': 1.0 + nrm(ks[17], (DEPTH, ATTN_WIDTH), 0.02),
        'w_out': nrm(ks[18], (DEPTH, D_MIX, D_MODEL), D_MIX ** -0.5 * DEEPNORM_BETA),
        'ln2_g': 1.0 + nrm(ks[19], (DEPTH, D_MODEL), 0.02),
        'ln2_b': nrm(ks[20], (DEPTH, D_MODEL), 0.02),
        'ffn2_w_gate': nrm(ks[21], (DEPTH, D_MODEL, D_FF), D_MODEL ** -0.5),
        'ffn2_w_up': nrm(ks[22], (DEPTH, D_MODEL, D_FF), D_MODEL ** -0.5),
        'ffn2_w_down': nrm(ks[23], (DEPTH, D_FF, D_MODEL), D_FF ** -0.5 * DEEPNORM_BETA),
        'ln3_g': 1.0 + nrm(ks[24], (DEPTH, D_MODEL), 0.02),
        'ln3_b': nrm(ks[25], (DEPTH, D_MODEL), 0.02),
    }

def reference(x, meta_tokens, ffn1_w_gate, ffn1_w_up, ffn1_w_down, ln1_g, ln1_b, w_in, conv_w, conv_b,
              gate_a_w, gate_a_b, gate_x_w, gate_x_b, lru_lambda, attn_sinks, norm_rec_g, norm_attn_g,
              w_out, ln2_g, ln2_b, ffn2_w_gate, ffn2_w_up, ffn2_w_down, ln3_g, ln3_b):
    B = x.shape[0]
    meta = jnp.broadcast_to(meta_tokens[None].astype(x.dtype), (B, N_META, D_MODEL))
    h = jnp.concatenate([meta, x], axis=1)
    cos, sin = rope_tables(h.shape[1])
    for l in range(DEPTH):
        h = layer_norm(DEEPNORM_ALPHA * h + 0.5 * swiglu(h, ffn1_w_gate[l], ffn1_w_up[l], ffn1_w_down[l]),
                       ln1_g[l], ln1_b[l])
        m = hybrid_mixer(h, w_in[l], conv_w[l], conv_b[l], gate_a_w[l], gate_a_b[l], gate_x_w[l], gate_x_b[l],
                         lru_lambda[l], attn_sinks[l], norm_rec_g[l], norm_attn_g[l], w_out[l], cos, sin)
        h = layer_norm(DEEPNORM_ALPHA * h + m, ln2_g[l], ln2_b[l])
        h = layer_norm(DEEPNORM_ALPHA * h + 0.5 * swiglu(h, ffn2_w_gate[l], ffn2_w_up[l], ffn2_w_down[l]),
                       ln3_g[l], ln3_b[l])
    return h[:, N_META:]


_drawn_inputs = setup_inputs


def setup_inputs(seed=0):
    import zlib

    import numpy as np

    out = dict(_drawn_inputs(seed))
    spreads = {}
    factors = {'gate_a_b': 8.0,
     'gate_x_b': 8.0,
     'attn_sinks': 8.0,
     'norm_rec_g': 7.821,
     'norm_attn_g': 7.324}
    for name, (base, spread) in spreads.items():
        noise = np.random.default_rng([zlib.crc32(name.encode()), seed]).standard_normal(out[name].shape)
        drawn = base * np.exp(spread * noise) if base else spread * noise
        out[name] = __import__('jax').numpy.asarray(drawn.astype(out[name].dtype))
    for name, factor in factors.items():
        out[name] = (out[name] * factor).astype(out[name].dtype)
    return out
```

```python
from contextlib import ExitStack

import numpy as np

import concourse.bass as bass
from concourse import mybir

F32 = mybir.dt.float32
F32R = mybir.dt.float32r
BF16 = mybir.dt.bfloat16
ACT = mybir.ActivationFunctionType
ALU = mybir.AluOpType
AX = mybir.AxisListType

P = 128
D_MODEL = 1024
SEQ = 256
DEPTH = 2
N_META = 16
D_FF = 2816
REC = 512
CONV = 4
LRU_C = 8.0
N_Q = 8
N_KV = 2
HEAD = 64
ATTN = N_Q * HEAD
WINDOW = 128
ROPE_DIM = HEAD // 4
ROPE_THETA = 500000.0
ALPHA = (2.0 * DEPTH) ** 0.25
LN_EPS = 1e-5
RMS_EPS = 1e-6
NEG_INF = -1e30
T = N_META + SEQ

KD = D_MODEL // P
KF = D_FF // P
RT = REC // P
QT = ATTN // P
KH = KF // 2
SLOTS = 4
GU_PAIRS = KF // 2
DOWN_STEPS = KD // 2

N_GU = 2 * KF
N_DOWN = 2 * KD
N_IN = 2 * RT + 2 + QT
N_OUT = KD
FFN_UNITS = N_GU + N_DOWN
LAYER_UNITS = 2 * FFN_UNITS + N_IN + N_OUT
ALL_UNITS = DEPTH * LAYER_UNITS
U_K, U_V, U_Q, U_GATE = RT, RT + 1, RT + 2, RT + 2 + QT

STEPS = [(0, 0, 4, 0, 128), (1, 0, 4, 0, 128),
         (0, 0, 2, 128, 256), (0, 2, 2, 128, 256), (1, 0, 2, 128, 256), (1, 2, 2, 128, 256),
         (None, 0, 1, 256, 272)]
NS = len(STEPS)
TAIL_Q = T - 2 * P

C_ID, C_PERM, C_COS, C_SIN, C_PICK = 0, P, 2 * P, 2 * P + T, 2 * P + 2 * T
C_MA = C_PICK + N_Q
C_MB, C_MC = C_MA + P, C_MA + 3 * P
C_ALL = C_MC + T

LN_COLS = 6 * DEPTH * KD
PC_CONVW = LN_COLS
PC_CONVB = PC_CONVW + DEPTH * CONV * RT
PC_GA, PC_GX, PC_LAM, PC_GREC, PC_GATT = (PC_CONVB + DEPTH * RT * i for i in range(1, 6))
PC_ALL = PC_GATT + DEPTH * QT
ROWS_B = PC_ALL - LN_COLS


def constants():
    c = np.zeros((P, C_ALL), np.float32)
    c[:, C_ID:C_ID + P] = np.eye(P, dtype=np.float32)
    half = ROPE_DIM // 2
    pos = np.arange(T, dtype=np.float32)
    inv = np.float32(ROPE_THETA) ** (-np.arange(0, ROPE_DIM, 2, dtype=np.float32) / np.float32(ROPE_DIM))
    ang = pos[:, None] * inv[None, :]
    cos, sin = np.cos(ang), np.sin(ang)
    c[:, C_COS:C_COS + T] = 1.0
    for base in (0, HEAD):
        for d in range(half):
            a, b = base + d, base + half + d
            c[b, C_PERM + a] = 1.0
            c[a, C_PERM + b] = 1.0
            c[a, C_COS:C_COS + T] = cos[:, d]
            c[b, C_COS:C_COS + T] = cos[:, d]
            c[a, C_SIN:C_SIN + T] = -sin[:, d]
            c[b, C_SIN:C_SIN + T] = sin[:, d]

    def mask(q, k):
        seen = (k <= q) & ((k < N_META) | (q - k < WINDOW))
        return np.where(seen, 0.0, NEG_INF).astype(np.float32)

    rows = np.arange(P)[:, None]
    c[:, C_MA:C_MA + P] = mask(rows, np.arange(P)[None, :])
    c[:, C_MB:C_MB + 2 * P] = mask(rows + P, np.arange(2 * P)[None, :])
    c[:, C_MC:C_MC + T] = mask(2 * P + rows % TAIL_Q, np.arange(T)[None, :])
    for p in range(P):
        c[p, C_PICK + 4 * (p // 64) + (p % 64) // TAIL_Q] = 1.0
    return c


def build(nc, w, consts, out):
    with ExitStack() as ctx:
        def sb(name, shape, dt=F32):
            return ctx.enter_context(nc.sbuf_tensor(name, shape, dt))

        def sem(name):
            return ctx.enter_context(nc.semaphore(name))

        bank = [ctx.enter_context(nc.psum_tensor(f"bank{i}", [P, 512], F32)) for i in range(8)]
        arena_bytes = 2 * KF * T * 4
        arena = sb("arena", [P, arena_bytes // 4])
        arena_at = nc.sbuf_base - arena_bytes
        a_hi = nc.alloc_sbuf_tensor_at("a_hi", [P, KF, T], F32R, offset=arena_at)
        a_lo = nc.alloc_sbuf_tensor_at("a_lo", [P, KF, T], F32R, offset=arena_at + KF * T * 4)
        taken = [arena_at]

        def mix(name, shape):
            size = int(np.prod(shape[1:])) * 4
            t = nc.alloc_sbuf_tensor_at(name, shape, F32, offset=taken[0])
            taken[0] += (size + 31) // 32 * 32
            assert taken[0] <= arena_at + arena_bytes
            return t

        x_stage = nc.alloc_sbuf_tensor_at("x_stage", [P, 3, D_MODEL], F32, offset=arena_at)
        out_stage = nc.alloc_sbuf_tensor_at("out_stage", [P, 4, 512], F32, offset=arena_at)

        h = sb("h", [P, KD, T])
        h_hi = sb("h_hi", [P, KD, T], F32R)
        h_lo = sb("h_lo", [P, KD, T], F32R)
        raw = sb("raw", [P, SLOTS, KH * P])
        w_hi = sb("w_hi", [P, SLOTS, KH * P], F32R)
        w_lo = sb("w_lo", [P, SLOTS, KH * P], F32R)

        cst = sb("cst", [P, C_ALL])
        masks = sb("masks", [P, 3 * P + T], BF16)
        ident16 = sb("ident16", [P, P], BF16)
        ones_c = sb("ones_c", [P, P])
        ones_d = sb("ones_d", [P, P])
        ones_r = sb("ones_r", [P, P])
        eps = sb("eps", [P, 4])
        par_rows = sb("par_rows", [P, 2, P])
        par = sb("par", [P, PC_ALL])
        decay = sb("decay", [P, DEPTH * RT])
        soft = sb("soft", [P, 4, DEPTH * RT])
        sink = sb("sink", [P, DEPTH, N_Q])
        sink_pick = sb("sink_pick", [P, DEPTH, N_Q])
        sink_tail = sb("sink_tail", [P, DEPTH])
        gate_w = sb("gate_w", [P, DEPTH, 2, RT, P])

        sg = sb("sg", [P, 2, T])
        act = sb("act", [P, 2, T])
        csum = sb("csum", [P, T])
        center = sb("center", [P, T])
        sq = sb("sq", [P, KD, T])
        sumsq = sb("sumsq", [P, T])
        mu = sb("mu", [P, T])
        dmu = sb("dmu", [P, T])
        var = sb("var", [P, T])
        rstd = sb("rstd", [P, T])

        xr = mix("xr", [P, RT, T + CONV - 1])
        xc = mix("xc", [P, RT, T])
        ra = mix("ra", [P, RT, T])
        th = mix("th", [P, RT, T])
        ig = mix("ig", [P, RT, T])
        gl = mix("gl", [P, RT, T])
        yr = mix("yr", [P, RT, T])
        q_raw = mix("q_raw", [P, QT, T])
        q_rot = mix("q_rot", [P, QT, T])
        ya = mix("ya", [P, QT, T])
        k_raw = mix("k_raw", [P, T])
        v_raw = mix("v_raw", [P, T])
        k_rot = sb("k_rot", [P, N_KV, T])
        v_tok = sb("v_tok", [P, 3, P])
        q_tail = sb("q_tail", [P, QT * TAIL_Q])
        turn = sb("turn", [P, 2, T])
        probs = sb("probs", [P, 4, 512])
        probs_t = sb("probs_t", [P, 2, 512])
        sm = sb("sm", [P, NS, 8, 4])
        MX, MAX, NEG, DSINK, ESINK, SUM, Z, RZ = range(8)

        ident = cst[:, C_ID:C_ID + P]
        perm = cst[:, C_PERM:C_PERM + P]
        cos = cst[:, C_COS:C_COS + T]
        sin = cst[:, C_SIN:C_SIN + T]

        raw_landed = [sem(f"raw_landed{s}") for s in range(SLOTS)]
        w_hi_ready = sem("w_hi_ready")
        w_lo_ready = sem("w_lo_ready")
        w_used = sem("w_used")
        consts_in = sem("consts_in")
        params_in = sem("params_in")
        x_in = sem("x_in")
        gates_in = sem("gates_in")
        zeroed = sem("zeroed")
        masks_ready = sem("masks_ready")
        params_turned = sem("params_turned")
        params_ready = sem("params_ready")
        soft_step = sem("soft_step")
        soft_exp = sem("soft_exp")
        x_turned = sem("x_turned")
        h_ready = sem("h_ready")
        h_hi_ready = sem("h_hi_ready")
        h_lo_ready = sem("h_lo_ready")
        silu_done = sem("silu_done")
        mult_done = sem("mult_done")
        a_hi_ready = sem("a_hi_ready")
        a_lo_ready = sem("a_lo_ready")
        z_ready = sem("z_ready")
        csum_step = sem("csum_step")
        c_psum = sem("c_psum")
        c_ready = sem("c_ready")
        zc_ready = sem("zc_ready")
        sq_ready = sem("sq_ready")
        sumsq_step = sem("sumsq_step")
        mu_psum = sem("mu_psum")
        var_psum = sem("var_psum")
        mu_ready = sem("mu_ready")
        dmu_step = sem("dmu_step")
        sd_ready = sem("sd_ready")
        rstd_ready = sem("rstd_ready")
        t_ready = sem("t_ready")
        u_ready = sem("u_ready")
        xr_padded = sem("xr_padded")
        xr_ready = sem("xr_ready")
        k_raw_ready = sem("k_raw_ready")
        v_raw_ready = sem("v_raw_ready")
        q_raw_ready = sem("q_raw_ready")
        conv_step = sem("conv_step")
        gates_psum = sem("gates_psum")
        sig_ready = sem("sig_ready")
        decay_ready = sem("decay_ready")
        m_step = sem("m_step")
        root_ready = sem("root_ready")
        ix_ready = sem("ix_ready")
        gx_ready = sem("gx_ready")
        scan_ready = sem("scan_ready")
        gelu_ready = sem("gelu_ready")
        yr_ready = sem("yr_ready")
        ya_ready = sem("ya_ready")
        ysq_ready = sem("ysq_ready")
        ysq_step = sem("ysq_step")
        rms_psum = sem("rms_psum")
        rms_sd = sem("rms_sd")
        rms_ready = sem("rms_ready")
        yn_ready = sem("yn_ready")
        y_hi_ready = sem("y_hi_ready")
        y_lo_ready = sem("y_lo_ready")
        z_rec_ready = sem("z_rec_ready")
        swap_psum = sem("swap_psum")
        rope_c = sem("rope_c")
        rope_s = sem("rope_s")
        rope_ready = sem("rope_ready")
        q_tail_ready = sem("q_tail_ready")
        v_psum = sem("v_psum")
        v_ready = sem("v_ready")
        scores_psum = sem("scores_psum")
        max_step = sem("max_step")
        sum_step = sem("sum_step")
        exp_ready = sem("exp_ready")
        probs_ready = sem("probs_ready")
        probs_psum = sem("probs_psum")
        pt_act = sem("pt_act")
        pt_dve = sem("pt_dve")
        pv_done = sem("pv_done")
        out_turned = sem("out_turned")
        out_act = sem("out_act")
        out_dve = sem("out_dve")
        stored = sem("stored")

        block = ctx.enter_context(nc.Block())

        def slot(n0):
            return n0 % SLOTS

        def ffn_unit0(f):
            return (f // 2) * LAYER_UNITS + (f % 2) * (LAYER_UNITS - FFN_UNITS)

        def in_unit0(layer):
            return layer * LAYER_UNITS + FFN_UNITS

        def out_unit0(layer):
            return in_unit0(layer) + N_IN

        def unit_tiles(n):
            r = n % LAYER_UNITS
            if r >= FFN_UNITS + N_IN + N_OUT:
                r -= FFN_UNITS + N_IN + N_OUT
            return KH if N_GU <= r < FFN_UNITS else KD

        def tokens(f_or_norm_last):
            return slice(N_META if f_or_norm_last else 0, T)

        @block.sync
        def _(sp):
            def load(n0, i, tiles, sources):
                if not (isinstance(i, int) and n0 + 4 * i < SLOTS):
                    sp.wait_ge(w_lo_ready, n0 + 4 * i - 3)
                s = slot(n0)
                for to, src in sources:
                    sp.dma_start(to(raw[:, s, 0:tiles * P]), src).then_inc(raw_landed[s], 32 // len(sources))

            def chunks(k):
                return lambda r: r.rearrange("p (k m) -> p k m", k=k)

            def load_gate_up(f, i):
                layer, name = f // 2, ("ffn1", "ffn2")[f % 2]
                for j in range(4):
                    src = w[name + ("_w_gate", "_w_up")[j % 2]][layer].rearrange("(k p) n -> p k n", p=P)
                    cols = bass.ds((2 * i + j // 2) * P, P)
                    load(ffn_unit0(f) + j, i, KD, [(chunks(KD), src[:, :, cols])])

            def load_down(f, i):
                layer, name = f // 2, ("ffn1", "ffn2")[f % 2]
                for j in range(4):
                    src = w[name + "_w_down"][layer].rearrange("(k p) n -> p k n", p=P)
                    cols = bass.ds((2 * i + j // 2) * P, P)
                    k0 = (j % 2) * KH
                    load(ffn_unit0(f) + N_GU + j, i, KH, [(chunks(KH), src[:, k0:k0 + KH, cols])])

            def load_ffn(f):
                load_gate_up(f, 0)
                with sp.Fori(1, GU_PAIRS, 1) as i:
                    load_gate_up(f, i)
                with sp.Fori(0, DOWN_STEPS, 1) as i:
                    load_down(f, i)

            def load_mixer(layer):
                w_in = w["w_in"][layer].rearrange("(k p) n -> p k n", p=P)
                w_out = w["w_out"][layer]
                starts = ([t * P for t in range(RT)]
                          + [2 * REC + ATTN, 2 * REC + ATTN + N_KV * HEAD]
                          + [None] * QT + [REC + t * P for t in range(RT)])
                for j, c0 in enumerate(starts):
                    if c0 is not None:
                        sources = [(chunks(KD), w_in[:, :, c0:c0 + P])]
                    else:
                        t = j - U_Q
                        sources = []
                        for g in range(N_KV):
                            c0 = 2 * REC + (4 * g + t) * HEAD
                            sources.append((lambda r, g=g: r.rearrange("p (k m) -> p k m", k=KD)
                                            [:, :, g * HEAD:(g + 1) * HEAD], w_in[:, :, c0:c0 + HEAD]))
                    load(in_unit0(layer) + j, 0, KD, sources)
                for j in range(N_OUT):
                    cols = slice((j % 4) * 2 * P, (j % 4 + 1) * 2 * P)
                    if j < 4:
                        src = w_out[0:REC].rearrange("(k p) n -> p k n", p=P)
                        sources = [(chunks(RT), src[:, :, cols])]
                    else:
                        src = w_out[REC:REC + ATTN].rearrange("(g t d) n -> g d t n", g=N_KV, t=QT)
                        sources = [(lambda r, g=g: r[g * HEAD:(g + 1) * HEAD].rearrange(
                            "p (k m) -> p k m", k=QT), src[g][:, :, cols]) for g in range(N_KV)]
                    load(out_unit0(layer) + j, 0, KD, sources)

            for layer in range(DEPTH):
                load_ffn(2 * layer)
                load_mixer(layer)
                load_ffn(2 * layer + 1)

            for b in range(2):
                for a in range(2):
                    sp.wait_ge((out_act, out_dve)[a], b + 1)
                    sp.dma_start(out[0, a * P:(a + 1) * P, b * 512:(b + 1) * 512],
                                 out_stage[:, 2 * a + b, :]).then_inc(stored, 16)
            sp.wait_ge(stored, 64)

        @block.gpsimd
        def _(pool):
            nc.gpsimd.memset(gate_w[:], 0.0).then_inc(zeroed, 1)
            nc.gpsimd.memset(ones_c[:], 1.0 / (6 * P)).then_inc(zeroed, 1)
            nc.gpsimd.memset(ones_d[:], 1.0 / D_MODEL).then_inc(zeroed, 1)
            nc.gpsimd.memset(ones_r[:], 1.0 / REC).then_inc(zeroed, 1)
            nc.gpsimd.memset(eps[:, 0:1], LN_EPS / ALPHA ** 2).then_inc(zeroed, 1)
            nc.gpsimd.memset(eps[:, 1:2], RMS_EPS).then_inc(zeroed, 1)
            nc.gpsimd.memset(eps[:, 2:4], 1.0).then_inc(zeroed, 1)
            nc.gpsimd.memset(k_rot[:], 0.0).then_inc(zeroed, 1)

            def sum_squares(norm, tok):
                for d in range(1, 6):
                    pool.wait_ge(sq_ready, KD * norm + d + 1)
                    if d > 1:
                        pool.wait_ge(sumsq_step, 5 * norm + d - 1)
                    first = sq[:, 0, tok] if d == 1 else sumsq[:, tok]
                    nc.gpsimd.tensor_tensor(sumsq[:, tok], first, sq[:, d, tok], ALU.add).then_inc(sumsq_step, 1)

            def sum_group(layer, which, tok):
                for r in range(1, RT):
                    pool.wait_ge(ysq_ready, 8 * layer + 4 * which + r + 1)
                    if r > 1:
                        pool.wait_ge(ysq_step, 6 * layer + 3 * which + r - 1)
                    first = th[:, 0, tok] if r == 1 else sumsq[:, tok]
                    nc.gpsimd.tensor_tensor(sumsq[:, tok], first, th[:, r, tok], ALU.add).then_inc(ysq_step, 1)

            for layer in range(DEPTH):
                last = layer == DEPTH - 1
                sum_squares(3 * layer, tokens(False))
                sum_group(layer, 0, tokens(last))
                sum_group(layer, 1, tokens(last))
                sum_squares(3 * layer + 1, tokens(last))
                sum_squares(3 * layer + 2, tokens(last))

        @block.scalar
        def _(eng):
            act_fn = nc.scalar.activation

            def copy(to, src):
                return act_fn(to, src, ACT.Copy)

            def split(n0, i=0, tiles=None):
                if isinstance(i, int) and n0 + 4 * i >= ALL_UNITS:
                    return
                tiles = tiles or unit_tiles(n0 + 4 * i)
                s = slot(n0)
                eng.wait_ge(raw_landed[s], (n0 // SLOTS + i + 1) * 32)
                if not (isinstance(i, int) and n0 + 4 * i < SLOTS):
                    eng.wait_ge(w_used, n0 + 4 * i - 3)
                copy(w_hi[:, s, 0:tiles * P], raw[:, s, 0:tiles * P]).then_inc(w_hi_ready, 1)

            def gate_up(f, i, tiles, tok):
                u0 = ffn_unit0(f)
                for j in range(4):
                    split(u0 + 4 + j, i, tiles)
                    t0, b = KF * f + j // 2, j // 2
                    if j % 2 == 0:
                        eng.wait_ge(w_used, u0 + 4 * i + j + 1)
                        act_fn(sg[:, b, tok], bank[j][:, tok], ACT.Silu).then_inc(silu_done, 1)
                    else:
                        eng.wait_ge(mult_done, t0 + 2 * i + 1)
                        copy(a_hi[:, bass.ds(2 * i + b, 1), tok], act[:, b:b + 1, tok]).then_inc(a_hi_ready, 1)

            def norm_center(norm, tok):
                eng.wait_ge(c_psum, norm + 1)
                copy(center[:, tok], bank[6][:, tok]).then_inc(c_ready, 1)

            def norm_square(norm, d, tok):
                eng.wait_ge(zc_ready, KD * norm + d + 1)
                act_fn(sq[:, d, tok], sq[:, d, tok], ACT.Square).then_inc(sq_ready, 1)

            def load_sqrt():
                act_fn(eps[:, 3:4], eps[:, 2:3], ACT.Sqrt)

            def norm_tail(norm, tok, parts):
                norm_square(norm, KD - 1, tok)
                eng.wait_ge(mu_psum, norm + 1)
                copy(mu[:, tok], bank[6][:, tok]).then_inc(mu_ready, 1)
                eng.wait_ge(dmu_step, 3 * norm + 3)
                act_fn(var[:, tok], var[:, tok], ACT.Sqrt, bias=eps[:, 0:1]).then_inc(sd_ready, 1)
                if parts:
                    for k in range(KD):
                        high_part(norm + 1, k, tok)

            def high_part(version, k, tok):
                eng.wait_ge(h_ready, KD * version + k + 1)
                copy(h_hi[:, k, tok], h[:, k, tok]).then_inc(h_hi_ready, 1)

            def ffn(f, norm, tok, parts):
                gate_up(f, 0, KD, tok)
                with eng.Fori(1, GU_PAIRS - 1, 1) as i:
                    gate_up(f, i, KD, tok)
                gate_up(f, GU_PAIRS - 1, KH, tok)
                d0 = ffn_unit0(f) + N_GU
                with eng.Fori(0, DOWN_STEPS - 1, 1) as i:
                    for j in range(4):
                        split(d0 + 4 + j, i, KH)
                n = d0 + 4 * (DOWN_STEPS - 1)
                split(n + 4)
                norm_center(norm, tok)
                split(n + 5)
                for d in range(3):
                    norm_square(norm, d, tok)
                split(n + 6)
                for d in range(3, 7):
                    norm_square(norm, d, tok)
                load_sqrt()
                norm_tail(norm, tok, parts)
                split(n + 7)

            def softmax(layer, s):
                g, t0, heads, q0, keys = STEPS[s]
                eng.wait_ge(max_step, 4 * (NS * layer + s) + 4)
                if s >= 4:
                    eng.wait_ge(probs_psum, NS * layer + s - 3)
                act_fn(sm[:, s, ESINK, 0:heads], sm[:, s, DSINK, 0:heads], ACT.Exp)
                for i in range(heads):
                    last = act_fn(probs[:, s % 4, i * keys:(i + 1) * keys],
                                  bank[4 + s % 4][:, i * keys:(i + 1) * keys], ACT.Exp,
                                  bias=sm[:, s, NEG, i:i + 1], scale=HEAD ** -0.5,
                                  accum_out=sm[:, s, SUM, i:i + 1])
                last.then_inc(exp_ready, 1)

            def probs_copy(layer, s):
                eng.wait_ge(probs_psum, NS * layer + s + 1)
                if s == NS - 1:
                    copy(probs_t[:, s % 2, 0:2 * P], bank[s % 2][:, 0:2 * P])
                    copy(probs_t[0:TAIL_Q, s % 2, 2 * P:3 * P],
                         bank[s % 2][0:TAIL_Q, 2 * P:3 * P]).then_inc(pt_act, 1)
                else:
                    copy(probs_t[:, s % 2, :], bank[s % 2][:, :]).then_inc(pt_act, 1)

            def attended(layer, b, steps, src, q0, n):
                eng.wait_ge(pv_done, NS * layer + steps)
                copy(ya[:, :, q0:q0 + n], src[:, 0:QT * n].rearrange("p (t q) -> p t q", t=QT)).then_inc(ya_ready, 1)

            def group_squares(layer, which, src, ready, tok):
                for r in range(RT):
                    ready(r)
                    act_fn(th[:, r, tok], src[:, r, tok], ACT.Square).then_inc(ysq_ready, 1)

            def group_root(layer, which, src, tok):
                eng.wait_ge(rms_psum, 2 * layer + which + 1)
                act_fn(var[:, tok], src[:, tok], ACT.Sqrt, bias=eps[:, 1:2]).then_inc(rms_sd, 1)

            def group_high(layer, which, src, tok):
                for r in range(RT):
                    eng.wait_ge(yn_ready, 8 * layer + 4 * which + r + 1)
                    copy(h_hi[:, 4 * which + r, tok], src[:, r, tok]).then_inc(y_hi_ready, 1)

            def mixer(layer, norm, tok):
                u0, o0 = in_unit0(layer), out_unit0(layer)
                for j in range(RT):
                    split(u0 + 4 + j)
                    eng.wait_ge(w_used, u0 + j + 1)
                    copy(xr[:, j, CONV - 1:], bank[j][:, 0:T]).then_inc(xr_ready, 1)
                split(u0 + U_K + 4)
                eng.wait_ge(w_used, u0 + U_K + 1)
                copy(k_raw[:, :], bank[U_K % 4][:, 0:T]).then_inc(k_raw_ready, 1)
                split(u0 + U_V + 4)
                eng.wait_ge(w_used, u0 + U_V + 1)
                copy(v_raw[:, :], bank[U_V % 4][:, 0:T]).then_inc(v_raw_ready, 1)
                for t in range(QT):
                    eng.wait_ge(gates_psum, RT * layer + t + 1)
                    for x, to, pc in ((0, ra, PC_GA), (1, ig, PC_GX)):
                        c = pc + RT * layer + t
                        act_fn(to[:, t, :], bank[4 + x][:, 0:T], ACT.Sigmoid,
                               bias=par[:, c:c + 1]).then_inc(sig_ready, 1)
                    split(u0 + U_Q + t + 4)
                    eng.wait_ge(w_used, u0 + U_Q + t + 1)
                    copy(q_raw[:, t, :], bank[(U_Q + t) % 4][:, 0:T]).then_inc(q_raw_ready, 1)
                for r in range(RT):
                    eng.wait_ge(sig_ready, 2 * (RT * layer + r) + 2)
                    c = RT * layer + r
                    act_fn(th[:, r, :], ra[:, r, :], ACT.Tanh, scale=decay[:, c:c + 1])
                    act_fn(ra[:, r, :], ra[:, r, :], ACT.Exp, scale=decay[:, c:c + 1]).then_inc(decay_ready, 1)
                split(u0 + U_GATE + 4)
                for s in range(2):
                    softmax(layer, s)
                split(u0 + U_GATE + 5)
                for s in range(2, 4):
                    softmax(layer, s)
                split(u0 + U_GATE + 6)
                for r in range(RT):
                    eng.wait_ge(m_step, 2 * (RT * layer + r) + 2)
                    act_fn(th[:, r, :], th[:, r, :], ACT.Sqrt, scale=-1.0).then_inc(root_ready, 1)
                for r in range(RT):
                    eng.wait_ge(w_used, u0 + U_GATE + r + 1)
                    act_fn(gl[:, r, :], bank[(U_GATE + r) % 4][:, 0:T],
                           ACT.Gelu_apprx_tanh).then_inc(gelu_ready, 1)
                split(u0 + U_GATE + 7)
                probs_copy(layer, 0)
                softmax(layer, 4)
                softmax(layer, 5)
                probs_copy(layer, 2)
                attended(layer, 0, 2, bank[2], 0, P)
                softmax(layer, 6)
                group_squares(layer, 0, yr, lambda r: eng.wait_ge(yr_ready, RT * layer + r + 1), tok)
                probs_copy(layer, 4)
                group_root(layer, 0, bank[7], tok)
                group_high(layer, 0, yr, tok)
                probs_copy(layer, 6)
                attended(layer, 1, 6, bank[3], P, P)
                attended(layer, 2, 7, bank[1], 2 * P, TAIL_Q)
                group_squares(layer, 1, ya, lambda r: eng.wait_ge(ya_ready, 3 * layer + 3), tok)
                split(o0 + 4)
                group_root(layer, 1, bank[0], tok)
                split(o0 + 5)
                group_high(layer, 1, ya, tok)
                split(o0 + 6)
                split(o0 + 7)
                split(o0 + 8)
                split(o0 + 9)
                split(o0 + 10)
                norm_center(norm, tok)
                load_sqrt()
                for d in range(7):
                    norm_square(norm, d, tok)
                norm_tail(norm, tok, True)
                split(o0 + 11)

            eng.dma_start(cst[:], consts).then_inc(consts_in, 16)
            eng.dma_start(x_stage[0:N_META, 0, :], w["meta_tokens"]).then_inc(x_in, 16)
            first = P - N_META
            eng.dma_start(x_stage[N_META:P, 0, :], w["x"][0, 0:first]).then_inc(x_in, 16)
            eng.dma_start(x_stage[:, 1, :], w["x"][0, first:first + P]).then_inc(x_in, 16)
            eng.dma_start(x_stage[0:TAIL_Q, 2, :], w["x"][0, first + P:SEQ]).then_inc(x_in, 16)
            row = 0
            for name in ("ln1_g", "ln1_b", "ln2_g", "ln2_b", "ln3_g", "ln3_b"):
                n = DEPTH * KD
                eng.dma_start(par_rows[row:row + n, 0, :],
                              w[name].rearrange("l (k p) -> (l k) p", p=P)).then_inc(params_in, 16)
                row += n
            n = DEPTH * CONV * RT
            eng.dma_start(par_rows[0:n, 1, :], w["conv_w"].rearrange("l w (k p) -> (l w k) p", p=P)).then_inc(params_in, 16)
            row = n
            for name in ("conv_b", "gate_a_b", "gate_x_b", "lru_lambda", "norm_rec_g"):
                eng.dma_start(par_rows[row:row + DEPTH * RT, 1, :],
                              w[name].rearrange("l (k p) -> (l k) p", p=P)).then_inc(params_in, 16)
                row += DEPTH * RT
            for layer in range(DEPTH):
                for g in range(N_KV):
                    src = w["norm_attn_g"][layer].rearrange("(g t d) -> g t d", g=N_KV, t=QT)[g]
                    eng.dma_start(par_rows[row:row + QT, 1, g * HEAD:(g + 1) * HEAD], src).then_inc(params_in, 16)
                row += QT
            eng.dma_start(sink[:], w["attn_sinks"].partition_broadcast(P)).then_inc(params_in, 16)
            eng.wait_ge(zeroed, 1)
            for layer in range(DEPTH):
                for x, name in enumerate(("gate_a_w", "gate_x_w")):
                    src = w[name][layer].rearrange("(r b) i j -> b i r j", b=2)
                    for b in range(2):
                        at = slice(b * HEAD, (b + 1) * HEAD)
                        eng.dma_start(gate_w[at, layer, x, :, at], src[b]).then_inc(gates_in, 16)

            split(0)
            split(1)
            split(2)
            for k in range(KD):
                high_part(0, k, slice(0, T))
            split(3)
            eng.wait_ge(soft_step, 1)
            act_fn(soft[:, 1, :], soft[:, 0, :], ACT.Exp, scale=-1.0).then_inc(soft_exp, 1)
            eng.wait_ge(consts_in, 16)
            copy(ident16[:], ident).then_inc(masks_ready, 1)
            copy(masks[:], cst[:, C_MA:C_ALL]).then_inc(masks_ready, 1)
            for layer in range(DEPTH):
                last = layer == DEPTH - 1
                ffn(2 * layer, 3 * layer, tokens(False), True)
                mixer(layer, 3 * layer + 1, tokens(last))
                ffn(2 * layer + 1, 3 * layer + 2, tokens(last), not last)
            for b in range(2):
                eng.wait_ge(out_turned, 2 * b + 1)
                copy(out_stage[:, b, :], bank[b][:, :]).then_inc(out_act, 1)

        @block.vector
        def _(eng):
            tt = nc.vector.tensor_tensor
            ts = nc.vector.tensor_scalar
            stt = nc.vector.scalar_tensor_tensor

            def split(n0, i=0, tiles=None):
                if isinstance(i, int) and n0 + 4 * i >= ALL_UNITS:
                    return
                tiles = tiles or unit_tiles(n0 + 4 * i)
                s = slot(n0)
                eng.wait_ge(w_hi_ready, n0 + 4 * i + 1)
                tt(w_lo[:, s, 0:tiles * P], raw[:, s, 0:tiles * P],
                   w_hi[:, s, 0:tiles * P].bitcast(F32), ALU.subtract).then_inc(w_lo_ready, 1)

            def gate_up(f, i, tiles, tok):
                u0 = ffn_unit0(f)
                for j in range(4):
                    t0, b = KF * f + j // 2, j // 2
                    if j % 2 == 0:
                        split(u0 + 4 + j, i, tiles)
                        continue
                    eng.wait_ge(w_used, u0 + 4 * i + j + 1)
                    eng.wait_ge(silu_done, t0 + 2 * i + 1)
                    tt(act[:, b, tok], sg[:, b, tok], bank[j][:, tok], ALU.mult).then_inc(mult_done, 1)
                    split(u0 + 4 + j, i, tiles)
                    eng.wait_ge(a_hi_ready, t0 + 2 * i + 1)
                    at = bass.ds(2 * i + b, 1)
                    tt(a_lo[:, at, tok], act[:, b:b + 1, tok], a_hi[:, at, tok].bitcast(F32),
                       ALU.subtract).then_inc(a_lo_ready, 1)

            def residual(norm, i, d, src, scale, tok):
                at = bass.ds(2 * i + d, 1)
                stt(out=h[:, at, tok], in0=src[:, tok].unsqueeze(1), scalar=scale, in1=h[:, at, tok],
                    op0=ALU.mult, op1=ALU.add).then_inc(z_ready, 1)

            def center_sum(norm, i, d, tok):
                at = bass.ds(2 * i + d, 1)
                eng.wait_ge(z_ready, KD * norm + 2 * i + d + 1)
                to = csum[:, tok].unsqueeze(1)
                if isinstance(i, int) and i == 0 and d == 0:
                    nc.vector.tensor_copy(to, h[:, at, tok]).then_inc(csum_step, 1)
                else:
                    eng.wait_ge(csum_step, 6 * norm + 2 * i + d)
                    tt(to, to, h[:, at, tok], ALU.add).then_inc(csum_step, 1)

            def centered(norm, d, tok):
                eng.wait_ge(c_ready, norm + 1)
                eng.wait_ge(z_ready, KD * norm + d + 1)
                tt(sq[:, d, tok], h[:, d, tok], center[:, tok], ALU.subtract).then_inc(zc_ready, 1)

            def low_part(version, k, tok):
                eng.wait_ge(h_hi_ready, KD * version + k + 1)
                tt(h_lo[:, k, tok], h[:, k, tok], h_hi[:, k, tok].bitcast(F32),
                   ALU.subtract).then_inc(h_lo_ready, 1)

            def norm_tail(norm, tok, parts):
                layer, which = norm // 3, norm % 3

                def subtract(k):
                    tt(h[:, k, tok], h[:, k, tok], mu[:, tok], ALU.subtract).then_inc(t_ready, 1)

                def scale(k):
                    eng.wait_ge(t_ready, KD * norm + k + 1)
                    tt(h[:, k, tok], h[:, k, tok], rstd[:, tok], ALU.mult).then_inc(u_ready, 1)

                def affine(k):
                    g = (2 * which) * DEPTH * KD + layer * KD + k
                    b = g + DEPTH * KD
                    eng.wait_ge(u_ready, KD * norm + k + 1)
                    ts(h[:, k, tok], h[:, k, tok], par[:, g:g + 1], par[:, b:b + 1],
                       ALU.mult, ALU.add).then_inc(h_ready, 1)

                eng.wait_ge(mu_ready, norm + 1)
                tt(dmu[:, tok], mu[:, tok], center[:, tok], ALU.subtract).then_inc(dmu_step, 1)
                subtract(0)
                eng.wait_ge(dmu_step, 3 * norm + 1)
                tt(dmu[:, tok], dmu[:, tok], dmu[:, tok], ALU.mult).then_inc(dmu_step, 1)
                subtract(1)
                eng.wait_ge(dmu_step, 3 * norm + 2)
                eng.wait_ge(var_psum, norm + 1)
                tt(var[:, tok], bank[7][:, tok], dmu[:, tok], ALU.subtract).then_inc(dmu_step, 1)
                for k in range(2, 4):
                    subtract(k)
                eng.wait_ge(sd_ready, norm + 1)
                nc.vector.reciprocal(rstd[:, tok], var[:, tok]).then_inc(rstd_ready, 1)
                for k in range(4, KD):
                    subtract(k)
                eng.wait_ge(rstd_ready, norm + 1)
                for k in range(KD + 2):
                    if k < KD:
                        scale(k)
                    if 1 <= k <= KD:
                        affine(k - 1)
                    if k >= 2 and parts:
                        low_part(norm + 1, k - 2, tok)

            def ffn(f, norm, tok, parts):
                gate_up(f, 0, KD, tok)
                with eng.Fori(1, GU_PAIRS - 1, 1) as i:
                    gate_up(f, i, KD, tok)
                gate_up(f, GU_PAIRS - 1, KH, tok)
                d0 = ffn_unit0(f) + N_GU

                def down(i):
                    for j in range(4):
                        if j % 2 == 0:
                            split(d0 + 4 + j, i, KH)
                            continue
                        eng.wait_ge(w_used, d0 + 4 * i + j + 1)
                        residual(norm, i, j // 2, bank[4 + j // 2], 0.5 / ALPHA, tok)
                        split(d0 + 4 + j, i, KH)
                        center_sum(norm, i, j // 2, tok)

                down(0)
                with eng.Fori(1, DOWN_STEPS - 1, 1) as i:
                    down(i)
                n = d0 + 4 * (DOWN_STEPS - 1)
                split(n + 4)
                for d in range(3):
                    centered(norm, d, tok)
                eng.wait_ge(w_used, n + 2)
                residual(norm, 0, 6, bank[4], 0.5 / ALPHA, tok)
                split(n + 5)
                for d in range(3, 7):
                    centered(norm, d, tok)
                split(n + 6)
                eng.wait_ge(w_used, n + 4)
                residual(norm, 0, 7, bank[5], 0.5 / ALPHA, tok)
                centered(norm, 7, tok)
                norm_tail(norm, tok, parts)
                split(n + 7)

            def conv(layer, r):
                eng.wait_ge(xr_ready, RT * layer + r + 1)
                eng.wait_ge(xr_padded, layer + 1)
                wc = [PC_CONVW + (layer * CONV + k) * RT + r for k in range(CONV)]
                cb = PC_CONVB + layer * RT + r
                base = CONV * (RT * layer + r)
                ts(xc[:, r, :], xr[:, r, 0:T], par[:, wc[0]:wc[0] + 1], par[:, cb:cb + 1],
                   ALU.mult, ALU.add).then_inc(conv_step, 1)
                for k in range(1, CONV):
                    eng.wait_ge(conv_step, base + k)
                    stt(out=xc[:, r, :], in0=xr[:, r, k:k + T], scalar=par[:, wc[k]:wc[k] + 1],
                        in1=xc[:, r, :], op0=ALU.mult, op1=ALU.add).then_inc(conv_step, 1)

            def rope(layer, p):
                if p == 0:
                    eng.wait_ge(k_raw_ready, layer + 1)
                else:
                    eng.wait_ge(q_raw_ready, QT * layer + p)
                src = k_raw[:, :] if p == 0 else q_raw[:, p - 1, :]
                mid = src if p == 0 else q_rot[:, p - 1, :]
                n = 5 * layer + p
                eng.wait_ge(swap_psum, n + 1)
                tt(turn[:, p % 2, :], bank[6][:, 0:T], sin, ALU.mult).then_inc(rope_s, 1)
                tt(mid, src, cos, ALU.mult).then_inc(rope_c, 1)
                eng.wait_ge(rope_c, n + 1)
                if p == 0:
                    for g in range(N_KV):
                        at = slice(g * HEAD, (g + 1) * HEAD)
                        tt(k_rot[at, g, :], k_raw[at, :], turn[at, 0, :], ALU.add).then_inc(rope_ready, 1)
                else:
                    tt(mid, mid, turn[:, p % 2, :], ALU.add).then_inc(rope_ready, 1)

            def values(layer):
                eng.wait_ge(v_psum, layer + 1)
                nc.vector.tensor_copy(v_tok[:, 0:2, :], bank[7][:, 0:2 * P].rearrange(
                    "p (b c) -> p b c", b=2)).then_inc(v_ready, 1)
                nc.vector.tensor_copy(v_tok[0:TAIL_Q, 2, :], bank[7][0:TAIL_Q, 2 * P:3 * P]).then_inc(v_ready, 1)

            def decay_root(layer, r):
                n = RT * layer + r
                eng.wait_ge(decay_ready, n + 1)
                tt(yr[:, r, :], ra[:, r, :], ra[:, r, :], ALU.mult).then_inc(m_step, 1)
                tt(ig[:, r, :], ig[:, r, :], xc[:, r, :], ALU.mult).then_inc(ix_ready, 1)
                eng.wait_ge(m_step, 2 * n + 1)
                stt(out=th[:, r, :], in0=yr[:, r, :], scalar=1.0, in1=th[:, r, :],
                    op0=ALU.add, op1=ALU.mult).then_inc(m_step, 1)

            def scan_input(layer, r):
                n = RT * layer + r
                eng.wait_ge(root_ready, n + 1)
                eng.wait_ge(ix_ready, n + 1)
                tt(ig[:, r, :], ig[:, r, :], th[:, r, :], ALU.mult).then_inc(gx_ready, 1)

            def scan(layer, r):
                n = RT * layer + r
                eng.wait_ge(gx_ready, n + 1)
                nc.vector.tensor_tensor_scan(yr[:, r, :], ra[:, r, :], ig[:, r, :], 0.0,
                                             ALU.mult, ALU.add).then_inc(scan_ready, 1)

            def gated(layer, r):
                n = RT * layer + r
                eng.wait_ge(scan_ready, n + 1)
                eng.wait_ge(gelu_ready, n + 1)
                tt(yr[:, r, :], yr[:, r, :], gl[:, r, :], ALU.mult).then_inc(yr_ready, 1)

            def maxima(layer, s):
                g, t0, heads, q0, keys = STEPS[s]
                n = 4 * (NS * layer + s)
                eng.wait_ge(scores_psum, NS * layer + s + 1)
                v = sm[:, s, :, 0:heads]
                if g is None:
                    own = sink_tail[:, layer:layer + 1]
                else:
                    own = sink[:, layer, 4 * g + t0:4 * g + t0 + heads]
                nc.vector.tensor_reduce(v[:, MX], bank[4 + s % 4][:, 0:heads * keys].rearrange(
                    "p (h k) -> p h k", h=heads), AX.X, ALU.max).then_inc(max_step, 1)
                eng.wait_ge(max_step, n + 1)
                stt(out=v[:, MAX], in0=v[:, MX], scalar=HEAD ** -0.5, in1=own,
                    op0=ALU.mult, op1=ALU.max).then_inc(max_step, 1)
                eng.wait_ge(max_step, n + 2)
                ts(v[:, NEG], v[:, MAX], -1.0, None, ALU.mult).then_inc(max_step, 1)
                tt(v[:, DSINK], own, v[:, MAX], ALU.subtract).then_inc(max_step, 1)

            def normalize(layer, s):
                g, t0, heads, q0, keys = STEPS[s]
                n = 2 * (NS * layer + s)
                v = sm[:, s, :, 0:heads]
                eng.wait_ge(exp_ready, NS * layer + s + 1)
                tt(v[:, Z], v[:, SUM], v[:, ESINK], ALU.add).then_inc(sum_step, 1)
                eng.wait_ge(sum_step, n + 1)
                nc.vector.reciprocal(v[:, RZ], v[:, Z]).then_inc(sum_step, 1)
                eng.wait_ge(sum_step, n + 2)
                for i in range(heads):
                    at = probs[:, s % 4, i * keys:(i + 1) * keys]
                    last = ts(at, at, sm[:, s, RZ, i:i + 1], None, ALU.mult)
                last.then_inc(probs_ready, 1)

            def probs_copy(layer, s):
                eng.wait_ge(probs_psum, NS * layer + s + 1)
                nc.vector.tensor_copy(probs_t[:, s % 2, :], bank[s % 2][:, :]).then_inc(pt_dve, 1)

            def group_norm(layer, which, src, pc, tok):
                eng.wait_ge(rms_sd, 2 * layer + which + 1)
                nc.vector.reciprocal(rstd[:, tok], var[:, tok]).then_inc(rms_ready, 1)
                eng.wait_ge(rms_ready, 2 * layer + which + 1)
                n = 8 * layer + 4 * which
                for r in range(RT + 1):
                    if r < RT:
                        c = pc + RT * layer + r
                        stt(out=src[:, r, tok], in0=src[:, r, tok], scalar=par[:, c:c + 1],
                            in1=rstd[:, tok], op0=ALU.mult, op1=ALU.mult).then_inc(yn_ready, 1)
                    if r >= 1:
                        eng.wait_ge(y_hi_ready, n + r)
                        tt(h_lo[:, 4 * which + r - 1, tok], src[:, r - 1, tok],
                           h_hi[:, 4 * which + r - 1, tok].bitcast(F32), ALU.subtract).then_inc(y_lo_ready, 1)

            def mixer(layer, norm, tok):
                u0, o0 = in_unit0(layer), out_unit0(layer)
                nc.vector.memset(xr[:, :, 0:CONV - 1], 0.0).then_inc(xr_padded, 1)
                for j in range(RT):
                    split(u0 + 4 + j)
                conv(layer, 0)
                split(u0 + 8)
                conv(layer, 1)
                split(u0 + 9)
                conv(layer, 2)
                rope(layer, 0)
                split(u0 + 10)
                conv(layer, 3)
                values(layer)
                for t in range(QT):
                    if t < QT - 1:
                        split(u0 + 11 + t)
                    rope(layer, t + 1)
                eng.wait_ge(rope_ready, 6 * layer + 6)
                nc.vector.tensor_copy(q_tail[:].rearrange("p (t q) -> p t q", t=QT),
                                      q_rot[:, :, 2 * P:T]).then_inc(q_tail_ready, 1)
                for r in range(RT):
                    decay_root(layer, r)
                split(u0 + 14)
                maxima(layer, 0)
                maxima(layer, 1)
                normalize(layer, 0)
                split(u0 + 15)
                maxima(layer, 2)
                normalize(layer, 1)
                maxima(layer, 3)
                normalize(layer, 2)
                split(u0 + 16)
                normalize(layer, 3)
                for r in range(RT):
                    scan_input(layer, r)
                for r in range(RT):
                    scan(layer, r)
                for r in range(RT):
                    gated(layer, r)
                split(u0 + 17)
                maxima(layer, 4)
                probs_copy(layer, 1)
                maxima(layer, 5)
                normalize(layer, 4)
                maxima(layer, 6)
                normalize(layer, 5)
                probs_copy(layer, 3)
                normalize(layer, 6)
                group_norm(layer, 0, yr, PC_GREC, tok)
                probs_copy(layer, 5)
                split(o0 + 4)
                for j in range(4):
                    if j == 1:
                        split(o0 + 5)
                    if j == 2:
                        group_norm(layer, 1, ya, PC_GATT, tok)
                        split(o0 + 6)
                    eng.wait_ge(w_used, o0 + j + 1)
                    for d in range(2 * j, 2 * j + 2):
                        stt(out=h[:, d, tok], in0=bank[4 + d % 4][:, tok], scalar=1.0 / ALPHA,
                            in1=h[:, d, tok], op0=ALU.mult, op1=ALU.add).then_inc(z_rec_ready, 1)
                split(o0 + 7)
                for j in range(4):
                    if j < 3:
                        split(o0 + 8 + j)
                    eng.wait_ge(w_used, o0 + 4 + j + 1)
                    for d in range(2 * j, 2 * j + 2):
                        eng.wait_ge(z_rec_ready, KD * layer + d + 1)
                        residual(norm, 0, d, bank[d % 4], 1.0 / ALPHA, tok)
                    if j < 3:
                        for d in range(2 * j, 2 * j + 2):
                            center_sum(norm, 0, d, tok)
                for d in range(KD):
                    centered(norm, d, tok)
                norm_tail(norm, tok, True)
                split(o0 + 11)

            eng.wait_ge(params_turned, 1)
            nc.vector.tensor_copy(par[:, 0:LN_COLS], bank[4][:, 0:LN_COLS]).then_inc(params_ready, 1)
            eng.wait_ge(params_turned, 2)
            nc.vector.tensor_copy(par[:, LN_COLS:PC_ALL], bank[5][:, 0:ROWS_B]).then_inc(params_ready, 1)
            split(0)
            split(1)
            split(2)
            for k in range(KD + 1):
                if k < KD:
                    eng.wait_ge(x_turned, k + 1)
                    nc.vector.tensor_copy(h[:, k, :], bank[k % 4][:, 0:T]).then_inc(h_ready, 1)
                if k >= 1:
                    low_part(0, k - 1, slice(0, T))
            split(3)

            eng.wait_ge(params_ready, 2)
            lam = par[:, PC_LAM:PC_LAM + DEPTH * RT]
            steps = [0]

            def chain(instruction):
                steps[0] += 1
                instruction.then_inc(soft_step, 1)
                eng.wait_ge(soft_step, steps[0])

            chain(stt(out=soft[:, 0, :], in0=lam, scalar=-1.0, in1=lam, op0=ALU.mult, op1=ALU.max))
            eng.wait_ge(soft_exp, 1)
            chain(ts(soft[:, 2, :], soft[:, 1, :], 2.0, None, ALU.add))
            chain(nc.vector.reciprocal(soft[:, 2, :], soft[:, 2, :]))
            chain(tt(soft[:, 1, :], soft[:, 1, :], soft[:, 2, :], ALU.mult))
            chain(tt(soft[:, 2, :], soft[:, 1, :], soft[:, 1, :], ALU.mult))
            chain(ts(soft[:, 3, :], soft[:, 2, :], 1.0 / 17, 1.0 / 15, ALU.mult, ALU.add))
            for odd in (13, 11, 9, 7, 5, 3, 1):
                chain(tt(soft[:, 3, :], soft[:, 3, :], soft[:, 2, :], ALU.mult))
                chain(ts(soft[:, 3, :], soft[:, 3, :], 1.0 / odd, None, ALU.add))
            chain(tt(soft[:, 3, :], soft[:, 3, :], soft[:, 1, :], ALU.mult))
            chain(ts(soft[:, 0, :], lam, -1.0, 0.0, ALU.mult, ALU.max))
            chain(stt(out=decay[:], in0=soft[:, 3, :], scalar=2.0, in1=soft[:, 0, :],
                      op0=ALU.mult, op1=ALU.add))
            chain(ts(decay[:], decay[:], -LRU_C, None, ALU.mult))
            eng.wait_ge(consts_in, 16)
            for layer in range(DEPTH):
                chain(tt(sink_pick[:, layer, :], sink[:, layer, :], cst[:, C_PICK:C_PICK + N_Q], ALU.mult))
            chain(nc.vector.tensor_reduce(sink_tail[:], sink_pick[:], AX.X, ALU.add))

            for layer in range(DEPTH):
                last = layer == DEPTH - 1
                ffn(2 * layer, 3 * layer, tokens(False), True)
                mixer(layer, 3 * layer + 1, tokens(last))
                ffn(2 * layer + 1, 3 * layer + 2, tokens(last), not last)
            for b in range(2):
                eng.wait_ge(out_turned, 2 * b + 2)
                nc.vector.tensor_copy(out_stage[:, 2 + b, :], bank[2 + b][:, :]).then_inc(out_dve, 1)

        @block.tensor
        def _(eng):
            mm = nc.tensor.matmul

            def product(to, s, at, x_hi, x_lo, start, stop):
                mm(to, w_hi[:, s, at:at + P], x_hi, start=start, stop=False)
                mm(to, w_hi[:, s, at:at + P], x_lo, start=False, stop=False)
                return mm(to, w_lo[:, s, at:at + P], x_hi, start=False, stop=stop)

            def wait_unit(n0, i=0):
                eng.wait_ge(w_lo_ready, n0 + 4 * i + 1)

            def project(n0, i, to, tok):
                wait_unit(n0, i)
                for k in range(KD):
                    last = product(to[:, tok], slot(n0), k * P, h_hi[:, k, tok], h_lo[:, k, tok],
                                   k == 0, k == KD - 1)
                last.then_inc(w_used, 1)

            def first_units(n0, version, tok, count=3):
                for k in range(KD):
                    eng.wait_ge(h_lo_ready, KD * version + k + 1)
                    for j in range(count):
                        if k == 0:
                            wait_unit(n0 + j)
                        last = product(bank[j][:, tok], slot(n0 + j), k * P, h_hi[:, k, tok],
                                       h_lo[:, k, tok], k == 0, k == KD - 1)
                        if k == KD - 1:
                            last.then_inc(w_used, 1)

            def norm_tail(norm, tok):
                eng.wait_ge(sumsq_step, 5 * norm + 5)
                mm(bank[7][:, tok], ones_d[:], sumsq[:, tok], start=True, stop=False)
                eng.wait_ge(sq_ready, KD * norm + 7)
                mm(bank[7][:, tok], ones_d[:], sq[:, 6, tok], start=False, stop=False)
                eng.wait_ge(z_ready, KD * norm + 8)
                mm(bank[6][:, tok], ones_d[:], h[:, 7, tok], start=False, stop=True).then_inc(mu_psum, 1)
                eng.wait_ge(sq_ready, KD * norm + 8)
                mm(bank[7][:, tok], ones_d[:], sq[:, 7, tok], start=False, stop=True).then_inc(var_psum, 1)

            def norm_center(norm, tok):
                eng.wait_ge(csum_step, 6 * norm + 6)
                mm(bank[6][:, tok], ones_c[:], csum[:, tok], start=True, stop=True).then_inc(c_psum, 1)

            def norm_mean(norm, tok):
                eng.wait_ge(c_ready, norm + 1)
                eng.wait_ge(z_ready, KD * norm + 7)
                mm(bank[6][:, tok], ones_d[:], csum[:, tok], start=True, stop=False)
                mm(bank[6][:, tok], ones_d[:], h[:, 6, tok], start=False, stop=False)

            def ffn(f, norm, version, tok):
                u0 = ffn_unit0(f)
                first_units(u0, version, tok)
                project(u0 + 3, 0, bank[3], tok)
                with eng.Fori(1, GU_PAIRS, 1) as i:
                    for j in range(4):
                        eng.wait_ge((silu_done, mult_done)[j % 2], KF * f + 2 * i + j // 2 - 1)
                        project(u0 + j, i, bank[j], tok)
                d0 = u0 + N_GU

                def down(i, j):
                    n0 = d0 + j
                    if j % 2 == 0 and not (isinstance(i, int) and i == 0):
                        eng.wait_ge(z_ready, KD * norm + 2 * i + j // 2 - 1)
                    wait_unit(n0, i)
                    for k in range(KH):
                        c = (j % 2) * KH + k
                        if isinstance(i, int) and i == 0 and j < 2:
                            eng.wait_ge(a_lo_ready, KF * f + c + 1)
                        last = product(bank[4 + j // 2][:, tok], slot(n0), k * P, a_hi[:, c, tok],
                                       a_lo[:, c, tok], c == 0, c == KF - 1)
                    last.then_inc(w_used, 1)

                for j in range(4):
                    down(0, j)
                with eng.Fori(1, DOWN_STEPS - 1, 1) as i:
                    for j in range(4):
                        down(i, j)
                down(DOWN_STEPS - 1, 0)
                norm_center(norm, tok)
                down(DOWN_STEPS - 1, 1)
                down(DOWN_STEPS - 1, 2)
                norm_mean(norm, tok)
                down(DOWN_STEPS - 1, 3)
                norm_tail(norm, tok)

            def gates(layer, r):
                n = RT * layer + r
                eng.wait_ge(conv_step, CONV * n + 4)
                if r >= 1:
                    eng.wait_ge(sig_ready, 2 * n)
                elif layer == 0:
                    eng.wait_ge(gates_in, 16 * 4 * DEPTH)
                mm(bank[4][:, 0:T], gate_w[:, layer, 0, r, :], xc[:, r, :], start=True, stop=True)
                mm(bank[5][:, 0:T], gate_w[:, layer, 1, r, :], xc[:, r, :], start=True,
                   stop=True).then_inc(gates_psum, 1)

            def swap(layer, p):
                n = 5 * layer + p
                if p == 0:
                    eng.wait_ge(k_raw_ready, layer + 1)
                    src = k_raw[:, :]
                else:
                    eng.wait_ge(q_raw_ready, QT * layer + p)
                    eng.wait_ge(rope_s, n)
                    src = q_raw[:, p - 1, :]
                mm(bank[6][:, 0:T], perm, src, start=True, stop=True).then_inc(swap_psum, 1)

            def turn_values(layer):
                eng.wait_ge(v_raw_ready, layer + 1)
                for b in range(3):
                    n = min(P, T - b * P)
                    last = nc.tensor.transpose(bank[7][0:n, b * P:(b + 1) * P],
                                               v_raw[:, b * P:b * P + n], ident)
                last.then_inc(v_psum, 1)

            def scores(layer, s):
                g, t0, heads, q0, keys = STEPS[s]
                to = bank[4 + s % 4]
                if s == 0:
                    eng.wait_ge(rope_ready, 6 * layer + 6)
                    eng.wait_ge(sig_ready, 2 * RT * (layer + 1))
                    eng.wait_ge(v_ready, 2 * layer + 2)
                    eng.wait_ge(masks_ready, 2)
                if s >= 4:
                    eng.wait_ge(exp_ready, NS * layer + s - 3)
                m0 = {128: 0, 256: P, 272: 3 * P}[keys]
                mm(to[:, 0:heads * keys], ident16[:], masks[:, m0:m0 + keys].unsqueeze(1).to_broadcast(
                    [P, heads, keys]), start=True, stop=False, skip_group_check=True)
                if g is None:
                    eng.wait_ge(q_tail_ready, layer + 1)
                    for g in range(N_KV):
                        last = mm(to[g * HEAD:(g + 1) * HEAD, 0:keys], q_tail[:],
                                  k_rot[:, g, 0:keys], start=False, stop=True, skip_group_check=True)
                else:
                    for i in range(heads):
                        last = mm(to[:, i * keys:(i + 1) * keys], q_rot[:, t0 + i, q0:q0 + P],
                                  k_rot[:, g, 0:keys], start=False, stop=(i == heads - 1), skip_group_check=True)
                last.then_inc(scores_psum, 1)

            def turn_probs(layer, s):
                g, t0, heads, q0, keys = STEPS[s]
                to = bank[s % 2]
                eng.wait_ge(probs_ready, NS * layer + s + 1)
                if s < 2:
                    eng.wait_ge(gelu_ready, RT * layer + RT)
                elif s % 2:
                    eng.wait_ge(pt_dve, 3 * layer + s // 2)
                else:
                    eng.wait_ge(pt_act, 4 * layer + s // 2)
                for b in range(-(-heads * keys // P)):
                    n = min(P, heads * keys - b * P)
                    last = nc.tensor.transpose(to[0:n, b * P:(b + 1) * P],
                                               probs[:, s % 4, b * P:b * P + n], ident)
                last.then_inc(probs_psum, 1)

            def attend(layer, s):
                g, t0, heads, q0, keys = STEPS[s]
                if s % 2:
                    eng.wait_ge(pt_dve, 3 * layer + s // 2 + 1)
                else:
                    eng.wait_ge(pt_act, 4 * layer + s // 2 + 1)
                pt = probs_t[:, s % 2, :]
                if g is None:
                    eng.wait_ge(pt_dve, 3 * layer + 3)
                    for g in range(N_KV):
                        at = slice(g * HEAD, (g + 1) * HEAD)
                        for b in range(3):
                            n = min(P, T - b * P)
                            last = mm(bank[1][at, 0:HEAD], v_tok[0:n, b, at],
                                      pt[0:n, b * P + g * HEAD:b * P + (g + 1) * HEAD],
                                      start=(b == 0), stop=(b == 2))
                else:
                    at = slice(g * HEAD, (g + 1) * HEAD)
                    kb = keys // P
                    to = bank[2] if s < 2 else bank[3]
                    view = pt.rearrange("p (h b q) -> p h b q", h=heads, b=kb)
                    for b in range(kb):
                        last = mm(to[at, t0 * P:(t0 + heads) * P], v_tok[:, b, at], view[:, :, b, :],
                                  start=(b == 0), stop=(b == kb - 1))
                last.then_inc(pv_done, 1)

            def group_mean(layer, which, to, tok):
                eng.wait_ge(ysq_step, 6 * layer + 3 * which + 3)
                mm(to[:, tok], ones_r[:], sumsq[:, tok], start=True, stop=True).then_inc(rms_psum, 1)

            def project_out(layer, which, j, banks, tok):
                n0 = out_unit0(layer) + 4 * which + j
                wait_unit(n0)
                for i in range(2):
                    for k in range(4):
                        if j == 0 and i == 0:
                            eng.wait_ge(y_lo_ready, 8 * layer + 4 * which + k + 1)
                        c = 4 * which + k
                        last = product(banks[i][:, tok], slot(n0), k * 2 * P + i * P, h_hi[:, c, tok],
                                       h_lo[:, c, tok], k == 0, k == 3)
                    if which == 1 and j == 3 and i == 0:
                        norm_center(3 * layer + 1, tok)
                last.then_inc(w_used, 1)

            def mixer(layer, norm, version, tok):
                u0 = in_unit0(layer)
                full = slice(0, T)
                first_units(u0, version, full)
                project(u0 + 3, 0, bank[3], full)

                def unit(j):
                    if j < U_K + 4:
                        eng.wait_ge(xr_ready, RT * layer + j - RT + 1)
                    elif j == U_K + 4:
                        eng.wait_ge(k_raw_ready, layer + 1)
                    elif j == U_K + 5:
                        eng.wait_ge(v_raw_ready, layer + 1)
                    else:
                        eng.wait_ge(q_raw_ready, QT * layer + j - U_Q - 3)
                    project(u0 + j, 0, bank[j % 4], full)

                unit(U_K)
                gates(layer, 0)
                unit(U_V)
                swap(layer, 0)
                gates(layer, 1)
                unit(U_Q)
                turn_values(layer)
                gates(layer, 2)
                unit(U_Q + 1)
                gates(layer, 3)
                swap(layer, 1)
                unit(U_Q + 2)
                swap(layer, 2)
                unit(U_Q + 3)
                swap(layer, 3)
                unit(U_GATE)
                swap(layer, 4)
                unit(U_GATE + 1)
                scores(layer, 0)
                scores(layer, 1)
                scores(layer, 2)
                scores(layer, 3)
                unit(U_GATE + 2)
                unit(U_GATE + 3)
                scores(layer, 4)
                turn_probs(layer, 0)
                scores(layer, 5)
                turn_probs(layer, 1)
                scores(layer, 6)
                attend(layer, 0)
                turn_probs(layer, 2)
                attend(layer, 1)
                turn_probs(layer, 3)
                attend(layer, 2)
                group_mean(layer, 0, bank[7], tok)
                turn_probs(layer, 4)
                attend(layer, 3)
                turn_probs(layer, 5)
                attend(layer, 4)
                turn_probs(layer, 6)
                attend(layer, 5)
                attend(layer, 6)
                for j in range(4):
                    if j >= 2:
                        eng.wait_ge(z_rec_ready, KD * layer + 2 * j - 2)
                    project_out(layer, 0, j, (bank[4 + 2 * (j % 2)], bank[5 + 2 * (j % 2)]), tok)
                    if j == 1:
                        group_mean(layer, 1, bank[0], tok)
                for j in range(4):
                    if j >= 2:
                        eng.wait_ge(z_ready, KD * norm + 2 * j - 2)
                    project_out(layer, 1, j, (bank[2 * (j % 2)], bank[2 * (j % 2) + 1]), tok)
                norm_mean(norm, tok)
                norm_tail(norm, tok)

            eng.wait_ge(consts_in, 16)
            eng.wait_ge(params_in, 16 * (6 + 1 + 5 + 2 * DEPTH + 1))
            nc.tensor.transpose(bank[4][:, 0:LN_COLS], par_rows[0:LN_COLS, 0, :],
                                cst[0:LN_COLS, C_ID:C_ID + LN_COLS]).then_inc(params_turned, 1)
            nc.tensor.transpose(bank[5][:, 0:ROWS_B], par_rows[0:ROWS_B, 1, :],
                                cst[0:ROWS_B, C_ID:C_ID + ROWS_B]).then_inc(params_turned, 1)
            eng.wait_ge(x_in, 64)
            for k in range(KD):
                if k >= 4:
                    eng.wait_ge(h_ready, k - 3)
                for a in range(3):
                    n = min(P, T - a * P)
                    last = nc.tensor.transpose(bank[k % 4][:, a * P:a * P + n],
                                               x_stage[0:n, a, k * P:(k + 1) * P],
                                               cst[0:n, C_ID:C_ID + n])
                last.then_inc(x_turned, 1)
            eng.wait_ge(zeroed, 8)
            eng.wait_ge(h_ready, KD)
            for layer in range(DEPTH):
                last = layer == DEPTH - 1
                ffn(2 * layer, 3 * layer, 3 * layer, tokens(False))
                mixer(layer, 3 * layer + 1, 3 * layer + 1, tokens(last))
                ffn(2 * layer + 1, 3 * layer + 2, 3 * layer + 2, tokens(last))
            for k in range(KD):
                eng.wait_ge(h_ready, KD * 3 * DEPTH + k + 1)
                for a in range(2):
                    q0 = N_META + a * P
                    mv = nc.tensor.transpose(bank[2 * a + k // 4][:, (k % 4) * P:(k % 4 + 1) * P],
                                             h[:, k, q0:q0 + P], ident)
                    if k % 4 == 3:
                        mv.then_inc(out_turned, 1)


_INS = ["x", "meta_tokens", "ffn1_w_gate", "ffn1_w_up", "ffn1_w_down", "ln1_g", "ln1_b", "w_in", "conv_w",
        "conv_b", "gate_a_w", "gate_a_b", "gate_x_w", "gate_x_b", "lru_lambda", "attn_sinks", "norm_rec_g",
        "norm_attn_g", "w_out", "ln2_g", "ln2_b", "ffn2_w_gate", "ffn2_w_up", "ffn2_w_down", "ln3_g", "ln3_b"]


def kernel(**inputs):
    import concourse.bacc as _bacc
    from concourse.bass_utils import run_bass_kernel_spmd as _run

    nc = _bacc.Bacc("TRN2", target_bir_lowering=False, num_devices=1)
    arrays, aps = {}, {}
    for name in _INS + ["shape_constants"]:
        a = np.ascontiguousarray(constants() if name == "shape_constants" else inputs[name])
        arrays[f"in_{name}"] = a
        aps[name] = nc.dram_tensor(f"in_{name}", a.shape, mybir.dt.from_np(a.dtype), kind="ExternalInput").ap()
    out = nc.dram_tensor("out", (1, SEQ, D_MODEL), F32, kind="ExternalOutput").ap()
    build(nc, aps, aps["shape_constants"], out)
    r = _run(nc, [arrays], core_ids=[0])
    return r.results[0]["out"]
```

```python
from contextlib import ExitStack

import numpy as np

import concourse.bass as bass
from concourse import mybir

F32 = mybir.dt.float32
F32R = mybir.dt.float32r
BF16 = mybir.dt.bfloat16
ACT = mybir.ActivationFunctionType
ALU = mybir.AluOpType
AX = mybir.AxisListType

P = 128
D_MODEL = 1024
SEQ = 256
DEPTH = 2
N_META = 16
D_FF = 2816
REC = 512
CONV = 4
LRU_C = 8.0
N_Q = 8
N_KV = 2
HEAD = 64
ATTN = N_Q * HEAD
WINDOW = 128
ROPE_DIM = HEAD // 4
ROPE_THETA = 500000.0
ALPHA = (2.0 * DEPTH) ** 0.25
LN_EPS = 1e-5
RMS_EPS = 1e-6
NEG_INF = -1e30
T = N_META + SEQ

KD = D_MODEL // P
KF = D_FF // P
RT = REC // P
QT = ATTN // P
SLOTS = 4
HALF = KD // 2
GU_STEPS = KF // 2
DOWN_STEPS = KD // 2
DOWN_K = [(0, 6), (6, 11), (11, 17), (17, 22)]
SLOT_TILES = 2 * 6

N_GU = 4 * GU_STEPS
N_DOWN = 4 * DOWN_STEPS
IN_PAIRS = 7
IN_BANKS = [(0, 1), (2, 3), (4, 5), (0, 1), (2, 3), (0, 1), (2, 0)]
N_IN = 2 * IN_PAIRS
N_OUT = KD
FFN_UNITS = N_GU + N_DOWN
LAYER_UNITS = 2 * FFN_UNITS + N_IN + N_OUT
ALL_UNITS = DEPTH * LAYER_UNITS

STEPS = [(0, 0, 4, 0, 128), (1, 0, 4, 0, 128), (None, 0, 1, 256, 272),
         (0, 0, 2, 128, 256), (0, 2, 2, 128, 256), (1, 0, 2, 128, 256), (1, 2, 2, 128, 256)]
NS = len(STEPS)
TAIL_STEP = 2
SCORE_BANKS = (6, 5)
TURN_BANKS = (7, 3)
PV_BANKS = (1, 1, 0, 2, 2, 2, 2)
OUT_BANKS = (1, 0, 4)
ATT_BANKS = (5, 2, 4, 1)
TAIL_Q = T - 2 * P

CENTER_TILES = (6, 4, 6)

C_ID, C_PERM, C_COS, C_SIN, C_PICK = 0, P, 2 * P, 2 * P + T, 2 * P + 2 * T
C_MA = C_PICK + N_Q
C_MB, C_MC = C_MA + P, C_MA + 3 * P
C_ALL = C_MC + T

LN_COLS = 6 * DEPTH * KD
PC_CONVW = LN_COLS
PC_CONVB = PC_CONVW + DEPTH * CONV * RT
PC_GA, PC_GX, PC_LAM, PC_GREC, PC_GATT = (PC_CONVB + DEPTH * RT * i for i in range(1, 6))
PC_ALL = PC_GATT + DEPTH * QT
ROWS_B = PC_ALL - LN_COLS


def constants():
    c = np.zeros((P, C_ALL), np.float32)
    c[:, C_ID:C_ID + P] = np.eye(P, dtype=np.float32)
    half = ROPE_DIM // 2
    pos = np.arange(T, dtype=np.float32)
    inv = np.float32(ROPE_THETA) ** (-np.arange(0, ROPE_DIM, 2, dtype=np.float32) / np.float32(ROPE_DIM))
    ang = pos[:, None] * inv[None, :]
    cos, sin = np.cos(ang), np.sin(ang)
    c[:, C_COS:C_COS + T] = 1.0
    for base in (0, HEAD):
        for d in range(half):
            a, b = base + d, base + half + d
            c[b, C_PERM + a] = 1.0
            c[a, C_PERM + b] = 1.0
            c[a, C_COS:C_COS + T] = cos[:, d]
            c[b, C_COS:C_COS + T] = cos[:, d]
            c[a, C_SIN:C_SIN + T] = -sin[:, d]
            c[b, C_SIN:C_SIN + T] = sin[:, d]

    def mask(q, k):
        seen = (k <= q) & ((k < N_META) | (q - k < WINDOW))
        return np.where(seen, 0.0, NEG_INF).astype(np.float32)

    rows = np.arange(P)[:, None]
    c[:, C_MA:C_MA + P] = mask(rows, np.arange(P)[None, :])
    c[:, C_MB:C_MB + 2 * P] = mask(rows + P, np.arange(2 * P)[None, :])
    c[:, C_MC:C_MC + T] = mask(2 * P + rows % TAIL_Q, np.arange(T)[None, :])
    for p in range(P):
        c[p, C_PICK + 4 * (p // 64) + (p % 64) // TAIL_Q] = 1.0
    return c


def build(nc, w, consts, out):
    with ExitStack() as ctx:
        def sb(name, shape, dt=F32):
            return ctx.enter_context(nc.sbuf_tensor(name, shape, dt))

        def sem(name):
            return ctx.enter_context(nc.semaphore(name))

        banks = ctx.enter_context(nc.psum_tensor("banks", [P, 8, 512], F32))
        bank = [banks[:, i, :] for i in range(8)]
        arena_bytes = 2 * KF * T * 4
        arena = sb("arena", [P, arena_bytes // 4])
        arena_at = nc.sbuf_base - arena_bytes
        a_hi = nc.alloc_sbuf_tensor_at("a_hi", [P, KF, T], F32R, offset=arena_at)
        a_lo = nc.alloc_sbuf_tensor_at("a_lo", [P, KF, T], F32R, offset=arena_at + KF * T * 4)
        taken = [arena_at]

        def mix(name, shape):
            size = int(np.prod(shape[1:])) * 4
            t = nc.alloc_sbuf_tensor_at(name, shape, F32, offset=taken[0])
            taken[0] += (size + 31) // 32 * 32
            assert taken[0] <= arena_at + arena_bytes
            return t

        x_stage = nc.alloc_sbuf_tensor_at("x_stage", [P, 3, D_MODEL], F32, offset=arena_at)
        out_stage = nc.alloc_sbuf_tensor_at("out_stage", [P, 4, 512], F32, offset=arena_at)

        h = sb("h", [P, KD, T])
        h_hi = sb("h_hi", [P, KD, T], F32R)
        h_lo = sb("h_lo", [P, KD, T], F32R)
        raw = sb("raw", [P, SLOTS, SLOT_TILES * P])
        w_hi = sb("w_hi", [P, SLOTS, SLOT_TILES * P], F32R)
        w_lo = sb("w_lo", [P, SLOTS, SLOT_TILES * P], F32R)

        cst = sb("cst", [P, C_ALL])
        masks = sb("masks", [P, 3 * P + T], BF16)
        ident16 = sb("ident16", [P, P], BF16)
        ones_c = sb("ones_c", [P, 2, P])
        ones_d = sb("ones_d", [P, P])
        ones_r = sb("ones_r", [P, P])
        eps = sb("eps", [P, 4])
        par_rows = sb("par_rows", [P, 2, P])
        par = sb("par", [P, PC_ALL])
        decay = sb("decay", [P, DEPTH * RT])
        soft = sb("soft", [P, 4, DEPTH * RT])
        sink = sb("sink", [P, DEPTH, N_Q])
        sink_pick = sb("sink_pick", [P, DEPTH, N_Q])
        sink_tail = sb("sink_tail", [P, DEPTH])
        gate_w = sb("gate_w", [P, DEPTH, 2, RT, P])

        sg = sb("sg", [P, 2, T])
        act = sb("act", [P, 2, T])
        csum = sb("csum", [P, T])
        center = sb("center", [P, T])
        sq = sb("sq", [P, KD, T])
        sumsq = sb("sumsq", [P, T])
        dsq = sb("dsq", [P, T])
        var = sb("var", [P, T])
        rstd = sb("rstd", [P, T])

        xr = mix("xr", [P, RT, T + CONV - 1])
        xc = mix("xc", [P, RT, T])
        ra = mix("ra", [P, RT, T])
        th = mix("th", [P, RT, T])
        ig = mix("ig", [P, RT, T])
        gl = mix("gl", [P, RT, T])
        yr = mix("yr", [P, RT, T])
        q_raw = mix("q_raw", [P, QT, T])
        q_rot = mix("q_rot", [P, QT, T])
        ya = mix("ya", [P, QT, T])
        kv_raw = mix("kv_raw", [P, 2, T])
        k_raw, v_raw = kv_raw[:, 0, :], kv_raw[:, 1, :]
        k_rot = sb("k_rot", [P, N_KV, T])
        v_tok = sb("v_tok", [P, 3, P])
        q_tail = sb("q_tail", [P, QT * TAIL_Q])
        turn = sb("turn", [P, 2, T])
        probs = sb("probs", [P, 4, 512])
        probs_t = sb("probs_t", [P, 2, 512])
        sm = sb("sm", [P, NS, 8, 4])
        MX, MAX, NEG, DSINK, ESINK, SUM, Z, RZ = range(8)

        ident = cst[:, C_ID:C_ID + P]
        perm = cst[:, C_PERM:C_PERM + P]
        cos = cst[:, C_COS:C_COS + T]
        sin = cst[:, C_SIN:C_SIN + T]

        raw_landed = [sem(f"raw_landed{s}") for s in range(SLOTS)]
        w_hi_ready = sem("w_hi_ready")
        w_lo_ready = sem("w_lo_ready")
        w_used = sem("w_used")
        ident_in = sem("ident_in")
        consts_in = sem("consts_in")
        params_in = sem("params_in")
        x_in = sem("x_in")
        gates_in = sem("gates_in")
        zeroed = sem("zeroed")
        masks_ready = sem("masks_ready")
        params_turned = sem("params_turned")
        params_ready = sem("params_ready")
        soft_step = sem("soft_step")
        soft_exp = sem("soft_exp")
        x_turned = sem("x_turned")
        h_ready = sem("h_ready")
        h_hi_ready = sem("h_hi_ready")
        h_lo_dve = sem("h_lo_dve")
        h_lo_pool = sem("h_lo_pool")
        even_psum = sem("even_psum")
        silu_done = sem("silu_done")
        mult_done = sem("mult_done")
        a_hi_ready = sem("a_hi_ready")
        a_lo_ready = sem("a_lo_ready")
        z_ready = sem("z_ready")
        csum_step = sem("csum_step")
        c_psum = sem("c_psum")
        c_ready = sem("c_ready")
        shifted = sem("shifted")
        zc_ready = sem("zc_ready")
        sq_ready = sem("sq_ready")
        sumsq_step = sem("sumsq_step")
        dmu_psum = sem("dmu_psum")
        var_psum = sem("var_psum")
        dsq_ready = sem("dsq_ready")
        var_ready = sem("var_ready")
        log_ready = sem("log_ready")
        rstd_ready = sem("rstd_ready")
        t_ready = sem("t_ready")
        u_ready = sem("u_ready")
        xr_padded = sem("xr_padded")
        xr_ready = sem("xr_ready")
        kv_raw_ready = sem("kv_raw_ready")
        q_raw_ready = sem("q_raw_ready")
        gate_ready = sem("gate_ready")
        tap_ready = sem("tap_ready")
        conv_step = sem("conv_step")
        gates_psum = sem("gates_psum")
        sig_ready = sem("sig_ready")
        decay_ready = sem("decay_ready")
        a2_ready = sem("a2_ready")
        m_ready = sem("m_ready")
        root_ready = sem("root_ready")
        ix_ready = sem("ix_ready")
        gx_ready = sem("gx_ready")
        scan_ready = sem("scan_ready")
        gelu_ready = sem("gelu_ready")
        yr_ready = sem("yr_ready")
        ya_ready = sem("ya_ready")
        ysq_ready = sem("ysq_ready")
        ysq_step = sem("ysq_step")
        att_sq_ready = sem("att_sq_ready")
        rms_psum = sem("rms_psum")
        rms_log = sem("rms_log")
        rms_ready = sem("rms_ready")
        yn_ready = sem("yn_ready")
        y_hi_ready = sem("y_hi_ready")
        y_lo_ready = sem("y_lo_ready")
        z_rec_ready = sem("z_rec_ready")
        swap_psum = sem("swap_psum")
        rope_c = sem("rope_c")
        rope_s = sem("rope_s")
        rope_ready = sem("rope_ready")
        q_tail_ready = sem("q_tail_ready")
        v_psum = sem("v_psum")
        v_ready = sem("v_ready")
        scores_psum = sem("scores_psum")
        max_step = sem("max_step")
        sum_step = sem("sum_step")
        exp_ready = sem("exp_ready")
        probs_ready = sem("probs_ready")
        probs_psum = sem("probs_psum")
        pt_act = sem("pt_act")
        pt_dve = sem("pt_dve")
        pv_done = sem("pv_done")
        out_turned = sem("out_turned")
        out_act = sem("out_act")
        out_dve = sem("out_dve")
        stored = sem("stored")

        block = ctx.enter_context(nc.Block())

        def slot(n0):
            return n0 % SLOTS

        def center_tiles(norm):
            return CENTER_TILES[norm % 3]

        def centers(norm):
            return sum(center_tiles(n) for n in range(norm))

        def shifts(norm):
            return KD * norm - centers(norm)

        def ffn_unit0(f):
            return (f // 2) * LAYER_UNITS + (f % 2) * (LAYER_UNITS - FFN_UNITS)

        def in_unit0(layer):
            return layer * LAYER_UNITS + FFN_UNITS

        def out_unit0(layer):
            return in_unit0(layer) + N_IN

        TAPS = CONV - 1
        EVENS = 2 * DOWN_STEPS + IN_PAIRS + N_OUT

        def unit_tiles(n0, i=0):
            n = n0 + 4 * (i if isinstance(i, int) else 1)
            r = n % LAYER_UNITS
            if r >= FFN_UNITS + N_IN + N_OUT:
                r -= FFN_UNITS + N_IN + N_OUT
            if N_GU <= r < FFN_UNITS:
                k0, k1 = DOWN_K[(r - N_GU) % 4]
                return 2 * (k1 - k0)
            return KD

        def is_query_unit(n):
            r = n % LAYER_UNITS - FFN_UNITS
            return 6 <= r < 10

        def query_views(ring, s):
            natural = ring[0][:, s, 0:KD * P].rearrange("p (k g t d) -> p k g t d", k=HALF, g=2, t=2)
            ordered = [r[:, s, 0:KD * P].rearrange("p (k t g d) -> p k t g d", k=HALF, g=2, t=2) for r in ring[1:]]
            return [(natural[:, :, :, t, :], [o[:, :, t, :, :] for o in ordered]) for t in range(2)]

        def tokens(f_or_norm_last):
            return slice(N_META if f_or_norm_last else 0, T)

        @block.sync
        def _(sp):
            def load(n0, i, tiles, sources):
                if not (isinstance(i, int) and n0 + 4 * i < SLOTS):
                    sp.wait_ge(w_lo_ready, n0 + 4 * i - 3)
                s = slot(n0)
                for to, src in sources:
                    sp.dma_start(to(raw[:, s, 0:tiles * P]), src).then_inc(raw_landed[s], 32 // len(sources))

            def chunks(k):
                return lambda r: r.rearrange("p (k m) -> p k m", k=k)

            def load_gate_up(f, i):
                layer, name = f // 2, ("ffn1", "ffn2")[f % 2]
                for j in range(4):
                    src = w[name + ("_w_gate", "_w_up")[j % 2]][layer].rearrange("(k p) n -> p k n", p=P)
                    k0 = (j // 2) * HALF
                    load(ffn_unit0(f) + j, i, KD,
                         [(chunks(HALF), src[:, k0:k0 + HALF, bass.ds(i * (2 * P), 2 * P)])])

            def load_down(f, i):
                layer, name = f // 2, ("ffn1", "ffn2")[f % 2]
                src = w[name + "_w_down"][layer].rearrange("(k p) n -> p k n", p=P)
                for j, (k0, k1) in enumerate(DOWN_K):
                    load(ffn_unit0(f) + N_GU + j, i, 2 * (k1 - k0),
                         [(chunks(k1 - k0), src[:, k0:k1, bass.ds(i * (2 * P), 2 * P)])])

            def load_ffn(f):
                load_gate_up(f, 0)
                with sp.Fori(1, GU_STEPS, 1) as i:
                    load_gate_up(f, i)
                with sp.Fori(0, DOWN_STEPS, 1) as i:
                    load_down(f, i)

            def load_mixer(layer):
                w_in = w["w_in"][layer].rearrange("(k p) n -> p k n", p=P)
                w_out = w["w_out"][layer]
                starts = [0, 2 * P, 2 * REC + ATTN, None, None, REC, REC + 2 * P]
                order = [(0, 0), (1, 0), (0, 1), (1, 1)] + [(p, b) for p in range(2, IN_PAIRS) for b in range(2)]
                for j, (pair, b) in enumerate(order):
                    ks = slice(b * HALF, (b + 1) * HALF)
                    if starts[pair] is not None:
                        c0 = starts[pair]
                        sources = [(chunks(HALF), w_in[:, ks, c0:c0 + 2 * P])]
                    else:
                        sources = []
                        for g in range(N_KV):
                            c0 = 2 * REC + (4 * g + 2 * (pair - 3)) * HEAD
                            sources.append((lambda r, g=g: r.rearrange("p (k m) -> p k m", k=HALF)
                                            [:, :, g * P:(g + 1) * P], w_in[:, ks, c0:c0 + P]))
                    load(in_unit0(layer) + j, 0, KD, sources)
                for j in range(N_OUT):
                    cols = slice((j % 4) * 2 * P, (j % 4 + 1) * 2 * P)
                    if j < 4:
                        src = w_out[0:REC].rearrange("(k p) n -> p k n", p=P)
                        sources = [(chunks(RT), src[:, :, cols])]
                    else:
                        src = w_out[REC:REC + ATTN].rearrange("(g t d) n -> g d t n", g=N_KV, t=QT)
                        sources = [(lambda r, g=g: r[g * HEAD:(g + 1) * HEAD].rearrange(
                            "p (k m) -> p k m", k=QT), src[g][:, :, cols]) for g in range(N_KV)]
                    load(out_unit0(layer) + j, 0, KD, sources)

            sp.dma_start(ident, consts[:, C_ID:C_ID + P]).then_inc(ident_in, 16)
            first = P - N_META
            sp.dma_start(x_stage[0:N_META, 0, :], w["meta_tokens"]).then_inc(x_in, 16)
            sp.dma_start(x_stage[N_META:P, 0, :], w["x"][0, 0:first]).then_inc(x_in, 16)
            sp.dma_start(x_stage[:, 1, :], w["x"][0, first:first + P]).then_inc(x_in, 16)
            sp.dma_start(x_stage[0:TAIL_Q, 2, :], w["x"][0, first + P:SEQ]).then_inc(x_in, 16)
            for layer in range(DEPTH):
                load_ffn(2 * layer)
                load_mixer(layer)
                load_ffn(2 * layer + 1)

            for b in range(2):
                for a in range(2):
                    sp.wait_ge((out_act, out_dve)[a], b + 1)
                    sp.dma_start(out[0, a * P:(a + 1) * P, b * 512:(b + 1) * 512],
                                 out_stage[:, 2 * a + b, :]).then_inc(stored, 16)
            sp.wait_ge(stored, 64)

        @block.gpsimd
        def _(pool):
            nc.gpsimd.memset(gate_w[:], 0.0).then_inc(zeroed, 1)
            nc.gpsimd.memset(ones_c[:, 0, :], 1.0 / (6 * P)).then_inc(zeroed, 1)
            nc.gpsimd.memset(ones_c[:, 1, :], 1.0 / (4 * P)).then_inc(zeroed, 1)
            nc.gpsimd.memset(ones_d[:], 1.0 / D_MODEL).then_inc(zeroed, 1)
            nc.gpsimd.memset(ones_r[:], 1.0 / REC).then_inc(zeroed, 1)
            nc.gpsimd.memset(eps[:, 0:1], LN_EPS / ALPHA ** 2).then_inc(zeroed, 1)
            nc.gpsimd.memset(eps[:, 1:2], RMS_EPS).then_inc(zeroed, 1)
            nc.gpsimd.memset(eps[:, 2:4], 1.0).then_inc(zeroed, 1)
            nc.gpsimd.memset(k_rot[:], 0.0).then_inc(zeroed, 1)

            def sum_squares(norm, tok):
                for d in range(1, 6):
                    pool.wait_ge(sq_ready, KD * norm + d + 1)
                    if d > 1:
                        pool.wait_ge(sumsq_step, 5 * norm + d - 1)
                    first = sq[:, 0, tok] if d == 1 else sumsq[:, tok]
                    nc.gpsimd.tensor_tensor(sumsq[:, tok], first, sq[:, d, tok], ALU.add).then_inc(sumsq_step, 1)

            def sum_group(layer, tok):
                for r in range(1, RT):
                    pool.wait_ge(ysq_ready, RT * layer + r + 1)
                    if r > 1:
                        pool.wait_ge(ysq_step, 3 * layer + r - 1)
                    first = th[:, 0, tok] if r == 1 else sumsq[:, tok]
                    nc.gpsimd.tensor_tensor(sumsq[:, tok], first, th[:, r, tok], ALU.add).then_inc(ysq_step, 1)

            def low_parts(version, tok):
                for k in range(1, KD, 2):
                    pool.wait_ge(h_ready, KD * version + k + 1)
                    pool.wait_ge(h_hi_ready, KD * version + k + 1)
                    nc.gpsimd.tensor_tensor(h_lo[:, k, tok], h[:, k, tok], h_hi[:, k, tok].bitcast(F32),
                                            ALU.subtract).then_inc(h_lo_pool, 1)

            def input_gate(layer, r):
                n = RT * layer + r
                pool.wait_ge(sig_ready, 2 * n + 2)
                pool.wait_ge(conv_step, TAPS * (n + 1))
                nc.gpsimd.tensor_tensor(ig[:, r, :], ig[:, r, :], xc[:, r, :], ALU.mult).then_inc(ix_ready, 1)

            def rope_cos(layer, p):
                if p == 0:
                    pool.wait_ge(swap_psum, 5 * layer + 1)
                    nc.gpsimd.tensor_tensor(k_raw, k_raw, cos, ALU.mult).then_inc(rope_c, 1)
                else:
                    pool.wait_ge(q_raw_ready, 2 * layer + (p + 1) // 2)
                    nc.gpsimd.tensor_tensor(q_rot[:, p - 1, :], q_raw[:, p - 1, :], cos,
                                            ALU.mult).then_inc(rope_c, 1)

            def mixer(layer, tok):
                input_gate(layer, 0)
                input_gate(layer, 1)
                rope_cos(layer, 0)
                input_gate(layer, 2)
                input_gate(layer, 3)
                rope_cos(layer, 1)
                rope_cos(layer, 2)
                for r in range(RT):
                    pool.wait_ge(decay_ready, RT * layer + r + 1)
                    nc.gpsimd.tensor_tensor(yr[:, r, :], ra[:, r, :], ra[:, r, :], ALU.mult).then_inc(a2_ready, 1)
                rope_cos(layer, 3)
                rope_cos(layer, 4)
                for r in range(RT):
                    pool.wait_ge(root_ready, RT * layer + r + 1)
                    pool.wait_ge(ix_ready, RT * layer + r + 1)
                    nc.gpsimd.tensor_tensor(ig[:, r, :], ig[:, r, :], th[:, r, :], ALU.mult).then_inc(gx_ready, 1)
                for r in range(RT):
                    pool.wait_ge(scan_ready, RT * layer + r + 1)
                    pool.wait_ge(gelu_ready, RT * layer + r + 1)
                    nc.gpsimd.tensor_tensor(yr[:, r, :], yr[:, r, :], gl[:, r, :], ALU.mult).then_inc(yr_ready, 1)
                sum_group(layer, tok)

            low_parts(0, slice(0, T))
            for layer in range(DEPTH):
                last = layer == DEPTH - 1
                sum_squares(3 * layer, tokens(False))
                low_parts(3 * layer + 1, tokens(False))
                mixer(layer, tokens(last))
                sum_squares(3 * layer + 1, tokens(last))
                low_parts(3 * layer + 2, tokens(last))
                sum_squares(3 * layer + 2, tokens(last))
                if not last:
                    low_parts(3 * layer + 3, tokens(False))

        @block.scalar
        def _(eng):
            act_fn = nc.scalar.activation

            def copy(to, src):
                return act_fn(to, src, ACT.Copy)

            def split(n0, i=0):
                if isinstance(i, int) and n0 + 4 * i >= ALL_UNITS:
                    return
                size = unit_tiles(n0, i) * P
                s = slot(n0)
                eng.wait_ge(raw_landed[s], (n0 // SLOTS + i + 1) * 32)
                if not (isinstance(i, int) and n0 + 4 * i < SLOTS):
                    eng.wait_ge(w_used, n0 + 4 * i - 3)
                if isinstance(i, int) and is_query_unit(n0 + 4 * i):
                    for src, (to,) in query_views((raw, w_hi), s):
                        last = copy(to, src)
                    last.then_inc(w_hi_ready, 1)
                else:
                    copy(w_hi[:, s, 0:size], raw[:, s, 0:size]).then_inc(w_hi_ready, 1)

            def gate_up(f, i, tok):
                u0, n = ffn_unit0(f), GU_STEPS * f + i
                split(u0 + 4, i)
                split(u0 + 5, i)
                eng.wait_ge(w_used, u0 + 4 * i + 3)
                act_fn(sg[:, :, tok], banks[:, 0:2, tok], ACT.Silu).then_inc(silu_done, 1)
                split(u0 + 6, i)
                split(u0 + 7, i)
                eng.wait_ge(mult_done, n + 1)
                copy(a_hi[:, bass.ds(2 * i, 2), tok], act[:, :, tok]).then_inc(a_hi_ready, 1)

            def norm_center(norm, tok):
                eng.wait_ge(c_psum, norm + 1)
                copy(center[:, tok], bank[6][:, tok]).then_inc(c_ready, 1)

            def norm_square(norm, d, tok):
                eng.wait_ge(zc_ready, KD * norm + d + 1)
                act_fn(sq[:, d, tok], h[:, d, tok], ACT.Square).then_inc(sq_ready, 1)

            def load_log_exp():
                nc.scalar.preload_act_table_set("natural_log_exp_and_others")

            def rsqrt_of(src, bias, log_done, done, count, tok):
                act_fn(var[:, tok], src, ACT.Ln, bias=bias).then_inc(log_done, 1)
                eng.wait_ge(log_done, count)
                act_fn(rstd[:, tok], var[:, tok], ACT.Exp, scale=-0.5).then_inc(done, 1)

            def norm_tail(norm, tok, last_split):
                layer, which = norm // 3, norm % 3
                norm_square(norm, KD - 1, tok)
                eng.wait_ge(dmu_psum, norm + 1)
                act_fn(dsq[:, tok], bank[6][:, tok], ACT.Square).then_inc(dsq_ready, 1)
                eng.wait_ge(var_ready, norm + 1)
                rsqrt_of(var[:, tok], eps[:, 0:1], log_ready, rstd_ready, norm + 1, tok)
                if last_split is None:
                    return
                for k in range(KD):
                    g = (2 * which) * DEPTH * KD + layer * KD + k
                    b = g + DEPTH * KD
                    eng.wait_ge(u_ready, KD * norm + k + 1)
                    act_fn(h_hi[:, k, tok], sq[:, k, tok], ACT.Identity, scale=par[:, g:g + 1],
                           bias=par[:, b:b + 1]).then_inc(h_hi_ready, 1)
                    if k == 1:
                        split(last_split)

            def ffn(f, norm, tok, parts):
                gate_up(f, 0, tok)
                if f == 0:
                    setup()
                nc.scalar.preload_act_table(ACT.Silu)
                with eng.Fori(1, GU_STEPS - 1, 1) as i:
                    gate_up(f, i, tok)
                gate_up(f, GU_STEPS - 1, tok)
                d0 = ffn_unit0(f) + N_GU
                with eng.Fori(0, DOWN_STEPS - 1, 1) as i:
                    for j in range(4):
                        split(d0 + 4 + j, i)
                n = d0 + 4 * (DOWN_STEPS - 1)
                norm_center(norm, tok)
                split(n + 4)
                for d in range(3):
                    norm_square(norm, d, tok)
                split(n + 5)
                for d in range(3, 6):
                    norm_square(norm, d, tok)
                load_log_exp()
                split(n + 6)
                norm_square(norm, 6, tok)
                norm_tail(norm, tok, n + 7 if parts else None)

            def softmax(layer, s):
                g, t0, heads, q0, keys = STEPS[s]
                eng.wait_ge(max_step, 4 * (NS * layer + s) + 4)
                if s >= 4:
                    eng.wait_ge(probs_psum, NS * layer + s - 3)
                act_fn(sm[:, s, ESINK, 0:heads], sm[:, s, DSINK, 0:heads], ACT.Exp)
                for i in range(heads):
                    last = act_fn(probs[:, s % 4, i * keys:(i + 1) * keys],
                                  bank[SCORE_BANKS[s % 2]][:, i * keys:(i + 1) * keys], ACT.Exp,
                                  bias=sm[:, s, NEG, i:i + 1], scale=HEAD ** -0.5,
                                  accum_out=sm[:, s, SUM, i:i + 1])
                last.then_inc(exp_ready, 1)

            def probs_copy(layer, s):
                eng.wait_ge(probs_psum, NS * layer + s + 1)
                if s == TAIL_STEP:
                    src = bank[TURN_BANKS[s % 2]]
                    copy(probs_t[:, s % 2, 0:2 * P], src[:, 0:2 * P])
                    copy(probs_t[0:TAIL_Q, s % 2, 2 * P:3 * P],
                         src[0:TAIL_Q, 2 * P:3 * P]).then_inc(pt_act, 1)
                else:
                    copy(probs_t[:, s % 2, :], bank[TURN_BANKS[s % 2]][:, :]).then_inc(pt_act, 1)

            def attended(layer, steps, src, q0, n):
                eng.wait_ge(pv_done, NS * layer + steps)
                eng.wait_ge(scan_ready, RT * (layer + 1))
                view = src[:, 0:QT * n].rearrange("p (t q) -> p t q", t=QT)
                act_fn(ig[:, :, q0:q0 + n], view, ACT.Square).then_inc(att_sq_ready, 1)
                copy(ya[:, :, q0:q0 + n], view).then_inc(ya_ready, 1)

            def recurrent_squares(layer, tok):
                for r in range(RT):
                    eng.wait_ge(yr_ready, RT * layer + r + 1)
                    act_fn(th[:, r, tok], yr[:, r, tok], ACT.Square).then_inc(ysq_ready, 1)

            def group_root(layer, which, src, tok):
                eng.wait_ge(rms_psum, 2 * layer + which + 1)
                rsqrt_of(src[:, tok], eps[:, 1:2], rms_log, rms_ready, 2 * layer + which + 1, tok)

            def group_high(layer, which, src, tok):
                for r in range(RT):
                    eng.wait_ge(yn_ready, 8 * layer + 4 * which + r + 1)
                    copy(h_hi[:, 4 * which + r, tok], src[:, r, tok]).then_inc(y_hi_ready, 1)

            def sigmoids(layer, r):
                eng.wait_ge(gates_psum, RT * layer + r + 1)
                for b, to, pc in ((6, ra, PC_GA), (7, ig, PC_GX)):
                    c = pc + RT * layer + r
                    act_fn(to[:, r, :], bank[b][:, 0:T], ACT.Sigmoid, bias=par[:, c:c + 1]).then_inc(sig_ready, 1)

            def decays(layer, r):
                c = RT * layer + r
                eng.wait_ge(sig_ready, 2 * c + 2)
                act_fn(th[:, r, :], ra[:, r, :], ACT.Tanh, scale=decay[:, c:c + 1])
                act_fn(ra[:, r, :], ra[:, r, :], ACT.Exp, scale=decay[:, c:c + 1]).then_inc(decay_ready, 1)

            def recurrent_tile(layer, r):
                wc, cb = PC_CONVW + (layer * CONV + CONV - 1) * RT + r, PC_CONVB + layer * RT + r
                copy(xr[:, r, CONV - 1:], bank[r][:, 0:T]).then_inc(xr_ready, 1)
                act_fn(xc[:, r, :], bank[r][:, 0:T], ACT.Identity, scale=par[:, wc:wc + 1],
                       bias=par[:, cb:cb + 1]).then_inc(tap_ready, 1)

            def roots(layer):
                for r in range(RT):
                    eng.wait_ge(m_ready, RT * layer + r + 1)
                    act_fn(th[:, r, :], th[:, r, :], ACT.Sqrt, scale=-1.0).then_inc(root_ready, 1)

            def gelus(layer):
                eng.wait_ge(gate_ready, RT * layer + RT)
                for r in range(RT):
                    act_fn(gl[:, r, :], gl[:, r, :], ACT.Gelu_apprx_tanh).then_inc(gelu_ready, 1)

            def mixer(layer, norm, tok):
                u0, o0 = in_unit0(layer), out_unit0(layer)

                def tile(pair, b):
                    if b == 0:
                        eng.wait_ge(even_psum, EVENS * layer + DOWN_STEPS + pair + 1)
                    else:
                        eng.wait_ge(w_used, u0 + 2 * pair + 2)

                split(u0 + 4)
                split(u0 + 5)
                eng.wait_ge(w_used, u0 + 4)
                for r in range(RT):
                    recurrent_tile(layer, r)
                split(u0 + 6)
                sigmoids(layer, 0)
                split(u0 + 7)
                split(u0 + 8)
                tile(2, 1)
                copy(kv_raw[:, :, :], banks[:, 4:6, 0:T]).then_inc(kv_raw_ready, 1)
                sigmoids(layer, 1)
                split(u0 + 9)
                sigmoids(layer, 2)
                split(u0 + 10)
                tile(3, 1)
                copy(q_raw[:, 0:2, :], banks[:, 0:2, 0:T]).then_inc(q_raw_ready, 1)
                sigmoids(layer, 3)
                split(u0 + 11)
                for r in range(RT):
                    decays(layer, r)
                split(u0 + 12)
                tile(4, 1)
                copy(q_raw[:, 2:4, :], banks[:, 2:4, 0:T]).then_inc(q_raw_ready, 1)
                split(u0 + 13)
                roots(layer)
                split(o0)
                load_log_exp()
                tile(5, 0)
                copy(gl[:, 0, :], bank[0][:, 0:T]).then_inc(gate_ready, 1)
                tile(5, 1)
                copy(gl[:, 1, :], bank[1][:, 0:T]).then_inc(gate_ready, 1)
                split(o0 + 1)
                softmax(layer, 0)
                softmax(layer, 1)
                tile(6, 0)
                copy(gl[:, 2, :], bank[2][:, 0:T]).then_inc(gate_ready, 1)
                tile(6, 1)
                copy(gl[:, 3, :], bank[0][:, 0:T]).then_inc(gate_ready, 1)
                probs_copy(layer, 0)
                gelus(layer)
                load_log_exp()
                softmax(layer, 2)
                split(o0 + 2)
                softmax(layer, 3)
                attended(layer, 2, bank[1], 0, P)
                probs_copy(layer, 2)
                softmax(layer, 4)
                attended(layer, 3, bank[0], 2 * P, TAIL_Q)
                recurrent_squares(layer, tok)
                softmax(layer, 5)
                probs_copy(layer, 4)
                group_root(layer, 0, bank[4], tok)
                softmax(layer, 6)
                group_high(layer, 0, yr, tok)
                split(o0 + 3)
                probs_copy(layer, 6)
                split(o0 + 4)
                attended(layer, 7, bank[2], P, P)
                split(o0 + 5)
                group_root(layer, 1, bank[3], tok)
                split(o0 + 6)
                group_high(layer, 1, ya, tok)
                for j in range(7, 10):
                    split(o0 + j)
                norm_center(norm, tok)
                norm_square(norm, 0, tok)
                norm_square(norm, 1, tok)
                split(o0 + 10)
                for d in range(2, 7):
                    norm_square(norm, d, tok)
                norm_tail(norm, tok, o0 + 11)

            def high_part(k):
                eng.wait_ge(h_ready, k + 1)
                copy(h_hi[:, k, :], h[:, k, :]).then_inc(h_hi_ready, 1)

            def setup():
                eng.wait_ge(ident_in, 16)
                copy(ident16[:], ident).then_inc(masks_ready, 1)
                eng.wait_ge(consts_in, 16)
                copy(masks[:], cst[:, C_MA:C_ALL]).then_inc(masks_ready, 1)
                eng.wait_ge(soft_step, 1)
                act_fn(soft[:, 1, :], soft[:, 0, :], ACT.Exp, scale=-1.0).then_inc(soft_exp, 1)

            for j in range(3):
                split(j)
            for k in range(KD):
                high_part(k)
                if k == 1:
                    split(3)
            eng.dma_start(cst[:, P:C_ALL], consts[:, P:C_ALL]).then_inc(consts_in, 16)
            row = 0
            for name in ("ln1_g", "ln1_b", "ln2_g", "ln2_b", "ln3_g", "ln3_b"):
                n = DEPTH * KD
                eng.dma_start(par_rows[row:row + n, 0, :],
                              w[name].rearrange("l (k p) -> (l k) p", p=P)).then_inc(params_in, 16)
                row += n
            n = DEPTH * CONV * RT
            eng.dma_start(par_rows[0:n, 1, :],
                          w["conv_w"].rearrange("l w (k p) -> (l w k) p", p=P)).then_inc(params_in, 16)
            row = n
            for name in ("conv_b", "gate_a_b", "gate_x_b", "lru_lambda", "norm_rec_g"):
                eng.dma_start(par_rows[row:row + DEPTH * RT, 1, :],
                              w[name].rearrange("l (k p) -> (l k) p", p=P)).then_inc(params_in, 16)
                row += DEPTH * RT
            for layer in range(DEPTH):
                for g in range(N_KV):
                    src = w["norm_attn_g"][layer].rearrange("(g t d) -> g t d", g=N_KV, t=QT)[g]
                    eng.dma_start(par_rows[row:row + QT, 1, g * HEAD:(g + 1) * HEAD], src).then_inc(params_in, 16)
                row += QT
            eng.dma_start(sink[:], w["attn_sinks"].partition_broadcast(P)).then_inc(params_in, 16)
            eng.wait_ge(zeroed, 1)
            for layer in range(DEPTH):
                for x, name in enumerate(("gate_a_w", "gate_x_w")):
                    src = w[name][layer].rearrange("(r b) i j -> b i r j", b=2)
                    for b in range(2):
                        at = slice(b * HEAD, (b + 1) * HEAD)
                        eng.dma_start(gate_w[at, layer, x, :, at], src[b]).then_inc(gates_in, 16)

            for layer in range(DEPTH):
                last = layer == DEPTH - 1
                ffn(2 * layer, 3 * layer, tokens(False), True)
                mixer(layer, 3 * layer + 1, tokens(last))
                ffn(2 * layer + 1, 3 * layer + 2, tokens(last), not last)
            for b in range(2):
                eng.wait_ge(out_turned, 2 * b + 1)
                copy(out_stage[:, b, :], bank[b][:, :]).then_inc(out_act, 1)

        @block.vector
        def _(eng):
            tt = nc.vector.tensor_tensor
            ts = nc.vector.tensor_scalar
            stt = nc.vector.scalar_tensor_tensor

            def split(n0, i=0):
                if isinstance(i, int) and n0 + 4 * i >= ALL_UNITS:
                    return
                size = unit_tiles(n0, i) * P
                s = slot(n0)
                eng.wait_ge(w_hi_ready, n0 + 4 * i + 1)
                if isinstance(i, int) and is_query_unit(n0 + 4 * i):
                    for src, (hi, lo) in query_views((raw, w_hi, w_lo), s):
                        last = tt(lo, src, hi.bitcast(F32), ALU.subtract)
                    last.then_inc(w_lo_ready, 1)
                else:
                    tt(w_lo[:, s, 0:size], raw[:, s, 0:size],
                       w_hi[:, s, 0:size].bitcast(F32), ALU.subtract).then_inc(w_lo_ready, 1)

            def gate_up(f, i, tok):
                u0, n = ffn_unit0(f), GU_STEPS * f + i
                split(u0 + 4, i)
                split(u0 + 5, i)
                split(u0 + 6, i)
                eng.wait_ge(silu_done, n + 1)
                eng.wait_ge(w_used, u0 + 4 * i + 4)
                if not (isinstance(i, int) and n == 0):
                    eng.wait_ge(a_lo_ready, n)
                tt(act[:, :, tok], sg[:, :, tok], banks[:, 2:4, tok], ALU.mult).then_inc(mult_done, 1)
                split(u0 + 7, i)
                eng.wait_ge(a_hi_ready, n + 1)
                at = bass.ds(2 * i, 2)
                tt(a_lo[:, at, tok], act[:, :, tok], a_hi[:, at, tok].bitcast(F32),
                   ALU.subtract).then_inc(a_lo_ready, 1)

            def residual(i, d, src, scale, tok, done):
                at = bass.ds(2 * i + d, 1)
                stt(out=h[:, at, tok], in0=src[:, tok].unsqueeze(1), scalar=scale, in1=h[:, at, tok],
                    op0=ALU.mult, op1=ALU.add).then_inc(done, 1)

            def center_sum(norm, i, d, tok):
                at = bass.ds(2 * i + d, 1)
                eng.wait_ge(z_ready, centers(norm) + 2 * i + d + 1)
                to = csum[:, tok].unsqueeze(1)
                if isinstance(i, int) and i == 0 and d == 0:
                    nc.vector.tensor_copy(to, h[:, at, tok]).then_inc(csum_step, 1)
                else:
                    eng.wait_ge(csum_step, centers(norm) + 2 * i + d)
                    tt(to, to, h[:, at, tok], ALU.add).then_inc(csum_step, 1)

            def centered(norm, d, tok):
                eng.wait_ge(c_ready, norm + 1)
                tt(h[:, d, tok], h[:, d, tok], center[:, tok], ALU.subtract).then_inc(
                    zc_ready if d < center_tiles(norm) else shifted, 1)

            def low_part(version, k, tok):
                if k % 2 == 0:
                    eng.wait_ge(h_ready, KD * version + k + 1)
                    eng.wait_ge(h_hi_ready, KD * version + k + 1)
                    tt(h_lo[:, k, tok], h[:, k, tok], h_hi[:, k, tok].bitcast(F32),
                       ALU.subtract).then_inc(h_lo_dve, 1)

            def norm_tail(norm, tok, last_split):
                layer, which = norm // 3, norm % 3

                def subtract(k):
                    tt(h[:, k, tok], h[:, k, tok], bank[6][:, tok], ALU.subtract).then_inc(t_ready, 1)

                def scale(k):
                    eng.wait_ge(t_ready, KD * norm + k + 1)
                    tt(sq[:, k, tok], h[:, k, tok], rstd[:, tok], ALU.mult).then_inc(u_ready, 1)

                def affine(k):
                    g = (2 * which) * DEPTH * KD + layer * KD + k
                    b = g + DEPTH * KD
                    eng.wait_ge(u_ready, KD * norm + k + 1)
                    ts(h[:, k, tok], sq[:, k, tok], par[:, g:g + 1], par[:, b:b + 1],
                       ALU.mult, ALU.add).then_inc(h_ready, 1)

                eng.wait_ge(dsq_ready, norm + 1)
                subtract(0)
                eng.wait_ge(var_psum, norm + 1)
                tt(var[:, tok], bank[7][:, tok], dsq[:, tok], ALU.subtract).then_inc(var_ready, 1)
                subtract(1)
                subtract(2)
                eng.wait_ge(rstd_ready, norm + 1)
                for k in range(KD + 2):
                    if k < KD:
                        scale(k)
                    if k + 3 < KD:
                        subtract(k + 3)
                    if 1 <= k <= KD:
                        affine(k - 1)
                    if last_split is not None:
                        if k >= 2:
                            low_part(norm + 1, k - 2, tok)
                        if k == 4:
                            split(last_split)

            def ffn(f, norm, tok, parts):
                gate_up(f, 0, tok)
                if f == 0:
                    setup()
                with eng.Fori(1, GU_STEPS - 1, 1) as i:
                    gate_up(f, i, tok)
                gate_up(f, GU_STEPS - 1, tok)
                d0 = ffn_unit0(f) + N_GU
                evens = EVENS * (f // 2) + (f % 2) * (EVENS - DOWN_STEPS)

                def down(i):
                    for j in range(3):
                        split(d0 + 4 + j, i)
                    for b in range(2):
                        if b == 0:
                            eng.wait_ge(even_psum, evens + i + 1)
                        else:
                            eng.wait_ge(w_used, d0 + 4 * i + 4)
                        residual(i, b, bank[4 + b], 0.5 / ALPHA, tok, z_ready)
                        center_sum(norm, i, b, tok)
                    split(d0 + 7, i)

                down(0)
                with eng.Fori(1, DOWN_STEPS - 1, 1) as i:
                    down(i)
                n = d0 + 4 * (DOWN_STEPS - 1)
                for d in (6, 7, 0, 1):
                    centered(norm, d, tok)
                split(n + 4)
                for d in range(2, 6):
                    centered(norm, d, tok)
                split(n + 5)
                split(n + 6)
                eng.wait_ge(shifted, shifts(norm) + 2)
                for b in range(2):
                    if b == 0:
                        eng.wait_ge(even_psum, evens + DOWN_STEPS)
                    else:
                        eng.wait_ge(w_used, n + 4)
                    residual(0, 6 + b, bank[4 + b], 0.5 / ALPHA, tok, zc_ready)
                norm_tail(norm, tok, n + 7 if parts else None)

            def conv(layer, r):
                eng.wait_ge(xr_ready, RT * layer + r + 1)
                eng.wait_ge(xr_padded, layer + 1)
                eng.wait_ge(tap_ready, RT * layer + r + 1)
                base = TAPS * (RT * layer + r)
                for k in range(TAPS):
                    c = PC_CONVW + (layer * CONV + k) * RT + r
                    if k:
                        eng.wait_ge(conv_step, base + k)
                    stt(out=xc[:, r, :], in0=xr[:, r, k:k + T], scalar=par[:, c:c + 1],
                        in1=xc[:, r, :], op0=ALU.mult, op1=ALU.add).then_inc(conv_step, 1)

            def rope(layer, p):
                mid = k_raw if p == 0 else q_rot[:, p - 1, :]
                n = 5 * layer + p
                eng.wait_ge(swap_psum, n + 1)
                if p >= 2:
                    eng.wait_ge(rope_ready, 6 * layer + p)
                elif layer:
                    eng.wait_ge(rope_ready, 6 * layer)
                tt(turn[:, p % 2, :], bank[4 + p % 2][:, 0:T], sin, ALU.mult).then_inc(rope_s, 1)
                eng.wait_ge(rope_s, n + 1)
                eng.wait_ge(rope_c, n + 1)
                if p == 0:
                    for g in range(N_KV):
                        at = slice(g * HEAD, (g + 1) * HEAD)
                        tt(k_rot[at, g, :], kv_raw[at, 0, :], turn[at, 0, :], ALU.add).then_inc(rope_ready, 1)
                else:
                    tt(mid, mid, turn[:, p % 2, :], ALU.add).then_inc(rope_ready, 1)

            def values(layer):
                eng.wait_ge(v_psum, layer + 1)
                nc.vector.tensor_copy(v_tok[:, 0:2, :], bank[7][:, 0:2 * P].rearrange(
                    "p (b c) -> p b c", b=2)).then_inc(v_ready, 1)
                nc.vector.tensor_copy(v_tok[0:TAIL_Q, 2, :], bank[7][0:TAIL_Q, 2 * P:3 * P]).then_inc(v_ready, 1)

            def decay_root(layer, r):
                n = RT * layer + r
                eng.wait_ge(a2_ready, n + 1)
                stt(out=th[:, r, :], in0=yr[:, r, :], scalar=1.0, in1=th[:, r, :],
                    op0=ALU.add, op1=ALU.mult).then_inc(m_ready, 1)

            def scan(layer, r):
                n = RT * layer + r
                eng.wait_ge(gx_ready, n + 1)
                nc.vector.tensor_tensor_scan(yr[:, r, :], ra[:, r, :], ig[:, r, :], 0.0,
                                             ALU.mult, ALU.add).then_inc(scan_ready, 1)

            def maxima(layer, s):
                g, t0, heads, q0, keys = STEPS[s]
                n = 4 * (NS * layer + s)
                eng.wait_ge(scores_psum, NS * layer + s + 1)
                v = sm[:, s, :, 0:heads]
                if g is None:
                    own = sink_tail[:, layer:layer + 1]
                else:
                    own = sink[:, layer, 4 * g + t0:4 * g + t0 + heads]
                nc.vector.tensor_reduce(v[:, MX], bank[SCORE_BANKS[s % 2]][:, 0:heads * keys].rearrange(
                    "p (h k) -> p h k", h=heads), AX.X, ALU.max).then_inc(max_step, 1)
                eng.wait_ge(max_step, n + 1)
                stt(out=v[:, MAX], in0=v[:, MX], scalar=HEAD ** -0.5, in1=own,
                    op0=ALU.mult, op1=ALU.max).then_inc(max_step, 1)
                eng.wait_ge(max_step, n + 2)
                ts(v[:, NEG], v[:, MAX], -1.0, None, ALU.mult).then_inc(max_step, 1)
                tt(v[:, DSINK], own, v[:, MAX], ALU.subtract).then_inc(max_step, 1)

            def normalize(layer, s):
                g, t0, heads, q0, keys = STEPS[s]
                n = 2 * (NS * layer + s)
                v = sm[:, s, :, 0:heads]
                eng.wait_ge(exp_ready, NS * layer + s + 1)
                tt(v[:, Z], v[:, SUM], v[:, ESINK], ALU.add).then_inc(sum_step, 1)
                eng.wait_ge(sum_step, n + 1)
                nc.vector.reciprocal(v[:, RZ], v[:, Z]).then_inc(sum_step, 1)
                eng.wait_ge(sum_step, n + 2)
                for i in range(heads):
                    at = probs[:, s % 4, i * keys:(i + 1) * keys]
                    last = ts(at, at, sm[:, s, RZ, i:i + 1], None, ALU.mult)
                last.then_inc(probs_ready, 1)

            def probs_copy(layer, s):
                eng.wait_ge(probs_psum, NS * layer + s + 1)
                nc.vector.tensor_copy(probs_t[:, s % 2, :], bank[TURN_BANKS[s % 2]][:, :]).then_inc(pt_dve, 1)

            def group_norm(layer, which, src, pc, tok):
                eng.wait_ge(rms_ready, 2 * layer + which + 1)
                n = 8 * layer + 4 * which
                for r in range(RT + 1):
                    if r < RT:
                        c = pc + RT * layer + r
                        stt(out=src[:, r, tok], in0=src[:, r, tok], scalar=par[:, c:c + 1],
                            in1=rstd[:, tok], op0=ALU.mult, op1=ALU.mult).then_inc(yn_ready, 1)
                    if r >= 1:
                        eng.wait_ge(y_hi_ready, n + r)
                        tt(h_lo[:, 4 * which + r - 1, tok], src[:, r - 1, tok],
                           h_hi[:, 4 * which + r - 1, tok].bitcast(F32), ALU.subtract).then_inc(y_lo_ready, 1)

            def mixer(layer, norm, tok):
                u0, o0 = in_unit0(layer), out_unit0(layer)
                evens = EVENS * layer + DOWN_STEPS + IN_PAIRS

                def out_tile(which, j, b):
                    if b == 0:
                        eng.wait_ge(even_psum, evens + 4 * which + j + 1)
                    else:
                        eng.wait_ge(w_used, o0 + 4 * which + j + 1)

                def recurrent_out(j):
                    for b in range(2):
                        out_tile(0, j, b)
                        d = 2 * j + b
                        residual(0, d, bank[OUT_BANKS[d % 3]], 1.0 / ALPHA, tok, z_rec_ready)

                nc.vector.memset(xr[:, :, 0:CONV - 1], 0.0).then_inc(xr_padded, 1)
                split(u0 + 4)
                split(u0 + 5)
                conv(layer, 0)
                split(u0 + 6)
                conv(layer, 1)
                conv(layer, 2)
                split(u0 + 7)
                conv(layer, 3)
                split(u0 + 8)
                rope(layer, 0)
                split(u0 + 9)
                rope(layer, 1)
                rope(layer, 2)
                split(u0 + 10)
                values(layer)
                split(u0 + 11)
                for r in range(RT):
                    decay_root(layer, r)
                split(u0 + 12)
                rope(layer, 3)
                rope(layer, 4)
                eng.wait_ge(rope_ready, 6 * layer + 6)
                nc.vector.tensor_copy(q_tail[:].rearrange("p (t q) -> p t q", t=QT),
                                      q_rot[:, :, 2 * P:T]).then_inc(q_tail_ready, 1)
                split(u0 + 13)
                split(o0)
                maxima(layer, 0)
                scan(layer, 0)
                maxima(layer, 1)
                scan(layer, 1)
                split(o0 + 1)
                normalize(layer, 0)
                scan(layer, 2)
                normalize(layer, 1)
                scan(layer, 3)
                maxima(layer, 2)
                probs_copy(layer, 1)
                maxima(layer, 3)
                normalize(layer, 2)
                split(o0 + 2)
                normalize(layer, 3)
                maxima(layer, 4)
                probs_copy(layer, 3)
                maxima(layer, 5)
                normalize(layer, 4)
                maxima(layer, 6)
                normalize(layer, 5)
                group_norm(layer, 0, yr, PC_GREC, tok)
                probs_copy(layer, 5)
                normalize(layer, 6)
                split(o0 + 3)
                recurrent_out(0)
                split(o0 + 4)
                recurrent_out(1)
                split(o0 + 5)
                recurrent_out(2)
                split(o0 + 6)
                group_norm(layer, 1, ya, PC_GATT, tok)
                recurrent_out(3)
                split(o0 + 7)
                m = center_tiles(norm)
                for j in range(4):
                    if j < 3:
                        split(o0 + 8 + j)
                    eng.wait_ge(z_rec_ready, KD * layer + 2 * j + 2)
                    if j >= 2:
                        eng.wait_ge(shifted, shifts(norm) + 2 * j - 2)
                    for b in range(2):
                        out_tile(1, j, b)
                        d = 2 * j + b
                        residual(0, d, bank[ATT_BANKS[d % 4]], 1.0 / ALPHA, tok, z_ready if d < m else zc_ready)
                        if d < m:
                            center_sum(norm, 0, d, tok)
                    if j == 1:
                        for d in range(4, 8):
                            centered(norm, d, tok)
                        for d in range(0, 4):
                            centered(norm, d, tok)
                norm_tail(norm, tok, o0 + 11)

            def setup():
                eng.wait_ge(params_turned, 1)
                nc.vector.tensor_copy(par[:, 0:LN_COLS], bank[4][:, 0:LN_COLS]).then_inc(params_ready, 1)
                eng.wait_ge(params_turned, 2)
                nc.vector.tensor_copy(par[:, LN_COLS:PC_ALL], bank[5][:, 0:ROWS_B]).then_inc(params_ready, 1)

                eng.wait_ge(params_ready, 2)
                lam = par[:, PC_LAM:PC_LAM + DEPTH * RT]
                steps = [0]

                def chain(instruction):
                    steps[0] += 1
                    instruction.then_inc(soft_step, 1)
                    eng.wait_ge(soft_step, steps[0])

                chain(stt(out=soft[:, 0, :], in0=lam, scalar=-1.0, in1=lam, op0=ALU.mult, op1=ALU.max))
                eng.wait_ge(soft_exp, 1)
                chain(ts(soft[:, 2, :], soft[:, 1, :], 2.0, None, ALU.add))
                chain(nc.vector.reciprocal(soft[:, 2, :], soft[:, 2, :]))
                chain(tt(soft[:, 1, :], soft[:, 1, :], soft[:, 2, :], ALU.mult))
                chain(tt(soft[:, 2, :], soft[:, 1, :], soft[:, 1, :], ALU.mult))
                chain(ts(soft[:, 3, :], soft[:, 2, :], 1.0 / 17, 1.0 / 15, ALU.mult, ALU.add))
                for odd in (13, 11, 9, 7, 5, 3, 1):
                    chain(tt(soft[:, 3, :], soft[:, 3, :], soft[:, 2, :], ALU.mult))
                    chain(ts(soft[:, 3, :], soft[:, 3, :], 1.0 / odd, None, ALU.add))
                chain(tt(soft[:, 3, :], soft[:, 3, :], soft[:, 1, :], ALU.mult))
                chain(ts(soft[:, 0, :], lam, -1.0, 0.0, ALU.mult, ALU.max))
                chain(stt(out=decay[:], in0=soft[:, 3, :], scalar=2.0, in1=soft[:, 0, :],
                          op0=ALU.mult, op1=ALU.add))
                chain(ts(decay[:], decay[:], -LRU_C, None, ALU.mult))
                eng.wait_ge(consts_in, 16)
                for layer in range(DEPTH):
                    chain(tt(sink_pick[:, layer, :], sink[:, layer, :], cst[:, C_PICK:C_PICK + N_Q], ALU.mult))
                chain(nc.vector.tensor_reduce(sink_tail[:], sink_pick[:], AX.X, ALU.add))

            for j in range(3):
                split(j)
            for k in range(KD + 1):
                if k < KD:
                    eng.wait_ge(x_turned, k + 1)
                    nc.vector.tensor_copy(h[:, k, :], bank[k % 4][:, 0:T]).then_inc(h_ready, 1)
                if k >= 1:
                    low_part(0, k - 1, slice(0, T))
                if k == 3:
                    split(3)

            for layer in range(DEPTH):
                last = layer == DEPTH - 1
                ffn(2 * layer, 3 * layer, tokens(False), True)
                mixer(layer, 3 * layer + 1, tokens(last))
                ffn(2 * layer + 1, 3 * layer + 2, tokens(last), not last)
            for b in range(2):
                eng.wait_ge(out_turned, 2 * b + 2)
                nc.vector.tensor_copy(out_stage[:, 2 + b, :], bank[2 + b][:, :]).then_inc(out_dve, 1)

        @block.tensor
        def _(eng):
            mm = nc.tensor.matmul

            def product(to, s, at, x_hi, x_lo, start, stop):
                mm(to, w_hi[:, s, at:at + P], x_hi, start=start, stop=False)
                mm(to, w_hi[:, s, at:at + P], x_lo, start=False, stop=False)
                return mm(to, w_lo[:, s, at:at + P], x_hi, start=False, stop=stop)

            def wait_unit(n0, i=0):
                eng.wait_ge(w_lo_ready, n0 + 4 * i + 1)

            def project(n0, i, half, to, tok, free=(None, None), inc_even=False):
                wait_unit(n0, i)
                for b in range(2):
                    if free[b] is not None:
                        eng.wait_ge(*free[b])
                    for k in range(HALF):
                        c = half * HALF + k
                        last = product(to[b][:, tok], slot(n0), (2 * k + b) * P, h_hi[:, c, tok],
                                       h_lo[:, c, tok], c == 0, c == KD - 1)
                    if b == 0 and half == 1 and inc_even:
                        last.then_inc(even_psum, 1)
                last.then_inc(w_used, 1)

            def first_units(n0, version, tok, inc_even=False):
                for k in range(KD + 1):
                    if k < KD:
                        eng.wait_ge(h_hi_ready, KD * version + k + 1)
                        for pair in range(2):
                            n = n0 + 2 * (k // HALF) + pair
                            if k % HALF == 0:
                                wait_unit(n)
                            for b in range(2):
                                to = bank[2 * pair + b][:, tok]
                                at = (2 * (k % HALF) + b) * P
                                mm(to, w_hi[:, slot(n), at:at + P], h_hi[:, k, tok], start=(k == 0), stop=False)
                                mm(to, w_lo[:, slot(n), at:at + P], h_hi[:, k, tok], start=False, stop=False)
                    if k >= 1:
                        c = k - 1
                        if c % 2 == 0:
                            eng.wait_ge(h_lo_dve, HALF * version + c // 2 + 1)
                        else:
                            eng.wait_ge(h_lo_pool, HALF * version + c // 2 + 1)
                        for pair in range(2):
                            n = n0 + 2 * (c // HALF) + pair
                            for b in range(2):
                                at = (2 * (c % HALF) + b) * P
                                last = mm(bank[2 * pair + b][:, tok], w_hi[:, slot(n), at:at + P],
                                          h_lo[:, c, tok], start=False, stop=(c == KD - 1))
                                if c == KD - 1 and b == 0 and inc_even:
                                    last.then_inc(even_psum, 1)
                            if c % HALF == HALF - 1:
                                last.then_inc(w_used, 1)

            def norm_center(norm, tok):
                m = center_tiles(norm)
                eng.wait_ge(csum_step, centers(norm) + m)
                mm(bank[6][:, tok], ones_c[:, 0 if m == 6 else 1, :], csum[:, tok], start=True,
                   stop=True).then_inc(c_psum, 1)

            def norm_squares(norm, tok):
                eng.wait_ge(sumsq_step, 5 * norm + 5)
                mm(bank[7][:, tok], ones_d[:], sumsq[:, tok], start=True, stop=False)

            def norm_means(norm, tok):
                eng.wait_ge(c_ready, norm + 1)
                for d in range(center_tiles(norm), 7):
                    eng.wait_ge(zc_ready, KD * norm + d + 1)
                    mm(bank[6][:, tok], ones_d[:], h[:, d, tok], start=(d == center_tiles(norm)), stop=False)
                eng.wait_ge(sq_ready, KD * norm + 7)
                mm(bank[7][:, tok], ones_d[:], sq[:, 6, tok], start=False, stop=False)

            def norm_tail(norm, tok):
                eng.wait_ge(zc_ready, KD * norm + 8)
                mm(bank[6][:, tok], ones_d[:], h[:, 7, tok], start=False, stop=True).then_inc(dmu_psum, 1)
                eng.wait_ge(sq_ready, KD * norm + 8)
                mm(bank[7][:, tok], ones_d[:], sq[:, 7, tok], start=False, stop=True).then_inc(var_psum, 1)

            def ffn(f, norm, version, tok):
                u0 = ffn_unit0(f)
                first_units(u0, version, tok)
                if f == 0:
                    turn_params()
                with eng.Fori(1, GU_STEPS, 1) as i:
                    for j in range(4):
                        free = ((silu_done, mult_done)[j % 2], GU_STEPS * f + i)
                        b = 2 * (j % 2)
                        project(u0 + j, i, j // 2, bank[b:b + 2], tok, (free if j < 2 else None, None))
                d0 = u0 + N_GU

                def down(i, j):
                    n0 = d0 + j
                    k0, k1 = DOWN_K[j]
                    first = isinstance(i, int) and i == 0
                    wait_unit(n0, i)
                    for b in range(2):
                        if j == 0 and not first:
                            eng.wait_ge(z_ready, centers(norm) + 2 * i + b - 1)
                        closing = i == DOWN_STEPS - 1 and j == 3 and b == 1 if isinstance(i, int) else False
                        if closing:
                            norm_squares(norm, tok)
                        for k in range(k0, k1):
                            if closing and k == k1 - 1:
                                norm_means(norm, tok)
                            if first and b == 0 and (k == k0 or k % 2 == 0):
                                eng.wait_ge(a_lo_ready, GU_STEPS * f + k // 2 + 1)
                            last = product(bank[4 + b][:, tok], slot(n0), (2 * (k - k0) + b) * P,
                                           a_hi[:, k, tok], a_lo[:, k, tok], k == 0, k == KF - 1)
                        if b == 0 and j == 3:
                            last.then_inc(even_psum, 1)
                    last.then_inc(w_used, 1)

                for j in range(4):
                    down(0, j)
                with eng.Fori(1, DOWN_STEPS - 1, 1) as i:
                    for j in range(4):
                        down(i, j)
                down(DOWN_STEPS - 1, 0)
                norm_center(norm, tok)
                for j in range(1, 4):
                    down(DOWN_STEPS - 1, j)
                norm_tail(norm, tok)

            def gates(layer, r):
                n = RT * layer + r
                eng.wait_ge(conv_step, TAPS * (n + 1))
                if r >= 1:
                    eng.wait_ge(sig_ready, 2 * n)
                else:
                    eng.wait_ge(gates_in, 16 * 4 * DEPTH)
                mm(bank[6][:, 0:T], gate_w[:, layer, 0, r, :], xc[:, r, :], start=True, stop=True)
                mm(bank[7][:, 0:T], gate_w[:, layer, 1, r, :], xc[:, r, :], start=True,
                   stop=True).then_inc(gates_psum, 1)

            def swap(layer, p):
                n = 5 * layer + p
                if p == 0:
                    eng.wait_ge(kv_raw_ready, layer + 1)
                    src = k_raw
                else:
                    eng.wait_ge(q_raw_ready, 2 * layer + (p + 1) // 2)
                    src = q_raw[:, p - 1, :]
                if p >= 2:
                    eng.wait_ge(rope_s, n - 1)
                mm(bank[4 + p % 2][:, 0:T], perm, src, start=True, stop=True).then_inc(swap_psum, 1)

            def turn_values(layer):
                eng.wait_ge(kv_raw_ready, layer + 1)
                eng.wait_ge(sig_ready, 2 * RT * (layer + 1))
                for b in range(3):
                    n = min(P, T - b * P)
                    last = nc.tensor.transpose(bank[7][0:n, b * P:(b + 1) * P],
                                               v_raw[:, b * P:b * P + n], ident)
                last.then_inc(v_psum, 1)

            def scores(layer, s):
                g, t0, heads, q0, keys = STEPS[s]
                to = bank[SCORE_BANKS[s % 2]]
                if s == 0:
                    eng.wait_ge(rope_ready, 6 * layer + 6)
                    eng.wait_ge(masks_ready, 2)
                if s >= 2:
                    eng.wait_ge(exp_ready, NS * layer + s - 1)
                m0 = {128: 0, 256: P, 272: 3 * P}[keys]
                mm(to[:, 0:heads * keys], ident16[:], masks[:, m0:m0 + keys].unsqueeze(1).to_broadcast(
                    [P, heads, keys]), start=True, stop=False, skip_group_check=True)
                if g is None:
                    eng.wait_ge(q_tail_ready, layer + 1)
                    for g in range(N_KV):
                        last = mm(to[g * HEAD:(g + 1) * HEAD, 0:keys], q_tail[:],
                                  k_rot[:, g, 0:keys], start=False, stop=True, skip_group_check=True)
                else:
                    for i in range(heads):
                        last = mm(to[:, i * keys:(i + 1) * keys], q_rot[:, t0 + i, q0:q0 + P],
                                  k_rot[:, g, 0:keys], start=False, stop=(i == heads - 1), skip_group_check=True)
                last.then_inc(scores_psum, 1)

            def turn_probs(layer, s):
                g, t0, heads, q0, keys = STEPS[s]
                to = bank[TURN_BANKS[s % 2]]
                eng.wait_ge(probs_ready, NS * layer + s + 1)
                if s == 0:
                    eng.wait_ge(v_ready, 2 * layer + 2)
                elif s == 1:
                    eng.wait_ge(q_raw_ready, 2 * layer + 2)
                elif s % 2:
                    eng.wait_ge(pt_dve, 3 * layer + s // 2)
                else:
                    eng.wait_ge(pt_act, 4 * layer + s // 2)
                for b in range(-(-heads * keys // P)):
                    n = min(P, heads * keys - b * P)
                    last = nc.tensor.transpose(to[0:n, b * P:(b + 1) * P],
                                               probs[:, s % 4, b * P:b * P + n], ident)
                last.then_inc(probs_psum, 1)

            def attend(layer, s):
                g, t0, heads, q0, keys = STEPS[s]
                if s % 2:
                    eng.wait_ge(pt_dve, 3 * layer + s // 2 + 1)
                else:
                    eng.wait_ge(pt_act, 4 * layer + s // 2 + 1)
                pt = probs_t[:, s % 2, :]
                to = bank[PV_BANKS[s]]
                if s in (0, 2, 3):
                    eng.wait_ge(gate_ready, RT * layer + {0: 2, 2: 4, 3: 3}[s])
                if g is None:
                    for g in range(N_KV):
                        at = slice(g * HEAD, (g + 1) * HEAD)
                        for b in range(3):
                            n = min(P, T - b * P)
                            last = mm(to[at, 0:HEAD], v_tok[0:n, b, at],
                                      pt[0:n, b * P + g * HEAD:b * P + (g + 1) * HEAD],
                                      start=(b == 0), stop=(b == 2))
                else:
                    at = slice(g * HEAD, (g + 1) * HEAD)
                    kb = keys // P
                    view = pt.rearrange("p (h b q) -> p h b q", h=heads, b=kb)
                    for b in range(kb):
                        last = mm(to[at, t0 * P:(t0 + heads) * P], v_tok[:, b, at], view[:, :, b, :],
                                  start=(b == 0), stop=(b == kb - 1))
                last.then_inc(pv_done, 1)

            def recurrent_mean(layer, to, tok):
                eng.wait_ge(ysq_step, 3 * layer + 3)
                mm(to[:, tok], ones_r[:], sumsq[:, tok], start=True, stop=True).then_inc(rms_psum, 1)

            def attention_mean(layer, to, tok):
                eng.wait_ge(att_sq_ready, 3 * layer + 3)
                for r in range(QT):
                    last = mm(to[:, tok], ones_r[:], ig[:, r, tok], start=(r == 0), stop=(r == QT - 1))
                last.then_inc(rms_psum, 1)

            def project_out(layer, which, j, tok):
                n0 = out_unit0(layer) + 4 * which + j
                norm = 3 * layer + 1
                wait_unit(n0)
                for i in range(2):
                    d = 2 * j + i
                    if which == 0:
                        to = bank[OUT_BANKS[d % 3]]
                        if d < 2:
                            eng.wait_ge(ya_ready, 3 * layer + d + 1)
                        elif d >= 3:
                            eng.wait_ge(z_rec_ready, KD * layer + d - 2)
                    else:
                        to = bank[ATT_BANKS[d % 4]]
                        if d == 1:
                            eng.wait_ge(ya_ready, 3 * layer + 3)
                        elif d in (2, 3):
                            eng.wait_ge(z_rec_ready, KD * layer + 4 + d)
                        elif d >= 4:
                            eng.wait_ge(z_ready, centers(norm) + d - 3)
                    closing = which == 1 and d == KD - 1
                    if closing:
                        norm_squares(norm, tok)
                    for k in range(4):
                        if closing and k == 3:
                            norm_means(norm, tok)
                        if j == 0 and i == 0:
                            eng.wait_ge(y_lo_ready, 8 * layer + 4 * which + k + 1)
                        c = 4 * which + k
                        last = product(to[:, tok], slot(n0), (2 * k + i) * P, h_hi[:, c, tok],
                                       h_lo[:, c, tok], k == 0, k == 3)
                    if i == 0:
                        last.then_inc(even_psum, 1)
                        if which == 1 and j == 2:
                            norm_center(norm, tok)
                last.then_inc(w_used, 1)

            def mixer(layer, norm, version, tok):
                u0 = in_unit0(layer)
                full = slice(0, T)
                first_units(u0, version, full, True)
                q01, q23 = (q_raw_ready, 2 * layer + 1), (q_raw_ready, 2 * layer + 2)
                taps = (tap_ready, RT * (layer + 1))
                free = {2: (None, None), 3: (taps, taps), 4: (taps, taps), 5: (q01, q01),
                        6: (q23, (gate_ready, RT * layer + 1))}

                def unit(j):
                    pair, half = j // 2, j % 2
                    project(u0 + j, 0, half, [bank[b] for b in IN_BANKS[pair]], full,
                            free[pair] if half == 0 else (None, None), True)

                unit(4)
                gates(layer, 0)
                unit(5)
                gates(layer, 1)
                unit(6)
                swap(layer, 0)
                gates(layer, 2)
                unit(7)
                gates(layer, 3)
                unit(8)
                swap(layer, 1)
                swap(layer, 2)
                turn_values(layer)
                unit(9)
                unit(10)
                swap(layer, 3)
                swap(layer, 4)
                unit(11)
                scores(layer, 0)
                scores(layer, 1)
                unit(12)
                unit(13)
                turn_probs(layer, 0)
                scores(layer, 2)
                turn_probs(layer, 1)
                attend(layer, 0)
                scores(layer, 3)
                turn_probs(layer, 2)
                attend(layer, 1)
                scores(layer, 4)
                turn_probs(layer, 3)
                attend(layer, 2)
                scores(layer, 5)
                turn_probs(layer, 4)
                attend(layer, 3)
                recurrent_mean(layer, bank[4], tok)
                scores(layer, 6)
                turn_probs(layer, 5)
                attend(layer, 4)
                project_out(layer, 0, 0, tok)
                turn_probs(layer, 6)
                attend(layer, 5)
                project_out(layer, 0, 1, tok)
                attend(layer, 6)
                project_out(layer, 0, 2, tok)
                attention_mean(layer, bank[3], tok)
                project_out(layer, 0, 3, tok)
                for j in range(4):
                    project_out(layer, 1, j, tok)
                norm_tail(norm, tok)

            def turn_params():
                eng.wait_ge(params_in, 16 * (6 + 1 + 5 + 2 * DEPTH + 1))
                nc.tensor.transpose(bank[4][:, 0:LN_COLS], par_rows[0:LN_COLS, 0, :],
                                    cst[0:LN_COLS, C_ID:C_ID + LN_COLS]).then_inc(params_turned, 1)
                nc.tensor.transpose(bank[5][:, 0:ROWS_B], par_rows[0:ROWS_B, 1, :],
                                    cst[0:ROWS_B, C_ID:C_ID + ROWS_B]).then_inc(params_turned, 1)

            eng.wait_ge(ident_in, 16)
            eng.wait_ge(x_in, 64)
            for k in range(KD):
                if k >= 4:
                    eng.wait_ge(h_ready, k - 3)
                for a in range(3):
                    n = min(P, T - a * P)
                    last = nc.tensor.transpose(bank[k % 4][:, a * P:a * P + n],
                                               x_stage[0:n, a, k * P:(k + 1) * P],
                                               cst[0:n, C_ID:C_ID + n])
                last.then_inc(x_turned, 1)
            eng.wait_ge(zeroed, 9)
            eng.wait_ge(h_ready, KD)
            for layer in range(DEPTH):
                last = layer == DEPTH - 1
                ffn(2 * layer, 3 * layer, 3 * layer, tokens(False))
                mixer(layer, 3 * layer + 1, 3 * layer + 1, tokens(last))
                ffn(2 * layer + 1, 3 * layer + 2, 3 * layer + 2, tokens(last))
            for k in range(KD):
                eng.wait_ge(h_ready, KD * 3 * DEPTH + k + 1)
                for a in range(2):
                    q0 = N_META + a * P
                    mv = nc.tensor.transpose(bank[2 * a + k // 4][:, (k % 4) * P:(k % 4 + 1) * P],
                                             h[:, k, q0:q0 + P], ident)
                    if k % 4 == 3:
                        mv.then_inc(out_turned, 1)


_INS = ["x", "meta_tokens", "ffn1_w_gate", "ffn1_w_up", "ffn1_w_down", "ln1_g", "ln1_b", "w_in", "conv_w",
        "conv_b", "gate_a_w", "gate_a_b", "gate_x_w", "gate_x_b", "lru_lambda", "attn_sinks", "norm_rec_g",
        "norm_attn_g", "w_out", "ln2_g", "ln2_b", "ffn2_w_gate", "ffn2_w_up", "ffn2_w_down", "ln3_g", "ln3_b"]


def kernel(**inputs):
    import concourse.bacc as _bacc
    from concourse.bass_utils import run_bass_kernel_spmd as _run

    nc = _bacc.Bacc("TRN2", target_bir_lowering=False, num_devices=1)
    arrays, aps = {}, {}
    for name in _INS + ["shape_constants"]:
        a = np.ascontiguousarray(constants() if name == "shape_constants" else inputs[name])
        arrays[f"in_{name}"] = a
        aps[name] = nc.dram_tensor(f"in_{name}", a.shape, mybir.dt.from_np(a.dtype), kind="ExternalInput").ap()
    out = nc.dram_tensor("out", (1, SEQ, D_MODEL), F32, kind="ExternalOutput").ap()
    build(nc, aps, aps["shape_constants"], out)
    r = _run(nc, [arrays], core_ids=[0])
    return r.results[0]["out"]
```

```python
from contextlib import ExitStack

import numpy as np

import concourse.bass as bass
from concourse import mybir

F32 = mybir.dt.float32
F32R = mybir.dt.float32r
BF16 = mybir.dt.bfloat16
ACT = mybir.ActivationFunctionType
ALU = mybir.AluOpType
AX = mybir.AxisListType

P = 128
D_MODEL = 1024
SEQ = 256
DEPTH = 2
N_META = 16
D_FF = 2816
REC = 512
CONV = 4
LRU_C = 8.0
N_Q = 8
N_KV = 2
HEAD = 64
ATTN = N_Q * HEAD
WINDOW = 128
ROPE_DIM = HEAD // 4
ROPE_THETA = 500000.0
ALPHA = (2.0 * DEPTH) ** 0.25
LN_EPS = 1e-5
RMS_EPS = 1e-6
NEG_INF = -1e30
T = N_META + SEQ

KD = D_MODEL // P
KF = D_FF // P
RT = REC // P
QT = ATTN // P
SLOTS = 4
HALF = KD // 2
GU_STEPS = KF // 2
DOWN_STEPS = KD // 2
DOWN_K = [(0, 6), (6, 11), (11, 17), (17, 22)]
SLOT_TILES = max(2 * (k1 - k0) for k0, k1 in DOWN_K)

N_GU = 4 * GU_STEPS
N_DOWN = 4 * DOWN_STEPS
IN_PAIRS = 7
IN_BANKS = [(0, 1), (2, 3), (4, 5), (0, 1), (2, 3), (0, 1), (2, 0)]
N_IN = 2 * IN_PAIRS
N_OUT = KD
FFN_UNITS = N_GU + N_DOWN
LAYER_UNITS = 2 * FFN_UNITS + N_IN + N_OUT
ALL_UNITS = DEPTH * LAYER_UNITS

STEPS = [(0, 0, 4, 0, 128), (1, 0, 4, 0, 128), (None, 0, 1, 256, 272),
         (0, 0, 2, 128, 256), (0, 2, 2, 128, 256), (1, 0, 2, 128, 256), (1, 2, 2, 128, 256)]
NS = len(STEPS)
TAIL_STEP = 2
SCORE_BANKS = (6, 5)
TURN_BANKS = (7, 3)
PV_BANKS = (1, 1, 0, 2, 2, 2, 2)
OUT_BANKS = (1, 0, 4)
ATT_BANKS = (5, 2, 4, 1)
TAIL_Q = T - 2 * P
WARM = 16

CENTER_TILES = (6, 4, 6)

C_ID, C_PERM, C_COS, C_SIN, C_PICK = 0, P, 2 * P, 2 * P + T, 2 * P + 2 * T
C_MA = C_PICK + N_Q
C_MB, C_MC = C_MA + P, C_MA + 3 * P
C_ALL = C_MC + T

LN_COLS = 6 * DEPTH * KD
PC_CONVW = LN_COLS
PC_CONVB = PC_CONVW + DEPTH * CONV * RT
PC_GA, PC_GX, PC_LAM, PC_GREC, PC_GATT = (PC_CONVB + DEPTH * RT * i for i in range(1, 6))
PC_ALL = PC_GATT + DEPTH * QT
ROWS_B = PC_ALL - LN_COLS


def constants():
    c = np.zeros((P, C_ALL), np.float32)
    c[:, C_ID:C_ID + P] = np.eye(P, dtype=np.float32)
    half = ROPE_DIM // 2
    pos = np.arange(T, dtype=np.float32)
    inv = np.float32(ROPE_THETA) ** (-np.arange(0, ROPE_DIM, 2, dtype=np.float32) / np.float32(ROPE_DIM))
    ang = pos[:, None] * inv[None, :]
    cos, sin = np.cos(ang), np.sin(ang)
    c[:, C_COS:C_COS + T] = 1.0
    for base in (0, HEAD):
        for d in range(half):
            a, b = base + d, base + half + d
            c[b, C_PERM + a] = 1.0
            c[a, C_PERM + b] = 1.0
            c[a, C_COS:C_COS + T] = cos[:, d]
            c[b, C_COS:C_COS + T] = cos[:, d]
            c[a, C_SIN:C_SIN + T] = -sin[:, d]
            c[b, C_SIN:C_SIN + T] = sin[:, d]

    def mask(q, k):
        seen = (k <= q) & ((k < N_META) | (q - k < WINDOW))
        return np.where(seen, 0.0, NEG_INF).astype(np.float32)

    rows = np.arange(P)[:, None]
    c[:, C_MA:C_MA + P] = mask(rows, np.arange(P)[None, :])
    c[:, C_MB:C_MB + 2 * P] = mask(rows + P, np.arange(2 * P)[None, :])
    c[:, C_MC:C_MC + T] = mask(2 * P + rows % TAIL_Q, np.arange(T)[None, :])
    for p in range(P):
        c[p, C_PICK + 4 * (p // 64) + (p % 64) // TAIL_Q] = 1.0
    return c


def build(nc, w, consts, out):
    with ExitStack() as ctx:
        def sb(name, shape, dt=F32):
            return ctx.enter_context(nc.sbuf_tensor(name, shape, dt))

        def sem(name):
            return ctx.enter_context(nc.semaphore(name))

        banks = ctx.enter_context(nc.psum_tensor("banks", [P, 8, 512], F32))
        bank = [banks[:, i, :] for i in range(8)]
        arena_bytes = 2 * KF * T * 4
        arena = sb("arena", [P, arena_bytes // 4])
        arena_at = nc.sbuf_base - arena_bytes
        a_hi = nc.alloc_sbuf_tensor_at("a_hi", [P, KF, T], F32R, offset=arena_at)
        a_lo = nc.alloc_sbuf_tensor_at("a_lo", [P, KF, T], F32R, offset=arena_at + KF * T * 4)
        taken = [arena_at]

        def mix(name, shape):
            size = int(np.prod(shape[1:])) * 4
            t = nc.alloc_sbuf_tensor_at(name, shape, F32, offset=taken[0])
            taken[0] += (size + 31) // 32 * 32
            assert taken[0] <= arena_at + arena_bytes
            return t

        x_stage = nc.alloc_sbuf_tensor_at("x_stage", [P, 3, D_MODEL], F32, offset=arena_at)
        out_stage = nc.alloc_sbuf_tensor_at("out_stage", [P, 4, 512], F32, offset=arena_at)

        h = sb("h", [P, KD, T])
        h_hi = sb("h_hi", [P, KD, T], F32R)
        h_lo = sb("h_lo", [P, KD, T], F32R)
        raw = sb("raw", [P, SLOTS, SLOT_TILES * P])
        w_hi = sb("w_hi", [P, SLOTS, SLOT_TILES * P], F32R)
        w_lo = sb("w_lo", [P, SLOTS, SLOT_TILES * P], F32R)

        cst = sb("cst", [P, C_ALL])
        masks = sb("masks", [P, 3 * P + T], BF16)
        ident16 = sb("ident16", [P, P], BF16)
        ones_c = sb("ones_c", [P, 2, P])
        ones_d = sb("ones_d", [P, P])
        ones_r = sb("ones_r", [P, P])
        eps = sb("eps", [P, 4])
        par_rows = sb("par_rows", [P, 2, P])
        par = sb("par", [P, PC_ALL])
        decay = sb("decay", [P, DEPTH * RT])
        soft = sb("soft", [P, 4, DEPTH * RT])
        sink = sb("sink", [P, DEPTH, N_Q])
        sink_neg = sb("sink_neg", [P, DEPTH, N_Q])
        sink_pick = sb("sink_pick", [P, DEPTH, N_Q])
        sink_tail = sb("sink_tail", [P, DEPTH])
        sink_tail_neg = sb("sink_tail_neg", [P, DEPTH])
        gate_w = sb("gate_w", [P, DEPTH, 2, RT, P])

        sg = sb("sg", [P, 2, T])
        act = sb("act", [P, 2, T])
        csum = sb("csum", [P, T])
        center = sb("center", [P, T])
        sq = sb("sq", [P, KD, T])
        sumsq = sb("sumsq", [P, T])
        dsq = sb("dsq", [P, T])
        var = sb("var", [P, T])
        rstd = sb("rstd", [P, T])

        xr = mix("xr", [P, RT, T + CONV - 1])
        xc = mix("xc", [P, RT, T])
        ra = mix("ra", [P, RT, T])
        th = mix("th", [P, RT, T])
        ig = mix("ig", [P, RT, T])
        gl = mix("gl", [P, RT, T])
        yr = mix("yr", [P, RT, T])
        q_raw = mix("q_raw", [P, QT, T])
        q_rot = mix("q_rot", [P, QT, T])
        ya = mix("ya", [P, QT, T])
        kv_raw = mix("kv_raw", [P, 2, T])
        k_raw, v_raw = kv_raw[:, 0, :], kv_raw[:, 1, :]
        k_rot = sb("k_rot", [P, N_KV, T])
        v_tok = sb("v_tok", [P, 3, P])
        q_tail = sb("q_tail", [P, QT * TAIL_Q])
        turn = sb("turn", [P, 2, T])
        probs = sb("probs", [P, 4, 512])
        probs_t = sb("probs_t", [P, 2, 512])
        sm = sb("sm", [P, NS, 7, 4])
        MX, NEG, DSINK, ESINK, SUM, Z, RZ = range(7)

        ident = cst[:, C_ID:C_ID + P]
        perm = cst[:, C_PERM:C_PERM + P]
        cos = cst[:, C_COS:C_COS + T]
        sin = cst[:, C_SIN:C_SIN + T]

        raw_landed = [sem(f"raw_landed{s}") for s in range(SLOTS)]
        w_hi_ready = sem("w_hi_ready")
        w_lo_ready = sem("w_lo_ready")
        w_used = sem("w_used")
        ident_in = sem("ident_in")
        consts_in = sem("consts_in")
        params_in = sem("params_in")
        x_in = sem("x_in")
        gates_in = sem("gates_in")
        zeroed = sem("zeroed")
        masks_ready = sem("masks_ready")
        params_turned = sem("params_turned")
        params_ready = sem("params_ready")
        soft_step = sem("soft_step")
        soft_exp = sem("soft_exp")
        x_turned = sem("x_turned")
        h_ready = sem("h_ready")
        h_hi_ready = sem("h_hi_ready")
        h_lo_dve = sem("h_lo_dve")
        h_lo_pool = sem("h_lo_pool")
        even_psum = sem("even_psum")
        silu_done = sem("silu_done")
        mult_done = sem("mult_done")
        a_hi_ready = sem("a_hi_ready")
        a_lo_ready = sem("a_lo_ready")
        z_ready = sem("z_ready")
        csum_step = sem("csum_step")
        c_psum = sem("c_psum")
        c_ready = sem("c_ready")
        shifted = sem("shifted")
        zc_ready = sem("zc_ready")
        sq_ready = sem("sq_ready")
        sumsq_step = sem("sumsq_step")
        dmu_psum = sem("dmu_psum")
        var_psum = sem("var_psum")
        dsq_ready = sem("dsq_ready")
        var_ready = sem("var_ready")
        log_ready = sem("log_ready")
        rstd_ready = sem("rstd_ready")
        t_ready = sem("t_ready")
        u_ready = sem("u_ready")
        xr_padded = sem("xr_padded")
        xr_ready = sem("xr_ready")
        kv_raw_ready = sem("kv_raw_ready")
        q_raw_ready = sem("q_raw_ready")
        gate_ready = sem("gate_ready")
        tap_ready = sem("tap_ready")
        conv_step = sem("conv_step")
        gates_psum = sem("gates_psum")
        sig_ready = sem("sig_ready")
        decay_ready = sem("decay_ready")
        a2_ready = sem("a2_ready")
        m_ready = sem("m_ready")
        root_ready = sem("root_ready")
        ix_ready = sem("ix_ready")
        gx_ready = sem("gx_ready")
        scan_ready = sem("scan_ready")
        gelu_ready = sem("gelu_ready")
        yr_ready = sem("yr_ready")
        ya_ready = sem("ya_ready")
        ysq_ready = sem("ysq_ready")
        ysq_step = sem("ysq_step")
        att_sq_ready = sem("att_sq_ready")
        rms_psum = sem("rms_psum")
        rms_log = sem("rms_log")
        rms_ready = sem("rms_ready")
        yn_ready = sem("yn_ready")
        y_hi_ready = sem("y_hi_ready")
        y_lo_ready = sem("y_lo_ready")
        z_rec_ready = sem("z_rec_ready")
        swap_psum = sem("swap_psum")
        rope_c = sem("rope_c")
        rope_s = sem("rope_s")
        rope_ready = sem("rope_ready")
        q_tail_ready = sem("q_tail_ready")
        v_psum = sem("v_psum")
        v_ready = sem("v_ready")
        scores_psum = sem("scores_psum")
        max_step = sem("max_step")
        sum_step = sem("sum_step")
        exp_ready = sem("exp_ready")
        probs_ready = sem("probs_ready")
        probs_psum = sem("probs_psum")
        pt_act = sem("pt_act")
        pt_dve = sem("pt_dve")
        pv_done = sem("pv_done")
        out_turned = sem("out_turned")
        out_act = sem("out_act")
        out_dve = sem("out_dve")
        stored = sem("stored")

        block = ctx.enter_context(nc.Block())

        def slot(n0):
            return n0 % SLOTS

        def center_tiles(norm):
            return CENTER_TILES[norm % 3]

        def centers(norm):
            return sum(center_tiles(n) for n in range(norm))

        def shifts(norm):
            return KD * norm - centers(norm)

        def ffn_unit0(f):
            return (f // 2) * LAYER_UNITS + (f % 2) * (LAYER_UNITS - FFN_UNITS)

        def in_unit0(layer):
            return layer * LAYER_UNITS + FFN_UNITS

        def out_unit0(layer):
            return in_unit0(layer) + N_IN

        TAPS = CONV - 1
        EVENS = 2 * DOWN_STEPS + IN_PAIRS + N_OUT

        def unit_tiles(n0, i=0):
            n = n0 + 4 * (i if isinstance(i, int) else 1)
            r = n % LAYER_UNITS
            if r >= FFN_UNITS + N_IN + N_OUT:
                r -= FFN_UNITS + N_IN + N_OUT
            if N_GU <= r < FFN_UNITS:
                k0, k1 = DOWN_K[(r - N_GU) % 4]
                return 2 * (k1 - k0)
            return KD

        def is_query_unit(n):
            r = n % LAYER_UNITS - FFN_UNITS
            return 6 <= r < 10

        def query_views(ring, s):
            natural = ring[0][:, s, 0:KD * P].rearrange("p (k g t d) -> p k g t d", k=HALF, g=2, t=2)
            ordered = [r[:, s, 0:KD * P].rearrange("p (k t g d) -> p k t g d", k=HALF, g=2, t=2) for r in ring[1:]]
            return [(natural[:, :, :, t, :], [o[:, :, t, :, :] for o in ordered]) for t in range(2)]

        def tokens(f_or_norm_last):
            return slice(N_META if f_or_norm_last else 0, T)

        @block.sync
        def _(sp):
            def load(n0, i, tiles, sources):
                if not (isinstance(i, int) and n0 + 4 * i < SLOTS):
                    sp.wait_ge(w_lo_ready, n0 + 4 * i - 3)
                s = slot(n0)
                for to, src in sources:
                    sp.dma_start(to(raw[:, s, 0:tiles * P]), src).then_inc(raw_landed[s], 32 // len(sources))

            def chunks(k):
                return lambda r: r.rearrange("p (k m) -> p k m", k=k)

            def load_gate_up(f, i):
                layer, name = f // 2, ("ffn1", "ffn2")[f % 2]
                for j in range(4):
                    src = w[name + ("_w_gate", "_w_up")[j % 2]][layer].rearrange("(k p) n -> p k n", p=P)
                    k0 = (j // 2) * HALF
                    load(ffn_unit0(f) + j, i, KD,
                         [(chunks(HALF), src[:, k0:k0 + HALF, bass.ds(i * (2 * P), 2 * P)])])

            def load_down(f, i):
                layer, name = f // 2, ("ffn1", "ffn2")[f % 2]
                src = w[name + "_w_down"][layer].rearrange("(k p) n -> p k n", p=P)
                for j, (k0, k1) in enumerate(DOWN_K):
                    load(ffn_unit0(f) + N_GU + j, i, 2 * (k1 - k0),
                         [(chunks(k1 - k0), src[:, k0:k1, bass.ds(i * (2 * P), 2 * P)])])

            def load_ffn(f):
                load_gate_up(f, 0)
                with sp.Fori(1, GU_STEPS, 1) as i:
                    load_gate_up(f, i)
                with sp.Fori(0, DOWN_STEPS, 1) as i:
                    load_down(f, i)

            def load_mixer(layer):
                w_in = w["w_in"][layer].rearrange("(k p) n -> p k n", p=P)
                w_out = w["w_out"][layer]
                starts = [0, 2 * P, 2 * REC + ATTN, None, None, REC, REC + 2 * P]
                order = [(0, 0), (1, 0), (0, 1), (1, 1)] + [(p, b) for p in range(2, IN_PAIRS) for b in range(2)]
                for j, (pair, b) in enumerate(order):
                    ks = slice(b * HALF, (b + 1) * HALF)
                    if starts[pair] is not None:
                        c0 = starts[pair]
                        sources = [(chunks(HALF), w_in[:, ks, c0:c0 + 2 * P])]
                    else:
                        sources = []
                        for g in range(N_KV):
                            c0 = 2 * REC + (4 * g + 2 * (pair - 3)) * HEAD
                            sources.append((lambda r, g=g: r.rearrange("p (k m) -> p k m", k=HALF)
                                            [:, :, g * P:(g + 1) * P], w_in[:, ks, c0:c0 + P]))
                    load(in_unit0(layer) + j, 0, KD, sources)
                for j in range(N_OUT):
                    cols = slice((j % 4) * 2 * P, (j % 4 + 1) * 2 * P)
                    if j < 4:
                        src = w_out[0:REC].rearrange("(k p) n -> p k n", p=P)
                        sources = [(chunks(RT), src[:, :, cols])]
                    else:
                        src = w_out[REC:REC + ATTN].rearrange("(g t d) n -> g d t n", g=N_KV, t=QT)
                        sources = [(lambda r, g=g: r[g * HEAD:(g + 1) * HEAD].rearrange(
                            "p (k m) -> p k m", k=QT), src[g][:, :, cols]) for g in range(N_KV)]
                    load(out_unit0(layer) + j, 0, KD, sources)

            sp.dma_start(ident, consts[:, C_ID:C_ID + P]).then_inc(ident_in, 16)
            first = P - N_META
            sp.dma_start(x_stage[0:N_META, 0, :], w["meta_tokens"]).then_inc(x_in, 16)
            sp.dma_start(x_stage[N_META:P, 0, :], w["x"][0, 0:first]).then_inc(x_in, 16)
            sp.dma_start(x_stage[:, 1, :], w["x"][0, first:first + P]).then_inc(x_in, 16)
            sp.dma_start(x_stage[0:TAIL_Q, 2, :], w["x"][0, first + P:SEQ]).then_inc(x_in, 16)
            for layer in range(DEPTH):
                load_ffn(2 * layer)
                load_mixer(layer)
                load_ffn(2 * layer + 1)

            for b in range(2):
                for a in range(2):
                    sp.wait_ge((out_act, out_dve)[a], b + 1)
                    sp.dma_start(out[0, a * P:(a + 1) * P, b * 512:(b + 1) * 512],
                                 out_stage[:, 2 * a + b, :]).then_inc(stored, 16)
            sp.wait_ge(stored, 64)

        @block.gpsimd
        def _(pool):
            nc.gpsimd.memset(gate_w[:], 0.0).then_inc(zeroed, 1)
            nc.gpsimd.memset(ones_c[:, 0, :], 1.0 / (6 * P)).then_inc(zeroed, 1)
            nc.gpsimd.memset(ones_c[:, 1, :], 1.0 / (4 * P)).then_inc(zeroed, 1)
            nc.gpsimd.memset(ones_d[:], 1.0 / D_MODEL).then_inc(zeroed, 1)
            nc.gpsimd.memset(ones_r[:], 1.0 / REC).then_inc(zeroed, 1)
            nc.gpsimd.memset(eps[:, 0:1], LN_EPS / ALPHA ** 2).then_inc(zeroed, 1)
            nc.gpsimd.memset(eps[:, 1:2], RMS_EPS).then_inc(zeroed, 1)
            nc.gpsimd.memset(eps[:, 2:4], 1.0).then_inc(zeroed, 1)
            nc.gpsimd.memset(k_rot[:], 0.0).then_inc(zeroed, 1)

            def sum_squares(norm, tok):
                for d in range(1, center_tiles(norm)):
                    pool.wait_ge(sq_ready, KD * norm + d + 1)
                    if d > 1:
                        pool.wait_ge(sumsq_step, centers(norm) - norm + d - 1)
                    first = sq[:, 0, tok] if d == 1 else sumsq[:, tok]
                    nc.gpsimd.tensor_tensor(sumsq[:, tok], first, sq[:, d, tok], ALU.add).then_inc(sumsq_step, 1)

            def sum_group(layer, tok):
                for r in range(1, RT):
                    pool.wait_ge(ysq_ready, RT * layer + r + 1)
                    if r > 1:
                        pool.wait_ge(ysq_step, 3 * layer + r - 1)
                    first = th[:, 0, tok] if r == 1 else sumsq[:, tok]
                    nc.gpsimd.tensor_tensor(sumsq[:, tok], first, th[:, r, tok], ALU.add).then_inc(ysq_step, 1)

            def low_parts(version, tok):
                for k in range(1, KD, 2):
                    pool.wait_ge(h_ready, KD * version + k + 1)
                    pool.wait_ge(h_hi_ready, KD * version + k + 1)
                    nc.gpsimd.tensor_tensor(h_lo[:, k, tok], h[:, k, tok], h_hi[:, k, tok].bitcast(F32),
                                            ALU.subtract).then_inc(h_lo_pool, 1)

            def input_gate(layer, r):
                n = RT * layer + r
                pool.wait_ge(sig_ready, 2 * n + 2)
                pool.wait_ge(conv_step, TAPS * (n + 1))
                nc.gpsimd.tensor_tensor(ig[:, r, :], ig[:, r, :], xc[:, r, :], ALU.mult).then_inc(ix_ready, 1)

            def rope_cos(layer, p):
                if p == 0:
                    pool.wait_ge(swap_psum, 5 * layer + 1)
                    nc.gpsimd.tensor_tensor(k_raw, k_raw, cos, ALU.mult).then_inc(rope_c, 1)
                else:
                    pool.wait_ge(q_raw_ready, 2 * layer + (p + 1) // 2)
                    nc.gpsimd.tensor_tensor(q_rot[:, p - 1, :], q_raw[:, p - 1, :], cos,
                                            ALU.mult).then_inc(rope_c, 1)

            def mixer(layer, tok):
                input_gate(layer, 0)
                input_gate(layer, 1)
                rope_cos(layer, 0)
                input_gate(layer, 2)
                input_gate(layer, 3)
                rope_cos(layer, 1)
                rope_cos(layer, 2)
                for r in range(RT):
                    pool.wait_ge(decay_ready, RT * layer + r + 1)
                    nc.gpsimd.tensor_tensor(yr[:, r, :], ra[:, r, :], ra[:, r, :], ALU.mult).then_inc(a2_ready, 1)
                rope_cos(layer, 3)
                rope_cos(layer, 4)
                for r in range(RT):
                    pool.wait_ge(root_ready, RT * layer + r + 1)
                    pool.wait_ge(ix_ready, RT * layer + r + 1)
                    nc.gpsimd.tensor_tensor(ig[:, r, :], ig[:, r, :], th[:, r, :], ALU.mult).then_inc(gx_ready, 1)
                for r in range(RT):
                    pool.wait_ge(scan_ready, RT * layer + r + 1)
                    pool.wait_ge(gelu_ready, RT * layer + r + 1)
                    nc.gpsimd.tensor_tensor(yr[:, r, :], yr[:, r, :], gl[:, r, :], ALU.mult).then_inc(yr_ready, 1)
                sum_group(layer, tok)

            def load_small():
                pool.dma_start(cst[:, P:C_ALL], consts[:, P:C_ALL]).then_inc(consts_in, 16)
                row = 0
                for name in ("ln1_g", "ln1_b", "ln2_g", "ln2_b", "ln3_g", "ln3_b"):
                    n = DEPTH * KD
                    pool.dma_start(par_rows[row:row + n, 0, :],
                                  w[name].rearrange("l (k p) -> (l k) p", p=P)).then_inc(params_in, 16)
                    row += n
                n = DEPTH * CONV * RT
                pool.dma_start(par_rows[0:n, 1, :],
                              w["conv_w"].rearrange("l w (k p) -> (l w k) p", p=P)).then_inc(params_in, 16)
                row = n
                for name in ("conv_b", "gate_a_b", "gate_x_b", "lru_lambda", "norm_rec_g"):
                    pool.dma_start(par_rows[row:row + DEPTH * RT, 1, :],
                                  w[name].rearrange("l (k p) -> (l k) p", p=P)).then_inc(params_in, 16)
                    row += DEPTH * RT
                for layer in range(DEPTH):
                    for g in range(N_KV):
                        src = w["norm_attn_g"][layer].rearrange("(g t d) -> g t d", g=N_KV, t=QT)[g]
                        pool.dma_start(par_rows[row:row + QT, 1, g * HEAD:(g + 1) * HEAD], src).then_inc(params_in, 16)
                    row += QT
                pool.dma_start(sink[:], w["attn_sinks"].partition_broadcast(P)).then_inc(params_in, 16)
                pool.wait_ge(zeroed, 1)
                for layer in range(DEPTH):
                    for x, name in enumerate(("gate_a_w", "gate_x_w")):
                        src = w[name][layer].rearrange("(r b) i j -> b i r j", b=2)
                        for b in range(2):
                            at = slice(b * HEAD, (b + 1) * HEAD)
                            pool.dma_start(gate_w[at, layer, x, :, at], src[b]).then_inc(gates_in, 16)

            low_parts(0, slice(0, T))
            load_small()
            for layer in range(DEPTH):
                last = layer == DEPTH - 1
                sum_squares(3 * layer, tokens(False))
                low_parts(3 * layer + 1, tokens(False))
                mixer(layer, tokens(last))
                sum_squares(3 * layer + 1, tokens(last))
                low_parts(3 * layer + 2, tokens(last))
                sum_squares(3 * layer + 2, tokens(last))
                if not last:
                    low_parts(3 * layer + 3, tokens(False))

        @block.scalar
        def _(eng):
            act_fn = nc.scalar.activation

            def copy(to, src):
                return act_fn(to, src, ACT.Copy)

            def split(n0, i=0):
                if isinstance(i, int) and n0 + 4 * i >= ALL_UNITS:
                    return
                size = unit_tiles(n0, i) * P
                s = slot(n0)
                eng.wait_ge(raw_landed[s], (n0 // SLOTS + i + 1) * 32)
                if not (isinstance(i, int) and n0 + 4 * i < SLOTS):
                    eng.wait_ge(w_used, n0 + 4 * i - 3)
                if isinstance(i, int) and is_query_unit(n0 + 4 * i):
                    for src, (to,) in query_views((raw, w_hi), s):
                        last = copy(to, src)
                    last.then_inc(w_hi_ready, 1)
                else:
                    copy(w_hi[:, s, 0:size], raw[:, s, 0:size]).then_inc(w_hi_ready, 1)

            def gate_up(f, i, tok):
                u0, n = ffn_unit0(f), GU_STEPS * f + i
                split(u0 + 4, i)
                split(u0 + 5, i)
                eng.wait_ge(w_used, u0 + 4 * i + 3)
                act_fn(sg[:, :, tok], banks[:, 0:2, tok], ACT.Silu).then_inc(silu_done, 1)
                split(u0 + 6, i)
                split(u0 + 7, i)
                eng.wait_ge(mult_done, n + 1)
                copy(a_hi[:, bass.ds(2 * i, 2), tok], act[:, :, tok]).then_inc(a_hi_ready, 1)

            def norm_center(norm, tok):
                eng.wait_ge(c_psum, norm + 1)
                copy(center[:, tok], bank[6][:, tok]).then_inc(c_ready, 1)

            def norm_square(norm, d, tok):
                eng.wait_ge(zc_ready, KD * norm + d + 1)
                act_fn(sq[:, d, tok], h[:, d, tok], ACT.Square).then_inc(sq_ready, 1)

            def load_log_exp():
                nc.scalar.preload_act_table_set("natural_log_exp_and_others")

            def rsqrt_of(src, bias, log_done, done, count, tok):
                act_fn(var[:, tok], src, ACT.Ln, bias=bias).then_inc(log_done, 1)
                eng.wait_ge(log_done, count)
                act_fn(rstd[:, tok], var[:, tok], ACT.Exp, scale=-0.5).then_inc(done, 1)

            def norm_tail(norm, tok, last_split):
                layer, which = norm // 3, norm % 3
                norm_square(norm, KD - 1, tok)
                eng.wait_ge(dmu_psum, norm + 1)
                act_fn(dsq[:, tok], bank[6][:, tok], ACT.Square).then_inc(dsq_ready, 1)
                eng.wait_ge(var_ready, norm + 1)
                rsqrt_of(var[:, tok], eps[:, 0:1], log_ready, rstd_ready, norm + 1, tok)
                if last_split is None:
                    for k in range(KD):
                        g = (2 * which) * DEPTH * KD + layer * KD + k
                        b = g + DEPTH * KD
                        eng.wait_ge(u_ready, KD * norm + k + 1)
                        act_fn(h[:, k, tok], sq[:, k, tok], ACT.Identity, scale=par[:, g:g + 1],
                               bias=par[:, b:b + 1]).then_inc(h_ready, 1)
                    return
                for k in range(KD):
                    g = (2 * which) * DEPTH * KD + layer * KD + k
                    b = g + DEPTH * KD
                    eng.wait_ge(u_ready, KD * norm + k + 1)
                    act_fn(h_hi[:, k, tok], sq[:, k, tok], ACT.Identity, scale=par[:, g:g + 1],
                           bias=par[:, b:b + 1]).then_inc(h_hi_ready, 1)
                    if k == 1:
                        split(last_split)

            def ffn(f, norm, tok, parts):
                gate_up(f, 0, tok)
                nc.scalar.preload_act_table(ACT.Silu)
                with eng.Fori(1, GU_STEPS - 1, 1) as i:
                    gate_up(f, i, tok)
                gate_up(f, GU_STEPS - 1, tok)
                if f == 0:
                    setup()
                d0 = ffn_unit0(f) + N_GU
                with eng.Fori(0, DOWN_STEPS - 1, 1) as i:
                    for j in range(4):
                        split(d0 + 4 + j, i)
                n = d0 + 4 * (DOWN_STEPS - 1)
                norm_center(norm, tok)
                split(n + 4)
                for d in range(3):
                    norm_square(norm, d, tok)
                split(n + 5)
                for d in range(3, 6):
                    norm_square(norm, d, tok)
                load_log_exp()
                split(n + 6)
                norm_square(norm, 6, tok)
                norm_tail(norm, tok, n + 7 if parts else None)

            def softmax(layer, s):
                g, t0, heads, q0, keys = STEPS[s]
                eng.wait_ge(max_step, 3 * (NS * layer + s) + 3)
                if s >= 4:
                    eng.wait_ge(probs_psum, NS * layer + s - 3)
                act_fn(sm[:, s, ESINK, 0:heads], sm[:, s, DSINK, 0:heads], ACT.Exp)
                for i in range(heads):
                    last = act_fn(probs[:, s % 4, i * keys:(i + 1) * keys],
                                  bank[SCORE_BANKS[s % 2]][:, i * keys:(i + 1) * keys], ACT.Exp,
                                  bias=sm[:, s, NEG, i:i + 1], scale=HEAD ** -0.5,
                                  accum_out=sm[:, s, SUM, i:i + 1])
                last.then_inc(exp_ready, 1)

            def probs_copy(layer, s):
                eng.wait_ge(probs_psum, NS * layer + s + 1)
                if s == TAIL_STEP:
                    src = bank[TURN_BANKS[s % 2]]
                    copy(probs_t[:, s % 2, 0:2 * P], src[:, 0:2 * P])
                    copy(probs_t[0:TAIL_Q, s % 2, 2 * P:3 * P],
                         src[0:TAIL_Q, 2 * P:3 * P]).then_inc(pt_act, 1)
                else:
                    copy(probs_t[:, s % 2, :], bank[TURN_BANKS[s % 2]][:, :]).then_inc(pt_act, 1)

            def attended(layer, steps, src, q0, n):
                eng.wait_ge(pv_done, NS * layer + steps)
                eng.wait_ge(scan_ready, RT * (layer + 1))
                view = src[:, 0:QT * n].rearrange("p (t q) -> p t q", t=QT)
                act_fn(ig[:, :, q0:q0 + n], view, ACT.Square).then_inc(att_sq_ready, 1)
                copy(ya[:, :, q0:q0 + n], view).then_inc(ya_ready, 1)

            def recurrent_squares(layer, tok):
                for r in range(RT):
                    eng.wait_ge(yr_ready, RT * layer + r + 1)
                    act_fn(th[:, r, tok], yr[:, r, tok], ACT.Square).then_inc(ysq_ready, 1)

            def group_root(layer, which, src, tok):
                eng.wait_ge(rms_psum, 2 * layer + which + 1)
                rsqrt_of(src[:, tok], eps[:, 1:2], rms_log, rms_ready, 2 * layer + which + 1, tok)

            def group_high(layer, which, src, tok):
                for r in range(RT):
                    eng.wait_ge(yn_ready, 8 * layer + 4 * which + r + 1)
                    copy(h_hi[:, 4 * which + r, tok], src[:, r, tok]).then_inc(y_hi_ready, 1)

            def sigmoids(layer, r):
                eng.wait_ge(gates_psum, RT * layer + r + 1)
                for b, to, pc in ((6, ra, PC_GA), (7, ig, PC_GX)):
                    c = pc + RT * layer + r
                    act_fn(to[:, r, :], bank[b][:, 0:T], ACT.Sigmoid, bias=par[:, c:c + 1]).then_inc(sig_ready, 1)

            def decays(layer, r):
                c = RT * layer + r
                eng.wait_ge(sig_ready, 2 * c + 2)
                act_fn(th[:, r, :], ra[:, r, :], ACT.Tanh, scale=decay[:, c:c + 1])
                act_fn(ra[:, r, :], ra[:, r, :], ACT.Exp, scale=decay[:, c:c + 1]).then_inc(decay_ready, 1)

            def recurrent_tile(layer, r):
                eng.wait_ge(w_used, in_unit0(layer) + 4)
                wc, cb = PC_CONVW + (layer * CONV + CONV - 1) * RT + r, PC_CONVB + layer * RT + r
                copy(xr[:, r, CONV - 1:], bank[r][:, 0:T]).then_inc(xr_ready, 1)
                act_fn(xc[:, r, :], bank[r][:, 0:T], ACT.Identity, scale=par[:, wc:wc + 1],
                       bias=par[:, cb:cb + 1]).then_inc(tap_ready, 1)

            def roots(layer):
                for r in range(RT):
                    eng.wait_ge(m_ready, RT * layer + r + 1)
                    act_fn(th[:, r, :], th[:, r, :], ACT.Sqrt, scale=-1.0).then_inc(root_ready, 1)

            def gelus(layer):
                eng.wait_ge(gate_ready, RT * layer + RT)
                for r in range(RT):
                    act_fn(gl[:, r, :], gl[:, r, :], ACT.Gelu_apprx_tanh).then_inc(gelu_ready, 1)

            def mixer(layer, norm, tok):
                u0, o0 = in_unit0(layer), out_unit0(layer)

                def tile(pair, b):
                    if b == 0:
                        eng.wait_ge(even_psum, EVENS * layer + DOWN_STEPS + pair + 1)
                    else:
                        eng.wait_ge(w_used, u0 + 2 * pair + 2)

                def take_kv():
                    tile(2, 1)
                    copy(kv_raw[:, :, :], banks[:, 4:6, 0:T]).then_inc(kv_raw_ready, 1)

                def take_queries(half):
                    tile(3 + half, 1)
                    at = slice(2 * half, 2 * half + 2)
                    copy(q_raw[:, at, :], banks[:, at, 0:T]).then_inc(q_raw_ready, 1)

                def take_gate(r):
                    tile(5 + r // 2, r % 2)
                    copy(gl[:, r, :], bank[IN_BANKS[5 + r // 2][r % 2]][:, 0:T]).then_inc(gate_ready, 1)

                split(u0 + 4)
                split(u0 + 5)
                recurrent_tile(layer, 0)
                recurrent_tile(layer, 1)
                recurrent_tile(layer, 2)
                recurrent_tile(layer, 3)
                split(u0 + 6)
                sigmoids(layer, 0)
                split(u0 + 7)
                split(u0 + 8)
                sigmoids(layer, 1)
                split(u0 + 9)
                sigmoids(layer, 2)
                take_kv()
                split(u0 + 10)
                split(u0 + 11)
                take_queries(0)
                sigmoids(layer, 3)
                decays(layer, 0)
                split(u0 + 12)
                decays(layer, 1)
                decays(layer, 2)
                split(u0 + 13)
                decays(layer, 3)
                take_queries(1)
                roots(layer)
                split(o0)
                take_gate(0)
                load_log_exp()
                take_gate(1)
                softmax(layer, 0)
                split(o0 + 1)
                softmax(layer, 1)
                split(o0 + 2)
                take_gate(2)
                take_gate(3)
                softmax(layer, 2)
                gelus(layer)
                probs_copy(layer, 0)
                load_log_exp()
                softmax(layer, 3)
                recurrent_squares(layer, tok)
                attended(layer, 2, bank[1], 0, P)
                probs_copy(layer, 2)
                softmax(layer, 4)
                softmax(layer, 5)
                attended(layer, 3, bank[0], 2 * P, TAIL_Q)
                group_root(layer, 0, bank[4], tok)
                split(o0 + 3)
                probs_copy(layer, 4)
                group_high(layer, 0, yr, tok)
                softmax(layer, 6)
                probs_copy(layer, 6)
                split(o0 + 4)
                attended(layer, 7, bank[2], P, P)
                split(o0 + 5)
                group_root(layer, 1, bank[3], tok)
                split(o0 + 6)
                group_high(layer, 1, ya, tok)
                split(o0 + 7)
                split(o0 + 8)
                norm_center(norm, tok)
                norm_square(norm, 0, tok)
                norm_square(norm, 1, tok)
                norm_square(norm, 2, tok)
                norm_square(norm, 3, tok)
                norm_square(norm, 4, tok)
                split(o0 + 9)
                norm_square(norm, 5, tok)
                norm_square(norm, 6, tok)
                split(o0 + 10)
                norm_tail(norm, tok, o0 + 11)

            def high_part(k):
                eng.wait_ge(h_ready, k + 1)
                copy(h_hi[:, k, :], h[:, k, :]).then_inc(h_hi_ready, 1)

            def setup():
                eng.wait_ge(ident_in, 16)
                copy(ident16[:], ident).then_inc(masks_ready, 1)
                eng.wait_ge(consts_in, 16)
                copy(masks[:], cst[:, C_MA:C_ALL]).then_inc(masks_ready, 1)
                eng.wait_ge(soft_step, 1)
                act_fn(soft[:, 1, :], soft[:, 0, :], ACT.Exp, scale=-1.0).then_inc(soft_exp, 1)

            split(0)
            for k in range(KD):
                high_part(k)
                if k in (1, 3, 5):
                    split(1 + k // 2)

            for layer in range(DEPTH):
                last = layer == DEPTH - 1
                ffn(2 * layer, 3 * layer, tokens(False), True)
                mixer(layer, 3 * layer + 1, tokens(last))
                ffn(2 * layer + 1, 3 * layer + 2, tokens(last), not last)
            for b in range(2):
                eng.wait_ge(out_turned, 2 * b + 1)
                copy(out_stage[:, b, :], bank[b][:, :]).then_inc(out_act, 1)

        @block.vector
        def _(eng):
            tt = nc.vector.tensor_tensor
            ts = nc.vector.tensor_scalar
            stt = nc.vector.scalar_tensor_tensor

            def split(n0, i=0):
                if isinstance(i, int) and n0 + 4 * i >= ALL_UNITS:
                    return
                size = unit_tiles(n0, i) * P
                s = slot(n0)
                eng.wait_ge(w_hi_ready, n0 + 4 * i + 1)
                if isinstance(i, int) and is_query_unit(n0 + 4 * i):
                    for src, (hi, lo) in query_views((raw, w_hi, w_lo), s):
                        last = tt(lo, src, hi.bitcast(F32), ALU.subtract)
                    last.then_inc(w_lo_ready, 1)
                else:
                    tt(w_lo[:, s, 0:size], raw[:, s, 0:size],
                       w_hi[:, s, 0:size].bitcast(F32), ALU.subtract).then_inc(w_lo_ready, 1)

            def gate_up(f, i, tok):
                u0, n = ffn_unit0(f), GU_STEPS * f + i
                split(u0 + 4, i)
                split(u0 + 5, i)
                split(u0 + 6, i)
                eng.wait_ge(silu_done, n + 1)
                eng.wait_ge(w_used, u0 + 4 * i + 4)
                if not (isinstance(i, int) and n == 0):
                    eng.wait_ge(a_lo_ready, n)
                tt(act[:, :, tok], sg[:, :, tok], banks[:, 2:4, tok], ALU.mult).then_inc(mult_done, 1)
                split(u0 + 7, i)
                eng.wait_ge(a_hi_ready, n + 1)
                at = bass.ds(2 * i, 2)
                tt(a_lo[:, at, tok], act[:, :, tok], a_hi[:, at, tok].bitcast(F32),
                   ALU.subtract).then_inc(a_lo_ready, 1)

            def residual(i, d, src, scale, tok, done):
                at = bass.ds(2 * i + d, 1)
                stt(out=h[:, at, tok], in0=src[:, tok].unsqueeze(1), scalar=scale, in1=h[:, at, tok],
                    op0=ALU.mult, op1=ALU.add).then_inc(done, 1)

            def center_sum(norm, i, d, tok):
                at = bass.ds(2 * i + d, 1)
                eng.wait_ge(z_ready, centers(norm) + 2 * i + d + 1)
                to = csum[:, tok].unsqueeze(1)
                if isinstance(i, int) and i == 0 and d == 0:
                    nc.vector.tensor_copy(to, h[:, at, tok]).then_inc(csum_step, 1)
                else:
                    eng.wait_ge(csum_step, centers(norm) + 2 * i + d)
                    tt(to, to, h[:, at, tok], ALU.add).then_inc(csum_step, 1)

            def centered(norm, d, tok):
                eng.wait_ge(c_ready, norm + 1)
                tt(h[:, d, tok], h[:, d, tok], center[:, tok], ALU.subtract).then_inc(
                    zc_ready if d < center_tiles(norm) else shifted, 1)

            def low_part(version, k, tok):
                if k % 2 == 0:
                    eng.wait_ge(h_ready, KD * version + k + 1)
                    eng.wait_ge(h_hi_ready, KD * version + k + 1)
                    tt(h_lo[:, k, tok], h[:, k, tok], h_hi[:, k, tok].bitcast(F32),
                       ALU.subtract).then_inc(h_lo_dve, 1)

            def norm_tail(norm, tok, last_split):
                layer, which = norm // 3, norm % 3

                def subtract(k):
                    tt(h[:, k, tok], h[:, k, tok], bank[6][:, tok], ALU.subtract).then_inc(t_ready, 1)

                def scale(k):
                    eng.wait_ge(t_ready, KD * norm + k + 1)
                    tt(sq[:, k, tok], h[:, k, tok], rstd[:, tok], ALU.mult).then_inc(u_ready, 1)

                def affine(k):
                    g = (2 * which) * DEPTH * KD + layer * KD + k
                    b = g + DEPTH * KD
                    eng.wait_ge(u_ready, KD * norm + k + 1)
                    ts(h[:, k, tok], sq[:, k, tok], par[:, g:g + 1], par[:, b:b + 1],
                       ALU.mult, ALU.add).then_inc(h_ready, 1)

                eng.wait_ge(dsq_ready, norm + 1)
                eng.wait_ge(var_psum, norm + 1)
                tt(var[:, tok], bank[7][:, tok], dsq[:, tok], ALU.subtract).then_inc(var_ready, 1)
                subtract(0)
                subtract(1)
                subtract(2)
                eng.wait_ge(rstd_ready, norm + 1)
                for k in range(KD + 2):
                    if k < KD:
                        scale(k)
                    if k + 3 < KD:
                        subtract(k + 3)
                    if 1 <= k <= KD and last_split is not None:
                        affine(k - 1)
                    if last_split is not None:
                        if k >= 2:
                            low_part(norm + 1, k - 2, tok)
                        if k == 4:
                            split(last_split)

            def ffn(f, norm, tok, parts):
                gate_up(f, 0, tok)
                with eng.Fori(1, GU_STEPS - 1, 1) as i:
                    gate_up(f, i, tok)
                gate_up(f, GU_STEPS - 1, tok)
                if f == 0:
                    setup()
                d0 = ffn_unit0(f) + N_GU
                evens = EVENS * (f // 2) + (f % 2) * (EVENS - DOWN_STEPS)

                def down(i):
                    split(d0 + 4, i)
                    split(d0 + 5, i)
                    eng.wait_ge(even_psum, evens + i + 1)
                    residual(i, 0, bank[4], 0.5 / ALPHA, tok, z_ready)
                    split(d0 + 6, i)
                    center_sum(norm, i, 0, tok)
                    eng.wait_ge(w_used, d0 + 4 * i + 4)
                    residual(i, 1, bank[5], 0.5 / ALPHA, tok, z_ready)
                    center_sum(norm, i, 1, tok)
                    split(d0 + 7, i)

                down(0)
                with eng.Fori(1, DOWN_STEPS - 1, 1) as i:
                    down(i)
                n = d0 + 4 * (DOWN_STEPS - 1)
                for d in (6, 7, 0, 1):
                    centered(norm, d, tok)
                split(n + 4)
                for d in range(2, 6):
                    centered(norm, d, tok)
                split(n + 5)
                split(n + 6)
                eng.wait_ge(shifted, shifts(norm) + 2)
                for b in range(2):
                    if b == 0:
                        eng.wait_ge(even_psum, evens + DOWN_STEPS)
                    else:
                        eng.wait_ge(w_used, n + 4)
                    residual(0, 6 + b, bank[4 + b], 0.5 / ALPHA, tok, zc_ready)
                norm_tail(norm, tok, n + 7 if parts else None)

            def conv(layer, r):
                eng.wait_ge(xr_ready, RT * layer + r + 1)
                eng.wait_ge(xr_padded, layer + 1)
                eng.wait_ge(tap_ready, RT * layer + r + 1)
                base = TAPS * (RT * layer + r)
                for k in range(TAPS):
                    c = PC_CONVW + (layer * CONV + k) * RT + r
                    if k:
                        eng.wait_ge(conv_step, base + k)
                    stt(out=xc[:, r, :], in0=xr[:, r, k:k + T], scalar=par[:, c:c + 1],
                        in1=xc[:, r, :], op0=ALU.mult, op1=ALU.add).then_inc(conv_step, 1)

            def rope(layer, p):
                mid = k_raw if p == 0 else q_rot[:, p - 1, :]
                n = 5 * layer + p
                eng.wait_ge(swap_psum, n + 1)
                if p >= 2:
                    eng.wait_ge(rope_ready, 6 * layer + p)
                elif layer:
                    eng.wait_ge(rope_ready, 6 * layer)
                tt(turn[:, p % 2, :], bank[4 + p % 2][:, 0:T], sin, ALU.mult).then_inc(rope_s, 1)
                eng.wait_ge(rope_s, n + 1)
                eng.wait_ge(rope_c, n + 1)
                if p == 0:
                    for g in range(N_KV):
                        at = slice(g * HEAD, (g + 1) * HEAD)
                        tt(k_rot[at, g, :], kv_raw[at, 0, :], turn[at, 0, :], ALU.add).then_inc(rope_ready, 1)
                else:
                    tt(mid, mid, turn[:, p % 2, :], ALU.add).then_inc(rope_ready, 1)

            def query_tail(layer):
                eng.wait_ge(rope_ready, 6 * layer + 6)
                nc.vector.tensor_copy(q_tail[:].rearrange("p (t q) -> p t q", t=QT),
                                      q_rot[:, :, 2 * P:T]).then_inc(q_tail_ready, 1)

            def values(layer):
                eng.wait_ge(v_psum, layer + 1)
                nc.vector.tensor_copy(v_tok[:, 0:2, :], bank[7][:, 0:2 * P].rearrange(
                    "p (b c) -> p b c", b=2)).then_inc(v_ready, 1)
                nc.vector.tensor_copy(v_tok[0:TAIL_Q, 2, :], bank[7][0:TAIL_Q, 2 * P:3 * P]).then_inc(v_ready, 1)

            def decay_root(layer, r):
                n = RT * layer + r
                eng.wait_ge(a2_ready, n + 1)
                stt(out=th[:, r, :], in0=yr[:, r, :], scalar=1.0, in1=th[:, r, :],
                    op0=ALU.add, op1=ALU.mult).then_inc(m_ready, 1)

            def scan(layer, r):
                n = RT * layer + r
                eng.wait_ge(gx_ready, n + 1)
                nc.vector.tensor_tensor_scan(yr[:, r, :], ra[:, r, :], ig[:, r, :], 0.0,
                                             ALU.mult, ALU.add).then_inc(scan_ready, 1)

            def maxima(layer, s):
                g, t0, heads, q0, keys = STEPS[s]
                n = 3 * (NS * layer + s)
                eng.wait_ge(scores_psum, NS * layer + s + 1)
                v = sm[:, s, :, 0:heads]
                if g is None:
                    own, own_neg = sink_tail[:, layer:layer + 1], sink_tail_neg[:, layer:layer + 1]
                else:
                    at = slice(4 * g + t0, 4 * g + t0 + heads)
                    own, own_neg = sink[:, layer, at], sink_neg[:, layer, at]
                nc.vector.tensor_reduce(v[:, MX], bank[SCORE_BANKS[s % 2]][:, 0:heads * keys].rearrange(
                    "p (h k) -> p h k", h=heads), AX.X, ALU.max).then_inc(max_step, 1)
                eng.wait_ge(max_step, n + 1)
                stt(out=v[:, NEG], in0=v[:, MX], scalar=-HEAD ** -0.5, in1=own_neg,
                    op0=ALU.mult, op1=ALU.min).then_inc(max_step, 1)
                eng.wait_ge(max_step, n + 2)
                tt(v[:, DSINK], own, v[:, NEG], ALU.add).then_inc(max_step, 1)

            def normalize(layer, s):
                g, t0, heads, q0, keys = STEPS[s]
                n = 2 * (NS * layer + s)
                v = sm[:, s, :, 0:heads]
                eng.wait_ge(exp_ready, NS * layer + s + 1)
                tt(v[:, Z], v[:, SUM], v[:, ESINK], ALU.add).then_inc(sum_step, 1)
                eng.wait_ge(sum_step, n + 1)
                nc.vector.reciprocal(v[:, RZ], v[:, Z]).then_inc(sum_step, 1)
                eng.wait_ge(sum_step, n + 2)
                for i in range(heads):
                    at = probs[:, s % 4, i * keys:(i + 1) * keys]
                    last = ts(at, at, sm[:, s, RZ, i:i + 1], None, ALU.mult)
                last.then_inc(probs_ready, 1)

            def probs_copy(layer, s):
                eng.wait_ge(probs_psum, NS * layer + s + 1)
                nc.vector.tensor_copy(probs_t[:, s % 2, :], bank[TURN_BANKS[s % 2]][:, :]).then_inc(pt_dve, 1)

            def group_norm(layer, which, src, pc, tok):
                eng.wait_ge(rms_ready, 2 * layer + which + 1)
                n = 8 * layer + 4 * which
                for r in range(RT + 1):
                    if r < RT:
                        c = pc + RT * layer + r
                        stt(out=src[:, r, tok], in0=src[:, r, tok], scalar=par[:, c:c + 1],
                            in1=rstd[:, tok], op0=ALU.mult, op1=ALU.mult).then_inc(yn_ready, 1)
                    if r >= 1:
                        eng.wait_ge(y_hi_ready, n + r)
                        tt(h_lo[:, 4 * which + r - 1, tok], src[:, r - 1, tok],
                           h_hi[:, 4 * which + r - 1, tok].bitcast(F32), ALU.subtract).then_inc(y_lo_ready, 1)

            def mixer(layer, norm, tok):
                u0, o0 = in_unit0(layer), out_unit0(layer)
                evens = EVENS * layer + DOWN_STEPS + IN_PAIRS

                def out_tile(which, j, b):
                    if b == 0:
                        eng.wait_ge(even_psum, evens + 4 * which + j + 1)
                    else:
                        eng.wait_ge(w_used, o0 + 4 * which + j + 1)

                def recurrent_out(d):
                    out_tile(0, d // 2, d % 2)
                    residual(0, d, bank[OUT_BANKS[d % 3]], 1.0 / ALPHA, tok, z_rec_ready)

                def attention_out(d):
                    eng.wait_ge(z_rec_ready, KD * layer + d + 1)
                    center = d < center_tiles(norm)
                    if not center:
                        eng.wait_ge(shifted, shifts(norm) + d - center_tiles(norm) + 1)
                    out_tile(1, d // 2, d % 2)
                    residual(0, d, bank[ATT_BANKS[d % 4]], 1.0 / ALPHA, tok, z_ready if center else zc_ready)
                    if center:
                        center_sum(norm, 0, d, tok)

                nc.vector.memset(xr[:, :, 0:CONV - 1], 0.0).then_inc(xr_padded, 1)
                split(u0 + 4)
                split(u0 + 5)
                conv(layer, 0)
                conv(layer, 1)
                conv(layer, 2)
                split(u0 + 6)
                split(u0 + 7)
                conv(layer, 3)
                split(u0 + 8)
                split(u0 + 9)
                split(u0 + 10)
                rope(layer, 0)
                rope(layer, 1)
                split(u0 + 11)
                rope(layer, 2)
                for r in range(RT):
                    decay_root(layer, r)
                split(u0 + 12)
                rope(layer, 3)
                rope(layer, 4)
                scan(layer, 0)
                split(u0 + 13)
                query_tail(layer)
                maxima(layer, 0)
                values(layer)
                split(o0)
                scan(layer, 1)
                maxima(layer, 1)
                scan(layer, 2)
                normalize(layer, 0)
                maxima(layer, 2)
                normalize(layer, 1)
                scan(layer, 3)
                split(o0 + 1)
                normalize(layer, 2)
                maxima(layer, 3)
                probs_copy(layer, 1)
                split(o0 + 2)
                normalize(layer, 3)
                maxima(layer, 4)
                probs_copy(layer, 3)
                maxima(layer, 5)
                normalize(layer, 4)
                maxima(layer, 6)
                normalize(layer, 5)
                group_norm(layer, 0, yr, PC_GREC, tok)
                probs_copy(layer, 5)
                normalize(layer, 6)
                recurrent_out(0)
                split(o0 + 3)
                recurrent_out(1)
                recurrent_out(2)
                split(o0 + 4)
                recurrent_out(3)
                split(o0 + 5)
                recurrent_out(4)
                recurrent_out(5)
                group_norm(layer, 1, ya, PC_GATT, tok)
                split(o0 + 6)
                attention_out(0)
                recurrent_out(6)
                split(o0 + 7)
                attention_out(1)
                attention_out(2)
                attention_out(3)
                split(o0 + 8)
                centered(norm, 0, tok)
                centered(norm, 1, tok)
                centered(norm, 2, tok)
                centered(norm, 3, tok)
                centered(norm, 4, tok)
                attention_out(4)
                centered(norm, 5, tok)
                recurrent_out(7)
                attention_out(5)
                centered(norm, 6, tok)
                attention_out(6)
                centered(norm, 7, tok)
                split(o0 + 9)
                split(o0 + 10)
                attention_out(7)
                norm_tail(norm, tok, o0 + 11)

            def setup():
                eng.wait_ge(params_turned, 1)
                nc.vector.tensor_copy(par[:, 0:LN_COLS], bank[6][:, 0:LN_COLS]).then_inc(params_ready, 1)
                eng.wait_ge(params_turned, 2)
                nc.vector.tensor_copy(par[:, LN_COLS:PC_ALL], bank[7][:, 0:ROWS_B]).then_inc(params_ready, 1)

                eng.wait_ge(params_ready, 2)
                lam = par[:, PC_LAM:PC_LAM + DEPTH * RT]
                steps = [0]

                def chain(instruction):
                    steps[0] += 1
                    instruction.then_inc(soft_step, 1)
                    eng.wait_ge(soft_step, steps[0])

                chain(stt(out=soft[:, 0, :], in0=lam, scalar=-1.0, in1=lam, op0=ALU.mult, op1=ALU.max))
                eng.wait_ge(soft_exp, 1)
                chain(ts(soft[:, 2, :], soft[:, 1, :], 2.0, None, ALU.add))
                chain(nc.vector.reciprocal(soft[:, 2, :], soft[:, 2, :]))
                chain(tt(soft[:, 1, :], soft[:, 1, :], soft[:, 2, :], ALU.mult))
                chain(tt(soft[:, 2, :], soft[:, 1, :], soft[:, 1, :], ALU.mult))
                chain(ts(soft[:, 3, :], soft[:, 2, :], 1.0 / 17, 1.0 / 15, ALU.mult, ALU.add))
                for odd in (13, 11, 9, 7, 5, 3, 1):
                    chain(tt(soft[:, 3, :], soft[:, 3, :], soft[:, 2, :], ALU.mult))
                    chain(ts(soft[:, 3, :], soft[:, 3, :], 1.0 / odd, None, ALU.add))
                chain(tt(soft[:, 3, :], soft[:, 3, :], soft[:, 1, :], ALU.mult))
                chain(ts(soft[:, 0, :], lam, -1.0, 0.0, ALU.mult, ALU.max))
                chain(stt(out=decay[:], in0=soft[:, 3, :], scalar=2.0, in1=soft[:, 0, :],
                          op0=ALU.mult, op1=ALU.add))
                chain(ts(decay[:], decay[:], -LRU_C, None, ALU.mult))
                eng.wait_ge(consts_in, 16)
                for layer in range(DEPTH):
                    chain(tt(sink_pick[:, layer, :], sink[:, layer, :], cst[:, C_PICK:C_PICK + N_Q], ALU.mult))
                chain(nc.vector.tensor_reduce(sink_tail[:], sink_pick[:], AX.X, ALU.add))
                chain(ts(sink_tail_neg[:], sink_tail[:], -1.0, None, ALU.mult))
                chain(ts(sink_neg[:], sink[:], -1.0, None, ALU.mult))

            def take_chunk(k):
                eng.wait_ge(x_turned, k + 1)
                nc.vector.tensor_copy(h[:, k, :], bank[k][:, 0:T]).then_inc(h_ready, 1)

            full = slice(0, T)
            for k in range(4):
                take_chunk(k)
            split(0)
            low_part(0, 0, full)
            split(1)
            take_chunk(4)
            take_chunk(5)
            low_part(0, 2, full)
            split(2)
            take_chunk(6)
            take_chunk(7)
            low_part(0, 4, full)
            split(3)
            low_part(0, 6, full)

            for layer in range(DEPTH):
                last = layer == DEPTH - 1
                ffn(2 * layer, 3 * layer, tokens(False), True)
                mixer(layer, 3 * layer + 1, tokens(last))
                ffn(2 * layer + 1, 3 * layer + 2, tokens(last), not last)
            for b in range(2):
                eng.wait_ge(out_turned, 2 * b + 2)
                nc.vector.tensor_copy(out_stage[:, 2 + b, :], bank[2 + b][:, :]).then_inc(out_dve, 1)

        @block.tensor
        def _(eng):
            mm = nc.tensor.matmul

            def product(to, s, at, x_hi, x_lo, start, stop):
                mm(to, w_hi[:, s, at:at + P], x_hi, start=start, stop=False)
                mm(to, w_hi[:, s, at:at + P], x_lo, start=False, stop=False)
                return mm(to, w_lo[:, s, at:at + P], x_hi, start=False, stop=stop)

            def wait_unit(n0, i=0):
                eng.wait_ge(w_lo_ready, n0 + 4 * i + 1)

            def project(n0, i, half, to, tok, free=(None, None), inc_even=False):
                wait_unit(n0, i)
                for b in range(2):
                    if free[b] is not None:
                        eng.wait_ge(*free[b])
                    for k in range(HALF):
                        c = half * HALF + k
                        last = product(to[b][:, tok], slot(n0), (2 * k + b) * P, h_hi[:, c, tok],
                                       h_lo[:, c, tok], c == 0, c == KD - 1)
                    if b == 0 and half == 1 and inc_even:
                        last.then_inc(even_psum, 1)
                last.then_inc(w_used, 1)

            def first_units(n0, version, tok, inc_even=False):
                for k in range(KD + 1):
                    if k < KD:
                        eng.wait_ge(h_hi_ready, KD * version + k + 1)
                        for pair in range(2):
                            n = n0 + 2 * (k // HALF) + pair
                            if k % HALF == 0:
                                wait_unit(n)
                            for b in range(2):
                                to = bank[2 * pair + b][:, tok]
                                at = (2 * (k % HALF) + b) * P
                                mm(to, w_hi[:, slot(n), at:at + P], h_hi[:, k, tok], start=(k == 0), stop=False)
                                mm(to, w_lo[:, slot(n), at:at + P], h_hi[:, k, tok], start=False, stop=False)
                    if k >= 1:
                        c = k - 1
                        if c % 2 == 0:
                            eng.wait_ge(h_lo_dve, HALF * version + c // 2 + 1)
                        else:
                            eng.wait_ge(h_lo_pool, HALF * version + c // 2 + 1)
                        for pair in range(2):
                            n = n0 + 2 * (c // HALF) + pair
                            for b in range(2):
                                at = (2 * (c % HALF) + b) * P
                                last = mm(bank[2 * pair + b][:, tok], w_hi[:, slot(n), at:at + P],
                                          h_lo[:, c, tok], start=False, stop=(c == KD - 1))
                                if c == KD - 1 and b == 0 and inc_even:
                                    last.then_inc(even_psum, 1)
                            if c % HALF == HALF - 1:
                                last.then_inc(w_used, 1)

            def norm_center(norm, tok):
                m = center_tiles(norm)
                eng.wait_ge(csum_step, centers(norm) + m)
                mm(bank[6][:, tok], ones_c[:, 0 if m == 6 else 1, :], csum[:, tok], start=True,
                   stop=True).then_inc(c_psum, 1)

            def norm_squares(norm, tok):
                m = center_tiles(norm)
                eng.wait_ge(sumsq_step, centers(norm + 1) - (norm + 1))
                mm(bank[7][:, tok], ones_d[:], sumsq[:, tok], start=True, stop=False)
                eng.wait_ge(c_ready, norm + 1)

            def norm_tile(norm, d, tok):
                last = d == KD - 1
                eng.wait_ge(zc_ready, KD * norm + d + 1)
                mean = mm(bank[6][:, tok], ones_d[:], h[:, d, tok], start=(d == center_tiles(norm)), stop=last)
                eng.wait_ge(sq_ready, KD * norm + d + 1)
                square = mm(bank[7][:, tok], ones_d[:], sq[:, d, tok], start=False, stop=last)
                if last:
                    mean.then_inc(dmu_psum, 1)
                    square.then_inc(var_psum, 1)

            def norm_tail(norm, tok):
                norm_tile(norm, KD - 1, tok)
                eng.wait_ge(masks_ready, 2)
                for _ in range(WARM):
                    mm(bank[4][:, tok], ident16[:], masks[:, 0:T][:, tok], start=True, stop=True)

            def ffn(f, norm, version, tok):
                u0 = ffn_unit0(f)
                first_units(u0, version, tok)
                with eng.Fori(1, GU_STEPS, 1) as i:
                    for j in range(4):
                        free = ((silu_done, mult_done)[j % 2], GU_STEPS * f + i)
                        b = 2 * (j % 2)
                        project(u0 + j, i, j // 2, bank[b:b + 2], tok, (free if j < 2 else None, None))
                if f == 0:
                    turn_params()
                d0 = u0 + N_GU

                def down(i, j):
                    n0 = d0 + j
                    k0, k1 = DOWN_K[j]
                    first = isinstance(i, int) and i == 0
                    wait_unit(n0, i)
                    for b in range(2):
                        if j == 0 and not first:
                            eng.wait_ge(z_ready, centers(norm) + 2 * i + b - 1)
                        closing = i == DOWN_STEPS - 1 and j == 3 and b == 1 if isinstance(i, int) else False
                        if closing:
                            norm_squares(norm, tok)
                        for k in range(k0, k1):
                            if closing and k == k1 - 1:
                                norm_tile(norm, KD - 2, tok)
                            if first and b == 0 and (k == k0 or k % 2 == 0):
                                eng.wait_ge(a_lo_ready, GU_STEPS * f + k // 2 + 1)
                            last = product(bank[4 + b][:, tok], slot(n0), (2 * (k - k0) + b) * P,
                                           a_hi[:, k, tok], a_lo[:, k, tok], k == 0, k == KF - 1)
                        if b == 0 and j == 3:
                            last.then_inc(even_psum, 1)
                    last.then_inc(w_used, 1)

                for j in range(4):
                    down(0, j)
                with eng.Fori(1, DOWN_STEPS - 1, 1) as i:
                    for j in range(4):
                        down(i, j)
                down(DOWN_STEPS - 1, 0)
                norm_center(norm, tok)
                for j in range(1, 4):
                    down(DOWN_STEPS - 1, j)
                norm_tail(norm, tok)

            def gates(layer, r):
                n = RT * layer + r
                eng.wait_ge(conv_step, TAPS * (n + 1))
                if r >= 1:
                    eng.wait_ge(sig_ready, 2 * n)
                else:
                    eng.wait_ge(gates_in, 16 * 4 * DEPTH)
                mm(bank[6][:, 0:T], gate_w[:, layer, 0, r, :], xc[:, r, :], start=True, stop=True)
                mm(bank[7][:, 0:T], gate_w[:, layer, 1, r, :], xc[:, r, :], start=True,
                   stop=True).then_inc(gates_psum, 1)

            def swap(layer, p):
                n = 5 * layer + p
                if p == 0:
                    eng.wait_ge(kv_raw_ready, layer + 1)
                    src = k_raw
                else:
                    eng.wait_ge(q_raw_ready, 2 * layer + (p + 1) // 2)
                    src = q_raw[:, p - 1, :]
                if p >= 2:
                    eng.wait_ge(rope_s, n - 1)
                mm(bank[4 + p % 2][:, 0:T], perm, src, start=True, stop=True).then_inc(swap_psum, 1)

            def turn_values(layer):
                eng.wait_ge(kv_raw_ready, layer + 1)
                eng.wait_ge(sig_ready, 2 * RT * (layer + 1))
                for b in range(3):
                    n = min(P, T - b * P)
                    last = nc.tensor.transpose(bank[7][0:n, b * P:(b + 1) * P],
                                               v_raw[:, b * P:b * P + n], ident)
                last.then_inc(v_psum, 1)

            def scores(layer, s):
                g, t0, heads, q0, keys = STEPS[s]
                to = bank[SCORE_BANKS[s % 2]]
                if s == 0:
                    eng.wait_ge(rope_ready, 6 * layer + 6)
                    eng.wait_ge(masks_ready, 2)
                if s >= 2:
                    eng.wait_ge(exp_ready, NS * layer + s - 1)
                m0 = {128: 0, 256: P, 272: 3 * P}[keys]
                mm(to[:, 0:heads * keys], ident16[:], masks[:, m0:m0 + keys].unsqueeze(1).to_broadcast(
                    [P, heads, keys]), start=True, stop=False, skip_group_check=True)
                if g is None:
                    eng.wait_ge(q_tail_ready, layer + 1)
                    for g in range(N_KV):
                        last = mm(to[g * HEAD:(g + 1) * HEAD, 0:keys], q_tail[:],
                                  k_rot[:, g, 0:keys], start=False, stop=True, skip_group_check=True)
                else:
                    for i in range(heads):
                        last = mm(to[:, i * keys:(i + 1) * keys], q_rot[:, t0 + i, q0:q0 + P],
                                  k_rot[:, g, 0:keys], start=False, stop=(i == heads - 1), skip_group_check=True)
                last.then_inc(scores_psum, 1)

            def turn_probs(layer, s):
                g, t0, heads, q0, keys = STEPS[s]
                to = bank[TURN_BANKS[s % 2]]
                eng.wait_ge(probs_ready, NS * layer + s + 1)
                if s == 0:
                    eng.wait_ge(v_ready, 2 * layer + 2)
                elif s == 1:
                    eng.wait_ge(q_raw_ready, 2 * layer + 2)
                elif s % 2:
                    eng.wait_ge(pt_dve, 3 * layer + s // 2)
                else:
                    eng.wait_ge(pt_act, 4 * layer + s // 2)
                for b in range(-(-heads * keys // P)):
                    n = min(P, heads * keys - b * P)
                    last = nc.tensor.transpose(to[0:n, b * P:(b + 1) * P],
                                               probs[:, s % 4, b * P:b * P + n], ident)
                last.then_inc(probs_psum, 1)

            def attend(layer, s):
                g, t0, heads, q0, keys = STEPS[s]
                if s % 2:
                    eng.wait_ge(pt_dve, 3 * layer + s // 2 + 1)
                else:
                    eng.wait_ge(pt_act, 4 * layer + s // 2 + 1)
                pt = probs_t[:, s % 2, :]
                to = bank[PV_BANKS[s]]
                if s in (0, 2, 3):
                    eng.wait_ge(gate_ready, RT * layer + {0: 2, 2: 4, 3: 3}[s])
                if g is None:
                    for g in range(N_KV):
                        at = slice(g * HEAD, (g + 1) * HEAD)
                        for b in range(3):
                            n = min(P, T - b * P)
                            last = mm(to[at, 0:HEAD], v_tok[0:n, b, at],
                                      pt[0:n, b * P + g * HEAD:b * P + (g + 1) * HEAD],
                                      start=(b == 0), stop=(b == 2))
                else:
                    at = slice(g * HEAD, (g + 1) * HEAD)
                    kb = keys // P
                    view = pt.rearrange("p (h b q) -> p h b q", h=heads, b=kb)
                    for b in range(kb):
                        last = mm(to[at, t0 * P:(t0 + heads) * P], v_tok[:, b, at], view[:, :, b, :],
                                  start=(b == 0), stop=(b == kb - 1))
                last.then_inc(pv_done, 1)

            def recurrent_mean(layer, to, tok):
                eng.wait_ge(ysq_step, 3 * layer + 3)
                mm(to[:, tok], ones_r[:], sumsq[:, tok], start=True, stop=True).then_inc(rms_psum, 1)

            def attention_mean(layer, to, tok):
                eng.wait_ge(att_sq_ready, 3 * layer + 3)
                for r in range(QT):
                    last = mm(to[:, tok], ones_r[:], ig[:, r, tok], start=(r == 0), stop=(r == QT - 1))
                last.then_inc(rms_psum, 1)

            def project_out(layer, which, d, tok):
                n0 = out_unit0(layer) + 4 * which + d // 2
                norm = 3 * layer + 1
                if d % 2 == 0:
                    wait_unit(n0)
                if which == 0:
                    to = bank[OUT_BANKS[d % 3]]
                    if d < 2:
                        eng.wait_ge(ya_ready, 3 * layer + d + 1)
                    elif d >= 3:
                        eng.wait_ge(z_rec_ready, KD * layer + d - 2)
                else:
                    to = bank[ATT_BANKS[d % 4]]
                    if d == 1:
                        eng.wait_ge(ya_ready, 3 * layer + 3)
                    elif d in (2, 3):
                        eng.wait_ge(z_rec_ready, KD * layer + 4 + d)
                    elif d >= 4:
                        eng.wait_ge(z_ready, centers(norm) + d - 3)
                if d == 0:
                    n = 8 * layer + 4 * which
                    for k in range(4):
                        eng.wait_ge(y_hi_ready, n + k + 1)
                        for part in (w_hi, w_lo):
                            mm(to[:, tok], part[:, slot(n0), 2 * k * P:(2 * k + 1) * P], h_hi[:, 4 * which + k, tok],
                               start=(k == 0 and part is w_hi), stop=False)
                    for k in range(4):
                        eng.wait_ge(y_lo_ready, n + k + 1)
                        last = mm(to[:, tok], w_hi[:, slot(n0), 2 * k * P:(2 * k + 1) * P],
                                  h_lo[:, 4 * which + k, tok], start=False, stop=(k == 3))
                else:
                    for k in range(4):
                        if which == 1 and d == KD - 1 and k == 3:
                            norm_tile(norm, KD - 2, tok)
                        c = 4 * which + k
                        last = product(to[:, tok], slot(n0), (2 * k + d % 2) * P, h_hi[:, c, tok],
                                       h_lo[:, c, tok], k == 0, k == 3)
                last.then_inc(w_used if d % 2 else even_psum, 1)

            def mixer(layer, norm, version, tok):
                u0 = in_unit0(layer)
                full = slice(0, T)
                first_units(u0, version, full, True)
                q01, q23 = (q_raw_ready, 2 * layer + 1), (q_raw_ready, 2 * layer + 2)
                taps = (tap_ready, RT * (layer + 1))
                free = {2: (None, None), 3: (taps, taps), 4: (taps, taps), 5: (q01, q01),
                        6: (q23, (gate_ready, RT * layer + 1))}

                def unit(j):
                    pair, half = j // 2, j % 2
                    project(u0 + j, 0, half, [bank[b] for b in IN_BANKS[pair]], full,
                            free[pair] if half == 0 else (None, None), True)

                unit(4)
                gates(layer, 0)
                unit(5)
                gates(layer, 1)
                unit(6)
                gates(layer, 2)
                unit(7)
                gates(layer, 3)
                swap(layer, 0)
                unit(8)
                swap(layer, 1)
                unit(9)
                swap(layer, 2)
                turn_values(layer)
                unit(10)
                swap(layer, 3)
                swap(layer, 4)
                unit(11)
                scores(layer, 0)
                unit(12)
                scores(layer, 1)
                unit(13)
                scores(layer, 2)
                turn_probs(layer, 0)
                scores(layer, 3)
                turn_probs(layer, 1)
                scores(layer, 4)
                turn_probs(layer, 2)
                attend(layer, 0)
                attend(layer, 1)
                scores(layer, 5)
                turn_probs(layer, 3)
                attend(layer, 2)
                scores(layer, 6)
                recurrent_mean(layer, bank[4], tok)
                turn_probs(layer, 4)
                attend(layer, 3)
                turn_probs(layer, 5)
                attend(layer, 4)
                project_out(layer, 0, 0, tok)
                project_out(layer, 0, 1, tok)
                project_out(layer, 0, 2, tok)
                attend(layer, 5)
                turn_probs(layer, 6)
                project_out(layer, 0, 3, tok)
                attend(layer, 6)
                project_out(layer, 0, 4, tok)
                attention_mean(layer, bank[3], tok)
                project_out(layer, 0, 5, tok)
                project_out(layer, 0, 6, tok)
                project_out(layer, 0, 7, tok)
                project_out(layer, 1, 0, tok)
                project_out(layer, 1, 1, tok)
                project_out(layer, 1, 2, tok)
                project_out(layer, 1, 3, tok)
                project_out(layer, 1, 4, tok)
                norm_center(norm, tok)
                project_out(layer, 1, 5, tok)
                project_out(layer, 1, 6, tok)
                norm_squares(norm, tok)
                norm_tile(norm, 4, tok)
                norm_tile(norm, 5, tok)
                project_out(layer, 1, 7, tok)
                norm_tail(norm, tok)

            def turn_params():
                eng.wait_ge(params_in, 16 * (6 + 1 + 5 + 2 * DEPTH + 1))
                nc.tensor.transpose(bank[6][:, 0:LN_COLS], par_rows[0:LN_COLS, 0, :],
                                    cst[0:LN_COLS, C_ID:C_ID + LN_COLS]).then_inc(params_turned, 1)
                nc.tensor.transpose(bank[7][:, 0:ROWS_B], par_rows[0:ROWS_B, 1, :],
                                    cst[0:ROWS_B, C_ID:C_ID + ROWS_B]).then_inc(params_turned, 1)

            eng.wait_ge(ident_in, 16)
            eng.wait_ge(x_in, 64)
            for k in range(KD):
                for a in range(3):
                    n = min(P, T - a * P)
                    last = nc.tensor.transpose(bank[k][:, a * P:a * P + n],
                                               x_stage[0:n, a, k * P:(k + 1) * P],
                                               cst[0:n, C_ID:C_ID + n])
                last.then_inc(x_turned, 1)
            eng.wait_ge(zeroed, 9)
            eng.wait_ge(h_ready, 4)
            for layer in range(DEPTH):
                last = layer == DEPTH - 1
                ffn(2 * layer, 3 * layer, 3 * layer, tokens(False))
                mixer(layer, 3 * layer + 1, 3 * layer + 1, tokens(last))
                ffn(2 * layer + 1, 3 * layer + 2, 3 * layer + 2, tokens(last))
            for k in range(KD):
                eng.wait_ge(h_ready, KD * 3 * DEPTH + k + 1)
                for a in range(2):
                    q0 = N_META + a * P
                    mv = nc.tensor.transpose(bank[2 * a + k // 4][:, (k % 4) * P:(k % 4 + 1) * P],
                                             h[:, k, q0:q0 + P], ident)
                    if k % 4 == 3:
                        mv.then_inc(out_turned, 1)


_INS = ["x", "meta_tokens", "ffn1_w_gate", "ffn1_w_up", "ffn1_w_down", "ln1_g", "ln1_b", "w_in", "conv_w",
        "conv_b", "gate_a_w", "gate_a_b", "gate_x_w", "gate_x_b", "lru_lambda", "attn_sinks", "norm_rec_g",
        "norm_attn_g", "w_out", "ln2_g", "ln2_b", "ffn2_w_gate", "ffn2_w_up", "ffn2_w_down", "ln3_g", "ln3_b"]


def kernel(**inputs):
    import concourse.bacc as _bacc
    from concourse.bass_utils import run_bass_kernel_spmd as _run

    nc = _bacc.Bacc("TRN2", target_bir_lowering=False, num_devices=1)
    arrays, aps = {}, {}
    for name in _INS + ["shape_constants"]:
        a = np.ascontiguousarray(constants() if name == "shape_constants" else inputs[name])
        arrays[f"in_{name}"] = a
        aps[name] = nc.dram_tensor(f"in_{name}", a.shape, mybir.dt.from_np(a.dtype), kind="ExternalInput").ap()
    out = nc.dram_tensor("out", (1, SEQ, D_MODEL), F32, kind="ExternalOutput").ap()
    build(nc, aps, aps["shape_constants"], out)
    r = _run(nc, [arrays], core_ids=[0])
    return r.results[0]["out"]
```
